# Optimizing a Trainium2 kernel written in Bass

```python
import math, functools
import jax, jax.numpy as jnp
from jax import lax
import numpy as np

D_MODEL = 1024
BATCH = 1
SEQ = 256
DEPTH = 2

GRID_W = 64
CTX_LEN = 256
CHUNK = 64
CONV_W = 5
EPS = 1e-6
MIN_LOWER = 1e-30

SSD_HEADS = 8
SSD_HEAD_DIM = 64
SSD_WIDTH = SSD_HEADS * SSD_HEAD_DIM
SSD_GROUPS = 2
SSD_STATE = 128
SSD_CONV_DIM = SSD_WIDTH + 2 * SSD_GROUPS * SSD_STATE

HGRN_HEADS = 4
HGRN_KEY_DIM = 64
HGRN_HEAD_DIM = 64
HGRN_KEY_WIDTH = HGRN_HEADS * HGRN_KEY_DIM
HGRN_WIDTH = HGRN_HEADS * HGRN_HEAD_DIM

GDN_HEADS = 4
GDN_KEY_DIM = 64
GDN_HEAD_DIM = 64
GDN_KEY_WIDTH = GDN_HEADS * GDN_KEY_DIM
GDN_WIDTH = GDN_HEADS * GDN_HEAD_DIM
GDN_CONV_DIM = 2 * GDN_KEY_WIDTH + GDN_WIDTH

MIX_WIDTH = SSD_WIDTH + HGRN_WIDTH + GDN_WIDTH
SSD_IN = SSD_WIDTH + SSD_CONV_DIM + 2 * SSD_HEADS
HGRN_IN = 3 * HGRN_KEY_WIDTH + 2 * HGRN_WIDTH
GDN_IN = GDN_CONV_DIM + 4 * GDN_HEADS + GDN_WIDTH
IN_COLS = SSD_IN + HGRN_IN + GDN_IN

N_EXPERTS = 64
TOP_K = 8
EXPERT_DIM = 256
SHARED_DIM = 256
ROUTED_SCALE = 2.5
EXPERT_BLOCK = 128

kernel_name = 'hybrid_ssd_hgrn2_gdn_moe_diffusion_prefix'

def _split(u, sizes):
    return jnp.split(u, [int(s) for s in np.cumsum(sizes)[:-1]], axis=-1)

def _masked_exp(diff, mask):
    return jnp.where(mask, jnp.exp(jnp.where(mask, diff, 0.0)), 0.0)

def _rmsnorm(x, w):
    x32 = x.astype(jnp.float32)
    y = x32 * lax.rsqrt(jnp.mean(x32 * x32, axis=-1, keepdims=True) + EPS)
    return (y * w.astype(jnp.float32)).astype(x.dtype)

def _group_rms(t, group, w):
    shp = t.shape
    tg = t.reshape(*shp[:-1], shp[-1] // group, group)
    tg = tg * lax.rsqrt(jnp.mean(tg * tg, axis=-1, keepdims=True) + EPS) * w
    return tg.reshape(shp)

def _l2norm(t):
    return t * lax.rsqrt(jnp.sum(t * t, axis=-1, keepdims=True) + 1e-6)

def _dwconv(u, w):
    half = CONV_W // 2
    n = u.shape[-2]
    up = jnp.pad(u, [(0, 0)] * (u.ndim - 2) + [(half, half), (0, 0)])
    return sum(up[..., j:j + n, :] * w[j] for j in range(CONV_W))

def _grid_conv(u, w, rows):
    bsz, n, ch = u.shape
    return _dwconv(u.reshape(bsz, rows, GRID_W, ch), w).reshape(bsz, n, ch)

def _two_way(scan_fn, ctx_fwd, ctx_bwd, lat_fwd, lat_bwd, state0):
    rev = lambda args: tuple(jnp.flip(a, axis=1) for a in args)
    yc_f, sc_f = scan_fn(*ctx_fwd, state0)
    yc_b, sc_b = scan_fn(*rev(ctx_bwd), state0)
    yl_f, _ = scan_fn(*lat_fwd, sc_f)
    yl_b, _ = scan_fn(*rev(lat_bwd), sc_b)
    return yc_f + jnp.flip(yc_b, axis=1), yl_f + jnp.flip(yl_b, axis=1)

def _ssd_scan(xdt, da, bm, cm, h0):
    bsz, n, nh, p = xdt.shape
    g, ns = bm.shape[2], bm.shape[3]
    r = nh // g
    nc = n // CHUNK
    xc = xdt.reshape(bsz, nc, CHUNK, g, r, p)
    acs = jnp.cumsum(da.reshape(bsz, nc, CHUNK, g, r), axis=2)
    bc = bm.reshape(bsz, nc, CHUNK, g, ns)
    cc = cm.reshape(bsz, nc, CHUNK, g, ns)
    causal = jnp.tril(jnp.ones((CHUNK, CHUNK), dtype=bool))[:, :, None, None]
    decay = _masked_exp(acs[:, :, :, None] - acs[:, :, None], causal)
    cb = jnp.einsum('bctgn,bcsgn->bctsg', cc, bc)
    y_diag = jnp.einsum('bctsg,bctsgr,bcsgrp->bctgrp', cb, decay, xc)
    states = jnp.einsum('bcsgn,bcsgr,bcsgrp->bcgrpn', bc, jnp.exp(acs[:, :, -1:] - acs), xc)
    chunk_decay = jnp.exp(acs[:, :, -1])

    def step(h, inp):
        st, dec = inp
        return dec[..., None, None] * h + st, h

    h_fin, h_in = lax.scan(step, h0.reshape(bsz, g, r, p, ns),
                           (jnp.moveaxis(states, 1, 0), jnp.moveaxis(chunk_decay, 1, 0)))
    y_off = jnp.einsum('bctgn,bcgrpn,bctgr->bctgrp', cc, jnp.moveaxis(h_in, 0, 1), jnp.exp(acs))
    return (y_diag + y_off).reshape(bsz, n, nh, p), h_fin.reshape(bsz, nh, p, ns)

def _ssd_mixer(u_ctx, u_lat, lat_conv, conv_w, conv_b, dt_bias, a_log, d_skip, norm_w):
    a = -jnp.exp(a_log.astype(jnp.float32))

    def prep(u, conv):
        z, xbc, dt_f, dt_b = _split(u, [SSD_WIDTH, SSD_CONV_DIM, SSD_HEADS, SSD_HEADS])
        xbc = jax.nn.silu(conv(xbc, conv_w) + conv_b)
        xs, bm, cm = _split(xbc, [SSD_WIDTH, SSD_GROUPS * SSD_STATE, SSD_GROUPS * SSD_STATE])
        bsz, n = u.shape[:2]
        xs = xs.reshape(bsz, n, SSD_HEADS, SSD_HEAD_DIM)
        bm = bm.reshape(bsz, n, SSD_GROUPS, SSD_STATE)
        cm = cm.reshape(bsz, n, SSD_GROUPS, SSD_STATE)
        dtf = jax.nn.softplus(dt_f + dt_bias[0])
        dtb = jax.nn.softplus(dt_b + dt_bias[1])
        fwd = (xs * dtf[..., None], dtf * a[0], bm, cm)
        bwd = (xs * dtb[..., None], dtb * a[1], bm, cm)
        return z, xs, fwd, bwd

    zc, xc, cf, cb = prep(u_ctx, _dwconv)
    zl, xl, lf, lb = prep(u_lat, lat_conv)
    h0 = jnp.zeros((u_lat.shape[0], SSD_HEADS, SSD_HEAD_DIM, SSD_STATE), jnp.float32)
    yc, yl = _two_way(_ssd_scan, cf, cb, lf, lb, h0)

    def out(y, xs, z):
        y = (y + d_skip[:, None] * xs).reshape(z.shape)
        return _group_rms(y * jax.nn.silu(z), SSD_WIDTH // SSD_GROUPS, norm_w.reshape(SSD_GROUPS, -1))

    return out(yc, xc, zc), out(yl, xl, zl)

def _hgrn2_scan(q, logf, k, v, s0):
    bsz, n, nh, dk = q.shape
    dv = v.shape[-1]
    nc = n // CHUNK
    chunks = lambda t: jnp.moveaxis(t.reshape(bsz, nc, CHUNK, *t.shape[2:]), 1, 0)
    causal = jnp.tril(jnp.ones((CHUNK, CHUNK), dtype=bool))[None, :, :, None, None]

    def step(s, inp):
        qc, gc, kc, vc = inp
        b = jnp.cumsum(gc, axis=1)
        w = _masked_exp(b[:, :, None] - b[:, None, :], causal)
        att = jnp.einsum('bthk,bshk,btshk->bhts', qc, kc, w)
        o = jnp.einsum('bhts,bshv->bthv', att, vc) + jnp.einsum('bthk,bhkv->bthv', qc * jnp.exp(b), s)
        b_last = b[:, -1]
        s = jnp.exp(b_last)[..., None] * s + jnp.einsum('bshk,bshv->bhkv', kc * jnp.exp(b_last[:, None] - b), vc)
        return s, o

    s_fin, o = lax.scan(step, s0, (chunks(q), chunks(logf), chunks(k), chunks(v)))
    return jnp.moveaxis(o, 0, 1).reshape(bsz, n, nh, dv), s_fin

def _hgrn_mixer(u_ctx, u_lat, lower, norm_w):
    log_lower = jnp.log(jnp.maximum(lower, MIN_LOWER))

    def gate(fr):
        logf = jnp.logaddexp(jax.nn.log_sigmoid(fr), log_lower + jax.nn.log_sigmoid(-fr))
        return logf, (1.0 - lower) * jax.nn.sigmoid(-fr)

    def prep(u):
        q, f_f, f_b, i, g = _split(u, [HGRN_KEY_WIDTH, HGRN_KEY_WIDTH, HGRN_KEY_WIDTH, HGRN_WIDTH, HGRN_WIDTH])
        bsz, n = u.shape[:2]
        heads = lambda t, d: t.reshape(bsz, n, HGRN_HEADS, d)
        q = heads(jax.nn.silu(q), HGRN_KEY_DIM)
        i = heads(i, HGRN_HEAD_DIM)
        lf, kf = gate(f_f)
        lbw, kb = gate(f_b)
        fwd = (q, heads(lf, HGRN_KEY_DIM), heads(kf, HGRN_KEY_DIM), i)
        bwd = (q, heads(lbw, HGRN_KEY_DIM), heads(kb, HGRN_KEY_DIM), i)
        return g, fwd, bwd

    gc, cf, cb = prep(u_ctx)
    gl, lf, lb = prep(u_lat)
    s0 = jnp.zeros((u_lat.shape[0], HGRN_HEADS, HGRN_KEY_DIM, HGRN_HEAD_DIM), jnp.float32)
    oc, ol = _two_way(_hgrn2_scan, cf, cb, lf, lb, s0)
    out = lambda o, g: _group_rms(o.reshape(g.shape), HGRN_HEAD_DIM, norm_w) * jax.nn.silu(g)
    return out(oc, gc), out(ol, gl)

def _gdn_scan(q, k, v, g, beta, s0):
    bsz, n, nh, dk = q.shape
    dv = v.shape[-1]
    nc = n // CHUNK

    def to_chunks(t):
        return jnp.moveaxis(t.reshape(bsz, nc, CHUNK, nh, *t.shape[3:]), 3, 2)

    qc, kc, vc, bc = to_chunks(q), to_chunks(k), to_chunks(v), to_chunks(beta)
    gam = jnp.cumsum(to_chunks(g), axis=-1)
    incl = jnp.tril(jnp.ones((CHUNK, CHUNK), dtype=bool))
    strict = jnp.tril(jnp.ones((CHUNK, CHUNK), dtype=bool), k=-1)
    decay = _masked_exp(gam[..., :, None] - gam[..., None, :], incl)
    kb = kc * bc[..., None]
    a_strict = jnp.where(strict, jnp.einsum('bchtk,bchsk->bchts', kb, kc) * decay, 0.0)
    lhs = a_strict + jnp.eye(CHUNK, dtype=a_strict.dtype)
    rhs = jnp.concatenate([vc * bc[..., None], kb * jnp.exp(gam)[..., None]], axis=-1)
    sol = lax.linalg.triangular_solve(lhs, rhs, left_side=True, lower=True, unit_diagonal=True)
    u, w = sol[..., :dv], sol[..., dv:]
    qk = jnp.einsum('bchtk,bchsk->bchts', qc, kc) * decay
    qg = qc * jnp.exp(gam)[..., None]
    kend = kc * jnp.exp(gam[..., -1:] - gam)[..., None]
    dec = jnp.exp(gam[..., -1])

    def step(s, inp):
        u_c, w_c, qk_c, qg_c, ke_c, d_c = inp
        v_new = u_c - jnp.einsum('bhtk,bhkv->bhtv', w_c, s)
        o = jnp.einsum('bhtk,bhkv->bhtv', qg_c, s) + jnp.einsum('bhts,bhsv->bhtv', qk_c, v_new)
        s = d_c[..., None, None] * s + jnp.einsum('bhsk,bhsv->bhkv', ke_c, v_new)
        return s, o

    mv = lambda t: jnp.moveaxis(t, 1, 0)
    s_fin, o = lax.scan(step, s0, (mv(u), mv(w), mv(qk), mv(qg), mv(kend), mv(dec)))
    o = jnp.moveaxis(jnp.moveaxis(o, 0, 1), 2, 3).reshape(bsz, n, nh, dv)
    return o, s_fin

def _gdn_mixer(u_ctx, u_lat, lat_conv, conv_w, dt_bias, a_log, norm_w):
    a = jnp.exp(a_log.astype(jnp.float32))

    def prep(u, conv):
        qkv, a_f, a_b, b_f, b_b, g = _split(u, [GDN_CONV_DIM, GDN_HEADS, GDN_HEADS, GDN_HEADS, GDN_HEADS, GDN_WIDTH])
        q, k, v = _split(jax.nn.silu(conv(qkv, conv_w)), [GDN_KEY_WIDTH, GDN_KEY_WIDTH, GDN_WIDTH])
        bsz, n = u.shape[:2]
        q = _l2norm(q.reshape(bsz, n, GDN_HEADS, GDN_KEY_DIM)) * GDN_KEY_DIM ** -0.5
        k = _l2norm(k.reshape(bsz, n, GDN_HEADS, GDN_KEY_DIM))
        v = v.reshape(bsz, n, GDN_HEADS, GDN_HEAD_DIM)
        g_f = -a[0] * jax.nn.softplus(a_f + dt_bias[0])
        g_b = -a[1] * jax.nn.softplus(a_b + dt_bias[1])
        return g, (q, k, v, g_f, jax.nn.sigmoid(b_f)), (q, k, v, g_b, jax.nn.sigmoid(b_b))

    gc, cf, cb = prep(u_ctx, _dwconv)
    gl, lf, lb = prep(u_lat, lat_conv)
    s0 = jnp.zeros((u_lat.shape[0], GDN_HEADS, GDN_KEY_DIM, GDN_HEAD_DIM), jnp.float32)
    oc, ol = _two_way(_gdn_scan, cf, cb, lf, lb, s0)
    out = lambda o, g: _group_rms(o.reshape(g.shape), GDN_HEAD_DIM, norm_w) * jax.nn.silu(g)
    return out(oc, gc), out(ol, gl)

def _routed_experts(h, router_w, router_bias, w_gate, w_up, w_down):
    n_tok, dm = h.shape
    n_assign = n_tok * TOP_K
    scores = jax.nn.sigmoid(jnp.dot(h.astype(jnp.float32), router_w.astype(jnp.float32)))
    _, idx = lax.top_k(scores + router_bias.astype(jnp.float32), TOP_K)
    gate = jnp.take_along_axis(scores, idx, axis=-1)
    gate = gate / jnp.sum(gate, axis=-1, keepdims=True) * ROUTED_SCALE
    flat_e = idx.reshape(-1)
    order = jnp.argsort(flat_e)
    e_sorted = flat_e[order]
    token = order // TOP_K
    counts = jnp.bincount(flat_e, length=N_EXPERTS)
    padded = (counts + EXPERT_BLOCK - 1) // EXPERT_BLOCK * EXPERT_BLOCK
    pad_end = jnp.cumsum(padded)
    slot = (pad_end - padded)[e_sorted] + jnp.arange(n_assign) - (jnp.cumsum(counts) - counts)[e_sorted]
    n_blocks = -(-n_assign // EXPERT_BLOCK) + N_EXPERTS
    buf = jnp.zeros((n_blocks * EXPERT_BLOCK, dm), h.dtype).at[slot].set(h[token])
    block_expert = jnp.minimum(
        jnp.searchsorted(pad_end, jnp.arange(n_blocks) * EXPERT_BLOCK, side='right'), N_EXPERTS - 1)

    def expert_block(args):
        xb, e = args
        return (jax.nn.silu(xb @ w_gate[e]) * (xb @ w_up[e])) @ w_down[e]

    out = lax.map(expert_block, (buf.reshape(n_blocks, EXPERT_BLOCK, dm), block_expert))
    out = out.reshape(n_blocks * EXPERT_BLOCK, dm)
    contrib = out[slot] * gate.reshape(-1)[order][:, None].astype(out.dtype)
    return jnp.zeros_like(h).at[token].add(contrib)

def _moe(h, router_w, router_bias, w_gate, w_up, w_down, sh_gate, sh_up, sh_down):
    routed = lax.map(lambda hs: _routed_experts(hs, router_w, router_bias, w_gate, w_up, w_down), h)
    shared = (jax.nn.silu(h @ sh_gate) * (h @ sh_up)) @ sh_down
    return routed + shared

def setup_inputs(seed: int = 0) -> dict:
    key = jax.random.key(seed)
    ks = jax.random.split(key, 31)
    nrm = lambda k, shape, scale: jax.random.normal(k, shape, jnp.float32) * scale

    def dt_bias(k, shape):
        dt = jnp.exp(jax.random.uniform(k, shape, jnp.float32) * (math.log(0.1) - math.log(1e-3)) + math.log(1e-3))
        return dt + jnp.log(-jnp.expm1(-dt))

    def a_log(k, shape):
        return jnp.log(jax.random.uniform(k, shape, jnp.float32, minval=1.0, maxval=16.0))

    L = DEPTH
    return {
        'x': nrm(ks[0], (BATCH, SEQ, D_MODEL), 1.0),
        'c': nrm(ks[1], (BATCH, D_MODEL), 1.0),
        'ctx': nrm(ks[2], (BATCH, CTX_LEN, D_MODEL), 1.0),
        'c_ctx': nrm(ks[3], (D_MODEL,), 1.0),
        'w_mod': nrm(ks[4], (L, D_MODEL, 6 * D_MODEL), 0.5 * D_MODEL ** -0.5),
        'b_mod': nrm(ks[5], (L, 6 * D_MODEL), 0.02),
        'norm_mix': 1.0 + nrm(ks[6], (L, D_MODEL), 0.02),
        'w_in': nrm(ks[7], (L, D_MODEL, IN_COLS), D_MODEL ** -0.5),
        'ssd_conv_w': nrm(ks[8], (L, CONV_W, SSD_CONV_DIM), CONV_W ** -0.5),
        'ssd_conv_b': nrm(ks[9], (L, SSD_CONV_DIM), 0.02),
        'ssd_dt_bias': dt_bias(ks[10], (L, 2, SSD_HEADS)),
        'ssd_a_log': a_log(ks[11], (L, 2, SSD_HEADS)),
        'ssd_d': 1.0 + nrm(ks[12], (L, SSD_HEADS), 0.02),
        'ssd_norm': 1.0 + nrm(ks[13], (L, SSD_WIDTH), 0.02),
        'hgrn_lb': nrm(ks[14], (L, HGRN_KEY_WIDTH), 0.1),
        'hgrn_norm': 1.0 + nrm(ks[15], (L, HGRN_HEAD_DIM), 0.02),
        'gdn_conv_w': nrm(ks[16], (L, CONV_W, GDN_CONV_DIM), CONV_W ** -0.5),
        'gdn_dt_bias': dt_bias(ks[17], (L, 2, GDN_HEADS)),
        'gdn_a_log': a_log(ks[18], (L, 2, GDN_HEADS)),
        'gdn_norm': 1.0 + nrm(ks[19], (L, GDN_HEAD_DIM), 0.02),
        'w_out': nrm(ks[20], (L, MIX_WIDTH, D_MODEL), MIX_WIDTH ** -0.5),
        'norm_ffn': 1.0 + nrm(ks[21], (L, D_MODEL), 0.02),
        'router_w': nrm(ks[22], (L, D_MODEL, N_EXPERTS), D_MODEL ** -0.5),
        'router_bias': nrm(ks[23], (L, N_EXPERTS), 0.01),
        'exp_gate': nrm(ks[24], (L, N_EXPERTS, D_MODEL, EXPERT_DIM), D_MODEL ** -0.5),
        'exp_up': nrm(ks[25], (L, N_EXPERTS, D_MODEL, EXPERT_DIM), D_MODEL ** -0.5),
        'exp_down': nrm(ks[26], (L, N_EXPERTS, EXPERT_DIM, D_MODEL), EXPERT_DIM ** -0.5),
        'sh_gate': nrm(ks[27], (L, D_MODEL, SHARED_DIM), D_MODEL ** -0.5),
        'sh_up': nrm(ks[28], (L, D_MODEL, SHARED_DIM), D_MODEL ** -0.5),
        'sh_down': nrm(ks[29], (L, SHARED_DIM, D_MODEL), SHARED_DIM ** -0.5),
        'norm_final': 1.0 + nrm(ks[30], (D_MODEL,), 0.02),
    }

def reference(x, c, ctx, c_ctx, w_mod, b_mod, norm_mix, w_in, ssd_conv_w, ssd_conv_b, ssd_dt_bias,
              ssd_a_log, ssd_d, ssd_norm, hgrn_lb, hgrn_norm, gdn_conv_w, gdn_dt_bias, gdn_a_log, gdn_norm,
              w_out, norm_ffn, router_w, router_bias, exp_gate, exp_up, exp_down, sh_gate, sh_up, sh_down,
              norm_final):
    rows = x.shape[1] // GRID_W
    lat_conv = functools.partial(_grid_conv, rows=rows)
    p_lb = jax.nn.softmax(hgrn_lb.astype(jnp.float32), axis=0)
    lower_all = jnp.cumsum(p_lb, axis=0) - p_lb[0]
    s_lat = jax.nn.silu(c)
    s_ctx = jax.nn.silu(c_ctx)[None]
    h, hc = x, ctx
    for l in range(DEPTH):
        mod_l = (s_lat @ w_mod[l] + b_mod[l])[:, None, :]
        mod_c = (s_ctx @ w_mod[l] + b_mod[l])[:, None, :]
        sh_m, sc_m, g_m, sh_f, sc_f, g_f = jnp.split(mod_l, 6, axis=-1)
        csh_m, csc_m, cg_m, csh_f, csc_f, cg_f = jnp.split(mod_c, 6, axis=-1)

        a_l = _rmsnorm(h, norm_mix[l]) * (1.0 + sc_m) + sh_m
        a_c = _rmsnorm(hc, norm_mix[l]) * (1.0 + csc_m) + csh_m
        u_l = (a_l @ w_in[l]).astype(jnp.float32)
        u_c = (a_c @ w_in[l]).astype(jnp.float32)
        ssd_c, hg_c, gd_c = _split(u_c, [SSD_IN, HGRN_IN, GDN_IN])
        ssd_l, hg_l, gd_l = _split(u_l, [SSD_IN, HGRN_IN, GDN_IN])
        ys_c, ys_l = _ssd_mixer(ssd_c, ssd_l, lat_conv, ssd_conv_w[l], ssd_conv_b[l], ssd_dt_bias[l],
                                ssd_a_log[l], ssd_d[l], ssd_norm[l])
        yh_c, yh_l = _hgrn_mixer(hg_c, hg_l, lower_all[l], hgrn_norm[l])
        yg_c, yg_l = _gdn_mixer(gd_c, gd_l, lat_conv, gdn_conv_w[l], gdn_dt_bias[l], gdn_a_log[l], gdn_norm[l])
        y_l = jnp.concatenate([ys_l, yh_l, yg_l], axis=-1).astype(h.dtype)
        h = h + g_m * (y_l @ w_out[l])

        f_l = _rmsnorm(h, norm_ffn[l]) * (1.0 + sc_f) + sh_f
        h = h + g_f * _moe(f_l, router_w[l], router_bias[l], exp_gate[l], exp_up[l], exp_down[l],
                           sh_gate[l], sh_up[l], sh_down[l])

        if l < DEPTH - 1:
            y_c = jnp.concatenate([ys_c, yh_c, yg_c], axis=-1).astype(hc.dtype)
            hc = hc + cg_m * (y_c @ w_out[l])
            f_c = _rmsnorm(hc, norm_ffn[l]) * (1.0 + csc_f) + csh_f
            hc = hc + cg_f * _moe(f_c, router_w[l], router_bias[l], exp_gate[l], exp_up[l], exp_down[l],
                                  sh_gate[l], sh_up[l], sh_down[l])
    return _rmsnorm(h, norm_final)


_drawn_inputs = setup_inputs


def setup_inputs(seed=0):
    import zlib

    import numpy as np

    out = dict(_drawn_inputs(seed))
    spreads = {}
    factors = {'ssd_d': 18.871,
     'hgrn_lb': 7.882,
     'hgrn_norm': 4.795,
     'gdn_norm': 4.799,
     'norm_final': 7.622,
     'ssd_conv_b': 2.838,
     'ssd_norm': 2.978}
    for name, (base, spread) in spreads.items():
        noise = np.random.default_rng([zlib.crc32(name.encode()), seed]).standard_normal(out[name].shape)
        drawn = base * np.exp(spread * noise) if base else spread * noise
        out[name] = __import__('jax').numpy.asarray(drawn.astype(out[name].dtype))
    for name, factor in factors.items():
        out[name] = (out[name] * factor).astype(out[name].dtype)
    return out
```

```python
import math
from contextlib import ExitStack

import numpy as np

import concourse.bass as bass
from concourse import mybir

F32 = mybir.dt.float32
I32 = mybir.dt.int32
U32 = mybir.dt.uint32
ALU = mybir.AluOpType
ACT = mybir.ActivationFunctionType
AX = mybir.AxisListType

P = 128
DEPTH = 2
DM = 1024
KT = DM // P
CTX = 256
SEQ = 256
TOK = CTX + SEQ
NT = TOK // P
GRID_W = 64
ROWS = SEQ // GRID_W
TAPS = 5
HALF = TAPS // 2
EPS = 1e-6

HS, NG, NSTATE = 8, 2, 128
HH = 4
HD = 64
SW = HS * HD
HW = HH * HD
NDEC = HS + HH
SSD_IN = SW + SW + 2 * NG * NSTATE + 2 * HS
HGRN_IN = 5 * HW
GDN_IN = 3 * HW + 4 * HH + HW
COL_HGRN = SSD_IN
COL_GDN = SSD_IN + HGRN_IN
CT = 14
LEVELS = 7
NE, TOPK, ED = 64, 8, 256
ROUTED_SCALE = 2.5
CAP = TOK
NBLK = CAP // P
NSLOT = 4
BW = 256
RSIZE = 33700
NEG = -1e30
SKIP = 1 << 20

CPAD = CTX + 2 * HALF
RPAD = GRID_W + 2 * HALF
LINE = CPAD + ROWS * RPAD
CONV = LINE - 2 * HALF

IN_BLOCKS = (
    [("conv", SW + BW * i, i) for i in range(4)]
    + [("conv", COL_GDN + BW * i, 4 + i) for i in range(3)]
    + [("hq", COL_HGRN, 0), ("gate", 0, 0), ("gate", BW, 1),
       ("gate", COL_HGRN + 4 * HW, 2), ("gate", COL_GDN + 3 * HW + 4 * HH, 3)]
    + [("val", COL_HGRN + 3 * HW, 0), ("hf", COL_HGRN + HW, 0), ("hf", COL_HGRN + 2 * HW, 1)]
)
N_CONV = 7
N_IN = len(IN_BLOCKS)
N_MOD = 6 * DM // BW
N_OUT = DM // BW
RING = N_MOD + N_IN + N_OUT + 3

R_BMOD, R_NMIX, R_NFFN = 0, 48, 56
R_CWS, R_CBS, R_CWG = 64, 104, 112
N_PRM = 142

UB = (0, 4, 6)
PRM_DMAS = 12
NROW_DMAS = 3
OVER = (NBLK - 1) * NE

ORDER = ((0, 1, 2, 3), (1, 0, 3, 2))
UNITS = [(i, d, ORDER[d][i]) for i in range(NT) for d in range(2)]
SEEN = {}
for _n, (_i, _d, _c) in enumerate(UNITS):
    SEEN.setdefault(_c, _n)


def line_rows(ap):
    return ap[:, CPAD:CPAD + (ROWS - 1) * RPAD + RPAD].rearrange("p (r x) -> p r x", r=ROWS)[:, :, 0:GRID_W]


def build(nc, A, out, scratch):
    f_dram, acc_dram, tab_dram = scratch
    with ExitStack() as ctx:
        def sb(name, shape, dt=F32):
            return ctx.enter_context(nc.sbuf_tensor(name, shape, dt))

        def sem(name):
            return ctx.enter_context(nc.semaphore(name))

        h = sb("h", [P, NT, DM])
        featT = sb("featT", [P, KT, TOK])
        yraw = featT[:, :, :].rearrange("p k t -> p (k t)").rearrange("p (c f) -> p c f", c=NT)
        X = sb("X", [P, 2, DM])
        ring = sb("ring", [P, 2, KT, BW])
        ident = sb("ident", [P, P])
        tri = sb("tri", [P, 2, P])
        negm = sb("negm", [P, 2, P])
        triS = sb("triS", [P, P])
        ones = sb("ones", [P, P])
        bd = sb("bd", [P, P])
        lev = sb("lev", [P, 2, LEVELS, P])
        iota_e = sb("iota_e", [P, NE])
        tokid = sb("tokid", [P, NT], I32)
        cst = sb("cst", [P, 4])
        condT = sb("condT", [P, 2, KT])
        stage = sb("stage", [P, 2, P])
        prm = sb("prm", [P, N_PRM])
        low = sb("low", [P, DEPTH, 2])
        lowv = sb("lowv", [P, 3, 2])
        mod = sb("mod", [P, 48, 2])
        amul = sb("amul", [P, 2, KT, 2])
        nrow = X[:, 1, :]
        dtb = sb("dtb", [P, 2, NDEC])
        alog = sb("alog", [P, 2, NDEC])
        nega = sb("nega", [P, 2, NDEC])
        dsk = sb("dsk", [P, HS])
        rbias = sb("rbias", [P, NE])
        wsm = sb("wsm", [P, KT, 32])
        rw = sb("rw", [P, KT, NE])
        st = sb("st", [P, 16])
        live = sb("live", [P, DEPTH, NT])
        lcur = sb("lcur", [P, NT])
        hdec = sb("hdec", [P, 2])
        ssq = sb("ssq", [P, NT, 10])
        R = sb("R", [P, RSIZE])
        at = [0]

        def cut(*shape):
            n = math.prod(shape)
            v = R[:, at[0]:at[0] + n]
            at[0] += n
            if len(shape) == 2:
                v = v.rearrange("p (a b) -> p a b", a=shape[0])
            if len(shape) == 3:
                v = v.rearrange("p (a b c) -> p a b c", a=shape[0], b=shape[1])
            return v

        cv = cut(CT, TOK)
        hq = cut(2, TOK)
        logf = cut(2, 2, TOK)
        hk = cut(2, 2, TOK)
        gates = cut(NT, DM)
        val = cut(NT, HW)
        Btok = cut(NT, NG * NSTATE)
        Ktok = cut(NT, HW)
        wk = at[0]
        line = cut(2, LINE)
        cvo = cut(2, LINE)
        hwt = cut(2 * 2, TOK)
        hwx = cut(2 * 2, TOK)
        lnw = cut(TOK)
        lnx = cut(TOK)
        sqw = cut(2, TOK)
        sm = cut(NT, 32)
        spw = cut(4, NT * 2 * NDEC)
        at[0] = wk
        E = cut(NDEC, P)
        AT = cut(HH, P)
        NTm = cut(HH, P)
        T = cut(HH, P)
        TT = cut(HH, P)
        Pm = cut(HH, P)
        e7 = cut(LEVELS, 2 * P)
        kL = cut(LEVELS, 2 * P)
        bh = cut(2 * P)
        eb = cut(2 * P)
        e1 = cut(2 * P)
        kend = cut(2 * P)
        kendT = cut(2 * P)
        attH = cut(HH, P)
        xw = cut(SW)
        rr = cut(HW)
        vn = cut(HW)
        kw = cut(HW)
        tmp = cut(SW)
        Ss = cut(2, NG, SW // NG)
        Sh = cut(2, 2, P)
        Sg = cut(2, 2, P)
        wdt = cut(NT, 2, NDEC)
        dt_ = cut(NT, 2, NDEC)
        da = cut(NT, 2, NDEC)
        acs = cut(NT, 2, NDEC)
        eacs = cut(NT, 2, NDEC)
        wend = cut(NT, 2, NDEC)
        etot = cut(NT, 2, NDEC)
        beta = cut(NT, 2, HH)
        dcol = cut(NT * 2, 2)
        assert at[0] <= RSIZE
        levt = e7[:, 0:1, :].bitcast(I32).rearrange("p a (b t) -> p (a b) t", b=2)
        at[0] = 0
        yT = cut(KT, TOK)
        sqo = cut(2, DM)
        grow = cut(2, DM)
        at[0] = 0
        wgu, wdn = [], []
        for _ in range(NSLOT):
            wgu.append(cut(KT, 2 * ED))
            wdn.append(cut(2, DM))
        ex = at[0]
        xg = [cut(DM) for _ in range(2)]
        xgT = [cut(KT, P) for _ in range(2)]
        oe = [cut(DM) for _ in range(2)]
        sg = [cut(ED) for _ in range(2)]
        hgu = [cut(ED) for _ in range(2)]
        hTe = [cut(2, P) for _ in range(2)]
        tabA = cut(NE, 2)
        assert at[0] <= RSIZE
        at[0] = ex
        scor = cut(NT, NE)
        sel = cut(NT, NE)
        mask = cut(NT, NE)
        pos = cut(NT, NE)
        hot2 = cut(TOPK, NE)
        hots = cut(NT, TOPK * NE)
        v8 = cut(NT, TOPK)
        i8 = cut(NT, TOPK).bitcast(U32)
        if8 = cut(NT, TOPK)
        s8 = cut(NT, TOPK)
        p8 = cut(NT, TOPK)
        dst8 = cut(NT, TOPK)
        dsti = cut(NT * TOPK, 1).bitcast(I32)
        pay = cut(NT * TOPK, 2)
        gsum = cut(NT)
        blank = cut(CAP * NE // P, 2)
        sgT = cut(2, TOK)
        hsh = cut(2, TOK)
        idxS = [sb(f"idx{i}", [P, 2]) for i in range(NSLOT)]
        flag = sb("flag", [1, 4])
        flagi = sb("flagi", [1, 1], I32)

        ps = ctx.enter_context(nc.psum_tensor("ps", [P, 8, 512], F32))


        PER = {}

        def signal(name, per_layer=0):
            PER[name] = per_layer
            S[name] = sem(name)

        S = {}
        for name in ("const_pool", "const_ready", "head_loaded", "cond_ps", "cond_sb", "out_loaded",
                     "out_sq", "out_ln", "low_a", "low_b",
                     "past", "ov_dma", "out_ready", "out_stored"):
            signal(name)
        U = len(UNITS)
        for name, n in (
            ("h_ready", 1), ("prm_loaded", 16 * PRM_DMAS), ("prm_ps", 1), ("small_loaded", 32), ("rw_loaded", 16),
            ("ring_full0", 16 * RING // 2), ("ring_full1", 16 * RING // 2), ("ring_used", RING),
            ("mod_ps", 1), ("mod_sb", 1),
            ("sumsq", 2), ("rstd", 2), ("xn", 2 * NT), ("xT_ps", 2 * NT), ("feat_d", 2 * NT), ("feat_a", 2 * NT),
            ("u_ps", N_IN), ("u_dve", N_CONV), ("u_act", N_IN - N_CONV), ("conv_out", CT), ("silu_out", CT),
            ("sm_ps", 1), ("sp_x", 1), ("sp_exp", 1), ("sp_done", 1), ("cum_ps", 1), ("cum_dve", 1),
            ("cum_act", 1), ("small_done", 1),
            ("l2_sq", 4), ("l2_ps", 4), ("l2_act", 4), ("l2_done", 4),
            ("low_c", 1), ("lowl", 1), ("hg_b", 1), ("hg_c", 1), ("hg_d", 1), ("hg_e", 1), ("hg_f", 1),
            ("tok_ps", NT), ("tok_d", NT), ("tok_a", NT), ("s_init", 1),
            ("pre_ps", U), ("dm_ready", U), ("e_ready", U), ("b_ready", U), ("hexp", U), ("kl_ready", U),
            ("ql_ready", U), ("a_init", U), ("t_init", U), ("kw_ready", U), ("at_ready", U), ("att_ready", U),
            ("ssd_ps", U), ("ssd_sb", U), ("nt_ready", U * LEVELS), ("p_ps", U * LEVELS), ("p_sb", U * LEVELS),
            ("q_ps", U * LEVELS), ("t_ready", U * LEVELS), ("h_ps", U * 4), ("h_cp", U * 4),
            ("ke_ps", U), ("ke_sb", U), ("ho_ps", U), ("hgrn_done", U),
            ("gks_ps", U), ("r_ready", U), ("vn_ps", U), ("vn_sb", U), ("go_ps", U), ("gdn_done", U),
            ("nrow_loaded", 16 * NROW_DMAS), ("y_sq", 1), ("y_rstd", 1), ("y_ready", NT), ("yT_ps", NT), ("yT_sb", NT),
            ("grow_ps", 2), ("grow_sb", 2), ("wo_ps", N_OUT), ("wo_sb", N_OUT),
            ("ftok_ps", NT), ("ftok_sb", NT), ("ftok_dram0", 32), ("ftok_dram1", 32), ("lg_ps", 1), ("lg_exp", 1),
            ("mask_ready", 1), ("pos_ps", 1), ("blank_ready", 1), ("blank_dram", 16), ("pay_ready", 1),
            ("tab_dram", 16 * NT * TOPK), ("tab_loaded", 16), ("flag_ready", 1),
            ("sh_ps", 2), ("sh_silu", 1), ("sh_mul", 1), ("shd_ps", NT), ("shd_sb", NT), ("acc_dram0", 32), ("acc_dram1", 32),
            ("w0", 32 * 24), ("w1", 32 * 24), ("w2", 32 * 24), ("w3", 32 * 24), 
            ("gathered0", 4 * NE), ("gathered1", 4 * NE), ("gathered2", 4 * NE), ("gathered3", 4 * NE), ("xt_ps", NE), ("xt_sb", 2 * NE), ("gu_ps", NE), ("gu_silu", NE), ("gu_mul", NE),
            ("hT_ps", NE), ("hT_sb", NE), ("dn_ps", NE), ("oe_ready", 2 * NE), ("scattered", 16 * NE), ("xg_init", 1),
            ("acc_loaded0", 32), ("acc_loaded1", 32), ("acc_added", NT), ("gf_ps", 1),
            ("ov_w", 48 * OVER), ("ov_tab", 16 * OVER), ("ov_g", OVER), ("ov_xt", OVER), ("ov_xs", OVER),
            ("ov_gu", OVER), ("ov_sl", OVER), ("ov_mu", OVER), ("ov_ht", OVER), ("ov_hs", OVER), ("ov_dn", OVER),
            ("ov_oe", OVER), ("ov_sc", OVER),
        ):
            signal(name, n)
        for s in range(NSLOT):
            PER[f"w{s}"] = 48 * NE // NSLOT

        block = ctx.enter_context(nc.Block())

        def tk(c):
            return slice(c * P, (c + 1) * P)

        def bank(b, n=1):
            return ps[:, b:b + n, :].rearrange("p b f -> p (b f)")

        def bc(ap, *shape):
            return ap.to_broadcast([P, *shape])

        @block.sync
        def _(sp):
            def past():
                sp.sem_inc(S["past"], 1)

            def wait(name, n, l):
                sp.wait_ge(S[name], l * PER[name] + n)
                past()

            sp.dma_start(h[:, 0:2, :], A["ctx"][0].rearrange("(c p) f -> p c f", p=P)).then_inc(S["head_loaded"], 16)
            sp.dma_start(h[:, 2:4, :], A["x"][0].rearrange("(c p) f -> p c f", p=P)).then_inc(S["head_loaded"], 16)
            sp.dma_start(stage[0:KT, 0, :], A["c_ctx"].rearrange("(k p) -> k p", p=P)).then_inc(S["head_loaded"], 16)
            sp.dma_start(stage[KT:2 * KT, 0, :], A["c"].rearrange("o (k p) -> (o k) p", p=P)).then_inc(S["head_loaded"], 16)
            sp.dma_start(stage[0:4, 1, :], A["hgrn_lb"].rearrange("l (t p) -> (l t) p", p=P)).then_inc(S["head_loaded"], 16)
            with sp.Fori(0, DEPTH) as l:
                L1 = bass.ds(l, 1)
                wait("h_ready", 1, l)
                def param(dst, src):
                    sp.dma_start(dst, src).then_inc(S["prm_loaded"], 16)
                param(stage[R_BMOD:R_BMOD + 48, 0, :], A["b_mod"][L1].rearrange("o (r p) -> (o r) p", p=P))
                param(stage[R_NMIX:R_NMIX + 8, 0, :], A["norm_mix"][L1].rearrange("o (r p) -> (o r) p", p=P))
                param(stage[R_NFFN:R_NFFN + 8, 0, :], A["norm_ffn"][L1].rearrange("o (r p) -> (o r) p", p=P))
                param(stage[0:40, 1, :], A["ssd_conv_w"][L1].rearrange("o j (t p) -> (o j t) p", p=P))
                param(stage[40:48, 1, :], A["ssd_conv_b"][L1].rearrange("o (t p) -> (o t) p", p=P))
                param(stage[48:78, 1, :], A["gdn_conv_w"][L1].rearrange("o j (t p) -> (o j t) p", p=P))
                param(dtb[:, :, 0:HS], A["ssd_dt_bias"][L1].to_broadcast([P, 2, HS]))
                param(dtb[:, :, HS:NDEC], A["gdn_dt_bias"][L1].to_broadcast([P, 2, HH]))
                param(alog[:, :, 0:HS], A["ssd_a_log"][L1].to_broadcast([P, 2, HS]))
                param(alog[:, :, HS:NDEC], A["gdn_a_log"][L1].to_broadcast([P, 2, HH]))
                param(dsk[:, :], A["ssd_d"][L1].to_broadcast([P, HS]))
                param(rbias[:, :], A["router_bias"][L1].to_broadcast([P, NE]))

                def ring_block(n, dst, src, dyn=None):
                    wait("ring_used", n + 1, l) if dyn is None else sp.wait_ge(S["ring_used"], l * RING + dyn + n + 1)
                    sp.dma_start(dst, src).then_inc(S[f"ring_full{n % 2}"], 16)

                wmod = A["w_mod"][L1].rearrange("o (k p) n -> p (o k) n", p=P)
                with sp.Fori(0, N_MOD // 2) as i:
                    for s in range(2):
                        ring_block(s, ring[:, s, :, :], wmod[:, :, bass.ds(i * (2 * BW) + s * BW, BW)], dyn=i * 2)
                win = A["w_in"][L1].rearrange("o (k p) n -> p (o k) n", p=P)
                sp.dma_start(wsm[:, :, 0:16], win[:, :, 3 * SW:3 * SW + 16]).then_inc(S["small_loaded"], 16)
                sp.dma_start(wsm[:, :, 16:32], win[:, :, COL_GDN + 3 * HW:COL_GDN + 3 * HW + 16]).then_inc(S["small_loaded"], 16)
                for n, (_, col, _) in enumerate(IN_BLOCKS):
                    m = N_MOD + n
                    ring_block(m, ring[:, m % 2, :, :], win[:, :, col:col + BW])
                sp.dma_start(rw[:, :, :], A["router_w"][L1].rearrange("o (k p) n -> p (o k) n", p=P)).then_inc(S["rw_loaded"], 16)
                wout = A["w_out"][L1].rearrange("o (k p) n -> p (o k) n", p=P)
                for n in range(N_OUT):
                    m = N_MOD + N_IN + n
                    ring_block(m, ring[:, m % 2, :, :], wout[:, :, n * BW:(n + 1) * BW])
                    if n == 0:
                        wait("hgrn_done", U, l)
                        for q in range(1):
                            sp.dma_start(nrow[:, 0:SW], A["ssd_norm"][L1].to_broadcast([P, SW])).then_inc(S["nrow_loaded"], 16)
                            sp.dma_start(nrow[:, SW:SW + HD], A["hgrn_norm"][L1].to_broadcast([P, HD])).then_inc(S["nrow_loaded"], 16)
                            sp.dma_start(nrow[:, SW + HW:SW + HW + HD], A["gdn_norm"][L1].to_broadcast([P, HD])).then_inc(S["nrow_loaded"], 16)
                for n, name in enumerate(("sh_gate", "sh_up")):
                    m = N_MOD + N_IN + N_OUT + n
                    ring_block(m, ring[:, m % 2, :, :], A[name][L1].rearrange("o (k p) n -> p (o k) n", p=P))
                wait("wo_sb", N_OUT, l)
                gate_w = A["exp_gate"][L1].rearrange("o e (k p) n -> p (o e) k n", p=P)
                up_w = A["exp_up"][L1].rearrange("o e (k p) n -> p (o e) k n", p=P)
                down_w = A["exp_down"][L1].rearrange("o e (k p) n -> p (o e) k n", p=P)

                def expert(s, e):
                    one = bass.ds(e, 1)
                    sp.dma_start(wgu[s][:, :, 0:ED], gate_w[:, one].rearrange("p e k n -> p (e k) n")).then_inc(S[f"w{s}"], 16)
                    sp.dma_start(wgu[s][:, :, ED:2 * ED], up_w[:, one].rearrange("p e k n -> p (e k) n")).then_inc(S[f"w{s}"], 16)
                    sp.dma_start(wdn[s][:, :, :], down_w[:, one].rearrange("p e k n -> p (e k) n")).then_inc(S[f"w{s}"], 16)

                for s in range(NSLOT):
                    expert(s, s)
                for c in range(NT):
                    wait("ftok_sb", c + 1, l)
                    sp.dma_start(f_dram[tk(c), :], X[:, c % 2, :]).then_inc(S[f"ftok_dram{c % 2}"], 16)
                m = N_MOD + N_IN + N_OUT + 2
                ring_block(m, ring[:, m % 2, :, :].rearrange("p (a b) n -> p a (b n)", a=2),
                           A["sh_down"][L1].rearrange("o (k p) n -> p (o k) n", p=P))
                for c in range(NT):
                    wait("shd_sb", c + 1, l)
                    sp.dma_start(acc_dram[tk(c), :], X[:, c % 2, :]).then_inc(S[f"acc_dram{c % 2}"], 16)
                with sp.Fori(1, NE // NSLOT) as i:
                    for s in range(NSLOT):
                        sp.wait_ge(S["dn_ps"], l * NE + i * NSLOT + (s - NSLOT + 1))
                        past()
                        expert(s, i * NSLOT + s)
                wait("oe_ready", 2 * NE, l)
                sp.wait_ge(S["flag_ready"], l + 1)
                sp.sem_inc(S["past"], 1)
                over = sp.value_load(flagi[0:1, 0:1], min_val=0, max_val=1)
                with sp.If(over > 0):
                    with sp.Fori(1, NBLK) as b:
                        with sp.Fori(0, NE) as e:
                            one = bass.ds(e, 1)
                            sp.wait_ge(S["ov_sc"], l * OVER + b * NE + e + (1 - NE))
                            past()
                            sp.dma_start(wgu[0][:, :, 0:ED], gate_w[:, one].rearrange("p e k n -> p (e k) n")).then_inc(S["ov_w"], 16)
                            sp.dma_start(wgu[0][:, :, ED:2 * ED], up_w[:, one].rearrange("p e k n -> p (e k) n")).then_inc(S["ov_w"], 16)
                            sp.dma_start(wdn[0][:, :, :], down_w[:, one].rearrange("p e k n -> p (e k) n")).then_inc(S["ov_w"], 16)
                            sp.dma_start(idxS[0][:, :], tab_dram[bass.ds(b * P, P), one, :].rearrange("p o t -> p (o t)")).then_inc(S["ov_tab"], 16)
                with sp.Else():
                    sp.sem_inc(S["ov_w"], PER["ov_w"])
                    sp.sem_inc(S["ov_tab"], PER["ov_tab"])
                for c in range(NT):
                    wait("ov_sc", OVER + 1, l)
                    if c >= 2:
                        wait("acc_added", c - 1, l)
                    sp.dma_start(X[:, c % 2, :], acc_dram[tk(c), :]).then_inc(S[f"acc_loaded{c % 2}"], 16)
            sp.wait_ge(S["h_ready"], DEPTH + 1)
            sp.dma_start(grow[:, 0, :], A["norm_final"].rearrange("(o f) -> o f", o=1).to_broadcast([P, DM])).then_inc(S["out_loaded"], 16)
            for c in range(2):
                sp.wait_ge(S["out_ready"], c + 1)
                sp.dma_start(out[0, tk(c), :], X[:, c, :]).then_inc(S["out_stored"], 16)
            sp.wait_ge(S["out_stored"], 32)

        @block.gpsimd
        def _(pool):
            G = nc.gpsimd

            def wait(name, n, l):
                pool.wait_ge(S[name], l * PER[name] + n)
                pool.sem_inc(S["past"], 1)

            def do(ins, name=None, n=1):
                if name:
                    ins.then_inc(S[name], n)
                pool.drain()

            do(G.memset(ones[:, :], 1.0))
            do(G.memset(bd[:, :], 0.0))
            do(G.memset(bd[0:HD, 0:HD], 1.0))
            do(G.memset(bd[HD:P, HD:P], 1.0))
            do(G.affine_select(tri[:, 0, :], ones[:, :], [[1, P]], ALU.is_ge, 0.0, base=0, channel_multiplier=-1))
            do(G.affine_select(tri[:, 1, :], ones[:, :], [[-1, P]], ALU.is_ge, 0.0, base=0, channel_multiplier=1))
            do(G.affine_select(triS[:, :], ones[:, :], [[1, P]], ALU.is_gt, 0.0, base=0, channel_multiplier=-1))
            do(G.affine_select(ident[:, :], ones[:, :], [[1, P]], ALU.is_equal, 0.0, base=0, channel_multiplier=-1))
            do(G.iota(levt[:, 0, :], pattern=[[0, P]], base=0, channel_multiplier=1))
            do(G.iota(levt[:, 1, :], pattern=[[1, P]], base=0, channel_multiplier=0))
            do(G.iota(tokid[:, :], pattern=[[P, NT]], base=0, channel_multiplier=1))
            do(G.iota(iota_e[:, :], pattern=[[1, NE]], base=0, channel_multiplier=0, allow_small_or_imprecise_dtypes=True))
            do(G.memset(live[:, :, :], 1.0))
            do(G.memset(live[:, DEPTH - 1, 0:CTX // P], 0.0))
            do(G.memset(cst[:, 0:1], EPS))
            do(G.memset(cst[:, 1:2], -math.log(math.sqrt(HD))))
            do(G.memset(cst[:, 2:3], -40.0 * math.log(2.0)))
            do(G.memset(cst[:, 3:4], 0.0))
            pool.sem_inc(S["ring_used"], 2)
            pool.sem_inc(S["ov_sc"], 1)
            pool.drain().then_inc(S["const_pool"], 1)
            with pool.Fori(0, DEPTH) as l:
                wait("h_ready", 1, l)
                do(G.memset(Ss[:, :, :, :], 0.0))
                do(G.memset(Sh[:, :, :, :], 0.0))
                do(G.memset(Sg[:, :, :, :], 0.0), "s_init")
                wait("tok_d", NT, l)
                for u, (i, d, c) in enumerate(UNITS):
                    wait("small_done", 1, l) if u == 0 else wait("ho_ps", u, l)
                    if u:
                        wait("go_ps", u, l)
                    do(G.memset(attH[:, :, :], 0.0), "a_init")
                    do(G.tensor_copy(T[:, :, :], ident[:, :].unsqueeze(1).to_broadcast([P, HH, P])))
                    do(G.tensor_copy(TT[:, :, :], ident[:, :].unsqueeze(1).to_broadcast([P, HH, P])), "t_init")
                    wait("hexp", u + 1, l)
                    do(G.tensor_tensor(kL[:, :, :].rearrange("p j (t s) -> p j t s", t=2),
                                       e7[:, :, :].rearrange("p j (t s) -> p j t s", t=2),
                                       hk[:, d, :, tk(c)].unsqueeze(1).to_broadcast([P, LEVELS, 2, P]), ALU.mult), "kl_ready")
                    do(G.tensor_tensor(kw[:, :].rearrange("p (h k) -> p h k", h=HH),
                                       Ktok[:, c, :].rearrange("p (h k) -> p h k", h=HH),
                                       wend[:, c, d, HS:NDEC].unsqueeze(2).to_broadcast([P, HH, HD]), ALU.mult), "kw_ready")
                    for j in range(LEVELS):
                        if j == 0:
                            wait("at_ready", u + 1, l)
                        else:
                            wait("p_ps", u * LEVELS + j, l)
                        do(G.tensor_tensor(NTm[:, :, :], AT[:, :, :],
                                           lev[:, d, j, :].unsqueeze(1).to_broadcast([P, HH, P]), ALU.mult), "nt_ready")
                wait("blank_ready", 1, l)
                pool.dma_start(tab_dram.rearrange("a e t -> (a e t)").rearrange("(p n) -> p n", p=P),
                               blank[:, :, :].rearrange("p a b -> p (a b)")).then_inc(S["blank_dram"], 16)
                wait("blank_dram", 16, l)
                wait("pay_ready", 1, l)
                rows = tab_dram.rearrange("a e t -> (a e) t")
                for n in range(NT * TOPK):
                    pool.indirect_dma_start(rows, bass.IndirectOffsetOnAxis(dsti[:, n, :].bitcast(U32), 0), pay[:, n, :], None,
                                            bounds_check=CAP * NE - 1, oob_is_err=False).then_inc(S["tab_dram"], 16)
                wait("tab_dram", 16 * NT * TOPK, l)
                wait("shd_ps", NT, l)
                wait("shd_sb", NT, l)
                pool.dma_start(tabA[:, :, :], tab_dram[0:P, :, :]).then_inc(S["tab_loaded"], 16)
                do(G.memset(xg[0], 0.0))
                do(G.memset(xg[1], 0.0), "xg_init")
                wait("tab_loaded", 16, l)
                for b in range(2):
                    wait(f"ftok_dram{b}", 32, l)
                    wait(f"acc_dram{b}", 32, l)

                def gather(s, e):
                    do(G.tensor_copy(idxS[s][:, :].bitcast(I32), tabA[:, bass.ds(e, 1), :].rearrange("p a t -> p (a t)").bitcast(I32)))
                    pool.indirect_dma_start(xg[s % 2], None, f_dram, bass.IndirectOffsetOnAxis(idxS[s][:, 0:1].bitcast(U32), 0),
                                            bounds_check=TOK - 1, oob_is_err=False).then_inc(S[f"gathered{s}"], 16)

                def scatter(s):
                    pool.indirect_dma_start(acc_dram, bass.IndirectOffsetOnAxis(idxS[s][:, 0:1].bitcast(U32), 0), oe[s % 2], None,
                                            bounds_check=TOK - 1, oob_is_err=False, compute_op=ALU.add).then_inc(S["scattered"], 16)

                def pool_step(i, s, more):
                    e = l * NE + i * NSLOT + s
                    if more > 3:
                        pool.wait_ge(S["xt_ps"], e + 2)
                        pool.sem_inc(S["past"], 1)
                        gather((s + 3) % NSLOT, i * NSLOT + s + 3)
                    pool.wait_ge(S["oe_ready"], e * 2 + 2)
                    pool.sem_inc(S["past"], 1)
                    scatter(s)
                    pool.wait_ge(S["scattered"], e * 16 + 16)
                    pool.sem_inc(S["past"], 1)
                    pool.drain()

                gather(0, 0)
                gather(1, 1)
                wait("xt_ps", 1, l)
                gather(2, 2)
                with pool.Fori(0, NE // NSLOT - 1) as i:
                    for s in range(NSLOT):
                        pool_step(i, s, 5)
                for s in range(NSLOT):
                    pool_step(NE // NSLOT - 1, s, NSLOT - s)
                pool.wait_ge(S["flag_ready"], l + 1)
                pool.sem_inc(S["past"], 1)
                over = pool.value_load(flagi[0:1, 0:1], min_val=0, max_val=1)
                with pool.If(over > 0):
                    with pool.Fori(1, NBLK) as b:
                        with pool.Fori(0, NE) as e:
                            n = l * OVER + b * NE + e - NE
                            pool.wait_ge(S["ov_tab"], n * 16 + 16)
                            pool.sem_inc(S["past"], 1)
                            pool.indirect_dma_start(xg[0], None, f_dram, bass.IndirectOffsetOnAxis(idxS[0][:, 0:1].bitcast(U32), 0),
                                                    bounds_check=TOK - 1, oob_is_err=False).then_inc(S["ov_dma"], 16)
                            pool.wait_ge(S["ov_dma"], 16)
                            pool.dma_reset(range(S["ov_dma"].num, S["ov_dma"].num + 1))
                            pool.sem_clear(S["ov_dma"])
                            pool.drain().then_inc(S["ov_g"], 1)
                            pool.wait_ge(S["ov_oe"], n + 1)
                            pool.sem_inc(S["past"], 1)
                            pool.indirect_dma_start(acc_dram, bass.IndirectOffsetOnAxis(idxS[0][:, 0:1].bitcast(U32), 0), oe[0], None,
                                                    bounds_check=TOK - 1, oob_is_err=False, compute_op=ALU.add).then_inc(S["ov_dma"], 16)
                            pool.wait_ge(S["ov_dma"], 16)
                            pool.dma_reset(range(S["ov_dma"].num, S["ov_dma"].num + 1))
                            pool.sem_clear(S["ov_dma"])
                            pool.drain().then_inc(S["ov_sc"], 1)
                with pool.Else():
                    pool.sem_inc(S["ov_g"], PER["ov_g"])
                    pool.sem_inc(S["ov_sc"], PER["ov_sc"])

        @block.scalar
        def _(act):
            C = nc.scalar

            def wait(name, n, l):
                act.wait_ge(S[name], l * PER[name] + n)

            def do(ins, name=None):
                if name:
                    ins.then_inc(S[name], 1)
                act.drain()

            def f(out_, in_, func, name=None, **kw):
                do(C.activation(out_, in_, func, **kw), name)

            act.wait_ge(S["const_pool"], 1)
            act.wait_ge(S["cond_ps"], 1)
            f(condT[:, :, :].rearrange("p a k -> p (a k)"), ps[:, 0, 0:2 * KT], ACT.Silu, "cond_sb")
            act.wait_ge(S["low_a"], 1)
            f(low[:, :, :], low[:, :, :], ACT.Exp, "low_b")

            def norm_turn(q, l):
                wait("sumsq", q + 1, l)
                f(st[:, 4:8], st[:, 0:4], ACT.Ln, scale=1.0 / DM, bias=cst[:, 0:1])
                f(st[:, 8:12], st[:, 4:8], ACT.Exp, "rstd", scale=-0.5)
                for c in range(NT):
                    wait("xT_ps", q * NT + c + 1, l)
                    for k in range(KT // 2, KT):
                        ins = C.activation(featT[:, k, tk(c)], bank(4 + 2 * (c % 2), 2)[:, tk(k)], ACT.Identity,
                                           scale=amul[:, q, k, c // 2:c // 2 + 1], bias=mod[:, 24 * q + k, c // 2:c // 2 + 1])
                    do(ins, "feat_a")

            with act.Fori(0, DEPTH) as l:
                wait("h_ready", 1, l)
                wait("mod_sb", 1, l)
                norm_turn(0, l)
                for n in range(N_CONV):
                    for half in range(2):
                        t = 2 * n + half
                        wait("conv_out", t + 1, l)
                        b = prm[:, R_CBS + t:R_CBS + t + 1] if t < 8 else cst[:, 3:4]
                        C.activation(cv[:, t, 0:CTX], cvo[:, half, 0:CTX], ACT.Silu, bias=b)
                        do(C.activation(cv[:, t, CTX:TOK].rearrange("p (r x) -> p r x", r=ROWS),
                                        line_rows(cvo[:, half, :]), ACT.Silu, bias=b), "silu_out")
                for n in range(N_CONV, N_IN):
                    kind, _, i = IN_BLOCKS[n]
                    b0 = UB[n % 3]
                    wait("u_ps", n + 1, l)
                    if kind == "hq":
                        f(hq[:, :, :], ps[:, b0:b0 + 2, :], ACT.Silu, "u_act")
                    elif kind == "gate":
                        f(gates[:, :, i * BW:(i + 1) * BW], bank(b0, 2).rearrange("p (c f) -> p c f", c=NT), ACT.Silu, "u_act")
                    elif kind == "val":
                        f(val[:, :, :], bank(b0, 2).rearrange("p (c f) -> p c f", c=NT), ACT.Identity, "u_act")
                    else:
                        f(logf[:, i, :, :], ps[:, b0:b0 + 2, :], ACT.Identity, "u_act")
                wait("sp_x", 1, l)
                f(nega[:, :, :], alog[:, :, :], ACT.Exp)
                f(beta[:, :, :, :], beta[:, :, :, :], ACT.Exp, scale=-1.0)
                f(spw[:, 1, :], spw[:, 0, :], ACT.Abs)
                f(spw[:, 1, :], spw[:, 1, :], ACT.Exp, scale=-1.0)
                f(spw[:, 2, :], spw[:, 1, :], ACT.Ln, "sp_exp", bias=ones[:, 0:1])
                wait("low_c", 1, l)
                f(lowv[:, 1, :], lowv[:, 1, :], ACT.Ln)
                f(lowv[:, 1, :], lowv[:, 1, :], ACT.Identity, "lowl", bias=cst[:, 2:3])
                f(hwt[:, :, :], logf[:, :, :, :].rearrange("p a b t -> p (a b) t"), ACT.Abs)
                f(hwt[:, :, :], hwt[:, :, :], ACT.Exp, scale=-1.0)
                f(hwt[:, :, :], hwt[:, :, :], ACT.Ln, "hg_b", bias=ones[:, 0:1])
                wait("hg_c", 1, l)
                f(hwt[:, :, :], hwx[:, :, :], ACT.Abs)
                f(hwt[:, :, :], hwt[:, :, :], ACT.Exp, scale=-1.0)
                f(hwt[:, :, :], hwt[:, :, :], ACT.Ln, "hg_d", bias=ones[:, 0:1])
                wait("hg_e", 1, l)
                f(hk[:, :, :, :].rearrange("p a b t -> p (a b) t"), hwt[:, :, :], ACT.Exp, "hg_f")
                wait("cum_dve", 1, l)
                f(eacs[:, :, :, :], acs[:, :, :, :], ACT.Exp)
                f(wend[:, :, :, :], wend[:, :, :, :], ACT.Exp)
                f(etot[:, :, :, :], etot[:, :, :, :], ACT.Exp, "cum_act")
                for t in range(4):
                    wait("l2_ps", t + 1, l)
                    f(lnw[:, :], ps[:, t % 2, :], ACT.Ln, bias=cst[:, 0:1])
                    if t:
                        wait("l2_done", t, l)
                    f(lnx[:, :], lnw[:, :], ACT.Exp, "l2_act", scale=-0.5, bias=cst[:, 1:2] if t < 2 else cst[:, 3:4])
                for c in range(NT):
                    wait("tok_ps", c + 1, l)
                    b0 = 4 * (c % 2)
                    C.activation(Btok[:, c, :], ps[:, b0 + 1, 0:HW], ACT.Identity)
                    do(C.activation(Ktok[:, c, :], ps[:, b0 + 1, HW:2 * HW], ACT.Identity), "tok_a")
                for u, (i, d, c) in enumerate(UNITS):
                    wait("b_ready", u + 1, l)
                    f(e7[:, :, :], e7[:, :, :], ACT.Abs)
                    f(e7[:, :, :], e7[:, :, :], ACT.Exp, scale=-1.0)
                    f(eb[:, :], bh[:, :], ACT.Exp)
                    f(e1[:, :], e1[:, :], ACT.Exp, "hexp", scale=-1.0)
                    wait("dm_ready", u + 1, l)
                    f(E[:, :, :], E[:, :, :], ACT.Exp, "e_ready")
                    for j in range(LEVELS):
                        wait("p_ps", u * LEVELS + j + 1, l)
                        f(Pm[:, :, :].rearrange("p h t -> p (h t)"), ps[:, 1, :], ACT.Identity, "p_sb")
                        if j == 5:
                            wait("ke_ps", u + 1, l)
                            f(kendT[:, :], ps[:, 5, 0:2 * P], ACT.Identity, "ke_sb")
                    wait("vn_ps", u + 1, l)
                    f(vn[:, :], ps[:, 1, HW:2 * HW], ACT.Identity, "vn_sb")
                wait("y_sq", 1, l)
                f(ssq[:, :, 0:2], ssq[:, :, 0:2], ACT.Ln, scale=1.0 / HW, bias=cst[:, 0:1])
                f(ssq[:, :, 2:10], ssq[:, :, 2:10], ACT.Ln, scale=1.0 / HD, bias=cst[:, 0:1])
                f(ssq[:, :, :], ssq[:, :, :], ACT.Exp, "y_rstd", scale=-0.5)
                for j in range(2):
                    wait("grow_ps", j + 1, l)
                    f(grow[:, j, :], bank(2 * j, 2), ACT.Identity, "grow_sb")
                for c in range(NT):
                    wait("yT_ps", c + 1, l)
                    f(yT[:, :, tk(c)], bank(4 + 2 * (c % 2), 2).rearrange("p (k t) -> p k t", k=KT), ACT.Identity, "yT_sb")
                norm_turn(1, l)
                wait("lg_ps", 1, l)
                f(scor[:, :, :], ps[:, 0, 0:NT * NE].rearrange("p (c e) -> p c e", c=NT), ACT.Exp, "lg_exp", scale=-1.0)
                wait("sh_ps", 1, l)
                f(sgT[:, :, :], ps[:, 0:2, :], ACT.Silu, "sh_silu")
                def turned(e, b):
                    act.wait_ge(S["xt_ps"], e + 1)
                    do(C.activation(xgT[b][:, 0:4, :].rearrange("p k t -> p (k t)"), ps[:, 0, :], ACT.Identity), "xt_sb")

                def silu(e, b):
                    act.wait_ge(S["gu_ps"], e + 1)
                    f(sg[b], ps[:, 2 + b, 0:ED], ACT.Silu, "gu_silu")

                def act_step(i, s, more):
                    e = l * NE + i * NSLOT + s
                    if more > 1:
                        silu(e + 1, (s + 1) % 2)
                    act.wait_ge(S["hT_ps"], e + 1)
                    f(hTe[s % 2].rearrange("p k t -> p (k t)"), ps[:, 4, 0:2 * P], ACT.Identity, "hT_sb")
                    if more > 2:
                        turned(e + 2, s % 2)
                    act.wait_ge(S["dn_ps"], e + 1)
                    if not (isinstance(i, int) and i == 0 and s < 2):
                        act.wait_ge(S["scattered"], e * 16 - 16)
                    f(oe[s % 2][:, 0:512], ps[:, 5, :], ACT.Identity, "oe_ready", scale=idxS[s][:, 1:2])

                turned(l * NE, 0)
                silu(l * NE, 0)
                turned(l * NE + 1, 1)
                for s in range(NSLOT):
                    act_step(0, s, 5)
                with act.Fori(1, NE // NSLOT - 1) as i:
                    for s in range(NSLOT):
                        act_step(i, s, 5)
                for s in range(NSLOT):
                    act_step(NE // NSLOT - 1, s, NSLOT - s)
                act.wait_ge(S["flag_ready"], l + 1)
                act.sem_inc(S["past"], 1)
                over = act.value_load(flagi[0:1, 0:1], min_val=0, max_val=1)
                with act.If(over > 0):
                    with act.Fori(0, OVER) as n_:
                        n = l * OVER + n_
                        act.wait_ge(S["ov_gu"], n + 1)
                        f(sg[0], ps[:, 2, 0:ED], ACT.Silu, "ov_sl")
                with act.Else():
                    act.sem_inc(S["ov_sl"], OVER)
            act.wait_ge(S["out_sq"], 1)
            f(st[:, 4:6], st[:, 0:2], ACT.Ln, scale=1.0 / DM, bias=cst[:, 0:1])
            f(st[:, 8:10], st[:, 4:6], ACT.Exp, "out_ln", scale=-0.5)

        @block.vector
        def _(dve):
            V = nc.vector

            def wait(name, n, l):
                dve.wait_ge(S[name], l * PER[name] + n)

            def do(ins, name=None):
                if name:
                    ins.then_inc(S[name], 1)
                dve.drain()

            def tt(out_, a, b, op, name=None):
                do(V.tensor_tensor(out_, a, b, op), name)

            def ts(out_, a, s1, s2, op0, op1=None, name=None):
                do(V.tensor_scalar(out_, a, s1, s2, op0, *(() if op1 is None else (op1,))), name)

            def stt(out_, a, s_, b, op0, op1, name=None):
                do(V.scalar_tensor_tensor(out_, a, s_, b, op0, op1), name)

            def cp(out_, in_, name=None):
                do(V.tensor_copy(out_, in_), name)

            dve.wait_ge(S["const_pool"], 1)
            tt(levt[:, 0, :], levt[:, 0, :], levt[:, 1, :], ALU.bitwise_xor)
            for j in range(LEVELS):
                ts(levt[:, 1, :], levt[:, 0, :], j, None, ALU.logical_shift_right)
                cp(lev[:, 0, j, :], levt[:, 1, :])
                ts(lev[:, 0, j, :], lev[:, 0, j, :], 1.0, None, ALU.is_equal)
                tt(lev[:, 1, j, :], lev[:, 0, j, :], tri[:, 1, :], ALU.mult)
                tt(lev[:, 0, j, :], lev[:, 0, j, :], triS[:, :], ALU.mult)
            for d in range(2):
                ts(negm[:, d, :], tri[:, d, :], -1.0, -NEG, ALU.add, ALU.mult)
            dve.drain().then_inc(S["const_ready"], 1)
            dve.wait_ge(S["cond_ps"], 1)
            cp(low[:, :, :].rearrange("p l t -> p (l t)"), ps[:, 3, 0:4])
            tt(lowv[:, 0, :], low[:, 0, :], low[:, 1, :], ALU.max)
            tt(low[:, :, :], low[:, :, :], lowv[:, 0:1, :].to_broadcast([P, DEPTH, 2]), ALU.subtract, "low_a")
            dve.wait_ge(S["low_b"], 1)
            tt(lowv[:, 0, :], low[:, 0, :], low[:, 1, :], ALU.add)
            do(V.reciprocal(lowv[:, 1, :], lowv[:, 0, :]))
            tt(low[:, :, :], low[:, :, :], lowv[:, 1:2, :].to_broadcast([P, DEPTH, 2]), ALU.mult)
            tt(lowv[:, 0, :], low[:, 0, :], low[:, 1, :], ALU.add)
            tt(low[:, 1, :], lowv[:, 0, :], low[:, 0, :], ALU.subtract)
            tt(low[:, 0, :], low[:, 0, :], low[:, 0, :], ALU.subtract)
            dve.wait_ge(S["cond_sb"], 1)
            dve.wait_ge(S["head_loaded"], 16 * 5)
            dve.drain().then_inc(S["h_ready"], 1)

            def norm_turn(q, l):
                for c in range(NT):
                    V.tensor_tensor_reduce(out=X[:, c % 2, :], in0=h[:, c, :], in1=h[:, c, :], scale=1.0, scalar=0.0,
                                           op0=ALU.mult, op1=ALU.add, accum_out=st[:, c:c + 1])
                    dve.drain()
                dve.drain().then_inc(S["sumsq"], 1)
                wait("rstd", q + 1, l)
                for c in range(NT):
                    if c >= 2:
                        wait("xT_ps", q * NT + c - 1, l)
                    ts(X[:, c % 2, :], h[:, c, :], st[:, 8 + c:9 + c], None, ALU.mult, name="xn")
                    if c >= 1:
                        turned(q, c - 1, l)
                turned(q, NT - 1, l)

            def turned(q, c, l):
                wait("xT_ps", q * NT + c + 1, l)
                for k in range(KT // 2):
                    ins = V.tensor_scalar(featT[:, k, tk(c)], bank(4 + 2 * (c % 2), 2)[:, tk(k)],
                                          amul[:, q, k, c // 2:c // 2 + 1], mod[:, 24 * q + k, c // 2:c // 2 + 1],
                                          ALU.mult, ALU.add)
                do(ins, "feat_d")

            with dve.Fori(0, DEPTH) as l:
                L1 = bass.ds(l, 1)
                wait("prm_ps", 1, l)
                cp(prm[:, :], ps[:, 1, 0:N_PRM])
                cp(lowv[:, 0, :], low[:, L1, :].rearrange("p o t -> p (o t)"))
                ts(lowv[:, 2, :], lowv[:, 0, :], -1.0, 1.0, ALU.mult, ALU.add)
                ts(lowv[:, 1, :], lowv[:, 0, :], 1e-30, float(2.0 ** 40), ALU.max, ALU.mult, "low_c")
                wait("mod_ps", 1, l)
                tt(mod[:, :, :], ps[:, 2, 0:96].rearrange("p (r j) -> p r j", j=2),
                   prm[:, R_BMOD:R_BMOD + 48].unsqueeze(2).to_broadcast([P, 48, 2]), ALU.add)
                for q in range(2):
                    ts(amul[:, q, :, :], mod[:, 24 * q + 8:24 * q + 16, :], 1.0, None, ALU.add)
                    tt(amul[:, q, :, :], amul[:, q, :, :],
                       prm[:, R_NMIX + 8 * q:R_NMIX + 8 * q + 8].unsqueeze(2).to_broadcast([P, KT, 2]), ALU.mult)
                dve.drain().then_inc(S["mod_sb"], 1)
                norm_turn(0, l)
                do(V.memset(line[:, :, :], 0.0))
                for n in range(N_CONV):
                    wait("u_ps", n + 1, l)
                    for half in range(2):
                        src = ps[:, UB[n % 3] + half, :]
                        V.tensor_copy(line[:, half, HALF:HALF + CTX], src[:, 0:CTX])
                        V.tensor_copy(line[:, half, CPAD:LINE].rearrange("p (r x) -> p r x", r=ROWS)[:, :, HALF:HALF + GRID_W],
                                      src[:, CTX:TOK].rearrange("p (r x) -> p r x", r=ROWS))
                    dve.drain().then_inc(S["u_dve"], 1)
                    for half in range(2):
                        t = 2 * n + half
                        base, off, per = (R_CWS, t, 8) if t < 8 else (R_CWG, t - 8, 6)
                        if n:
                            wait("silu_out", t - 1, l)
                        for j in range(TAPS):
                            w = prm[:, base + j * per + off:base + j * per + off + 1]
                            o, s_ = cvo[:, half, 0:CONV], line[:, half, j:j + CONV]
                            if j == 0:
                                ts(o, s_, w, None, ALU.mult)
                            else:
                                stt(o, s_, w, o, ALU.mult, ALU.add, "conv_out" if j == TAPS - 1 else None)
                wait("sm_ps", 1, l)
                cp(sm[:, :, :].rearrange("p c f -> p (c f)"), ps[:, 3, 0:32 * NT])
                x3 = spw[:, 0, :].rearrange("p (c d h) -> p c d h", c=NT, d=2)
                for c in range(NT):
                    tt(x3[:, c, :, 0:HS], sm[:, c, 0:16].rearrange("p (d h) -> p d h", d=2), dtb[:, :, 0:HS], ALU.add)
                    tt(x3[:, c, :, HS:NDEC], sm[:, c, 16:24].rearrange("p (d h) -> p d h", d=2), dtb[:, :, HS:NDEC], ALU.add)
                    cp(beta[:, c, :, :].rearrange("p d h -> p (d h)"), sm[:, c, 24:32])
                dve.drain().then_inc(S["sp_x"], 1)
                wait("sp_exp", 1, l)
                ts(beta[:, :, :, :], beta[:, :, :, :], 1.0, None, ALU.add)
                do(V.reciprocal(beta[:, :, :, :], beta[:, :, :, :]))
                ts(spw[:, 3, :], spw[:, 1, :], 1.0, None, ALU.add)
                ts(spw[:, 3, :], spw[:, 3, :], -1.0, None, ALU.add)
                dtf = dt_[:, :, :, :].rearrange("p c d h -> p (c d h)")
                daf = da[:, :, :, :].rearrange("p c d h -> p (c d h)")
                ts(dtf, spw[:, 3, :], 0.0, None, ALU.is_equal)
                tt(spw[:, 2, :], spw[:, 2, :], dtf, ALU.add)
                tt(spw[:, 3, :], spw[:, 3, :], dtf, ALU.add)
                do(V.reciprocal(spw[:, 3, :], spw[:, 3, :]))
                tt(spw[:, 1, :], spw[:, 1, :], spw[:, 3, :], ALU.mult)
                tt(spw[:, 1, :], spw[:, 1, :], spw[:, 2, :], ALU.mult)
                stt(dtf, spw[:, 0, :], 0.0, spw[:, 1, :], ALU.max, ALU.add)
                stt(da[:, :, :, :].rearrange("p c d h -> p c (d h)"), dt_[:, :, :, :].rearrange("p c d h -> p c (d h)"), -1.0,
                    nega[:, :, :].rearrange("p d h -> p (d h)").unsqueeze(1).to_broadcast([P, NT, 2 * NDEC]),
                    ALU.mult, ALU.mult, "sp_done")
                wait("u_act", N_IN - N_CONV, l)
                wait("lowl", 1, l)
                raw = logf[:, :, :, :].rearrange("p a b t -> p (a b) t")
                ls = hk[:, :, :, :].rearrange("p a b t -> p (a b) t")
                for q in range(4):
                    V.tensor_scalar(hwx[:, q, :], raw[:, q, :], -1.0, lowv[:, 1, q % 2:q % 2 + 1], ALU.mult, ALU.add)
                dve.drain()
                wait("hg_b", 1, l)
                stt(ls, raw, 0.0, hwt[:, :, :], ALU.min, ALU.subtract)
                dve.drain().then_inc(S["hg_c"], 1)
                wait("cum_ps", 1, l)
                for d in range(2):
                    cp(acs[:, :, d, :], ps[:, 2, 48 * d:48 * d + 48].rearrange("p (c h) -> p c h", c=NT))
                cp(etot[:, :, :, :].rearrange("p c d h -> p (c d h)"), ps[:, 2, 96:192])
                tt(wend[:, :, :, :], etot[:, :, :, :], acs[:, :, :, :], ALU.subtract, "cum_dve")
                wait("hg_d", 1, l)
                stt(hwx[:, :, :], hwx[:, :, :], 0.0, hwt[:, :, :], ALU.max, ALU.add)
                tt(hwt[:, :, :], ls, raw, ALU.subtract)
                tt(raw, ls, hwx[:, :, :], ALU.add, "hg_e")
                for t in range(4):
                    if t >= 2:
                        wait("l2_ps", t - 1, l)
                    tt(sqw[:, t % 2, :], cv[:, 8 + t, :], cv[:, 8 + t, :], ALU.mult, "l2_sq")
                    if t >= 1:
                        wait("l2_act", t, l)
                        tt(cv[:, 7 + t, :], cv[:, 7 + t, :], lnx[:, :], ALU.mult, "l2_done")
                wait("l2_act", 4, l)
                tt(cv[:, 11, :], cv[:, 11, :], lnx[:, :], ALU.mult, "l2_done")
                wait("hg_f", 1, l)
                for t in range(2):
                    ts(hk[:, :, t, :], hk[:, :, t, :], lowv[:, 2, t:t + 1], None, ALU.mult)
                dve.drain()
                wait("cum_act", 1, l)
                tt(wdt[:, :, :, :], dt_[:, :, :, :], wend[:, :, :, :], ALU.mult)
                for t in range(2):
                    for par in range(2):
                        rows = slice(par * HD, (par + 1) * HD)
                        cp(dcol[rows, :, t], etot[rows, :, :, HS + 2 * t + par].rearrange("p c d -> p (c d)"))
                dve.drain().then_inc(S["small_done"], 1)
                for c in range(NT):
                    wait("tok_ps", c + 1, l)
                    b0 = 4 * (c % 2)
                    cp(cv[:, 0:4, tk(c)], ps[:, b0, :].rearrange("p (t f) -> p t f", t=4))
                    cp(cv[:, 12:14, tk(c)], ps[:, b0 + 2, 0:HW].rearrange("p (t f) -> p t f", t=2), "tok_d")
                wait("s_init", 1, l)
                for u, (i, d, c) in enumerate(UNITS):
                    first, last_step = SEEN[c] == u, i == NT - 1
                    end = P - 1 if d == 0 else 0
                    way = slice(None) if d == 0 else slice(None, None, -1)
                    b3 = bh[:, :].rearrange("p (t s) -> p t s", t=2)
                    for t in range(2):
                        V.tensor_tensor_scan(b3[:, t, way], ones[:, :], logf[:, d, t, tk(c)][:, way], 0.0, ALU.mult, ALU.add)
                    dve.drain()
                    for j in range(LEVELS):
                        w = 2 << j
                        mid = w // 2 - 1 if d == 0 else w // 2
                        v = bh[:, :].rearrange("p (n w) -> p n w", w=w)
                        V.tensor_tensor(e7[:, j, :].rearrange("p (n w) -> p n w", w=w), v,
                                        v[:, :, mid:mid + 1].to_broadcast([P, 2 * P // w, w]), ALU.subtract)
                    V.tensor_tensor(e1[:, :].rearrange("p (t s) -> p t s", t=2), b3, b3[:, :, end:end + 1].to_broadcast([P, 2, P]), ALU.subtract)
                    dve.drain().then_inc(S["b_ready"], 1)
                    wait("pre_ps", u + 1, l)
                    tt(E[:, :, :], bank(3, 3).rearrange("p (h t) -> p h t", h=NDEC),
                       acs[:, c, d, :].unsqueeze(2).to_broadcast([P, NDEC, P]), ALU.subtract)
                    tt(E[:, :, :], E[:, :, :], negm[:, d, :].unsqueeze(1).to_broadcast([P, NDEC, P]), ALU.add, "dm_ready")
                    wait("hexp", u + 1, l)
                    q3 = hq[:, :, tk(c)]
                    cp(hdec[:, :], eb[:, :].rearrange("p (t s) -> p t s", t=2)[:, :, end])
                    tt(eb[:, :].rearrange("p (t s) -> p t s", t=2), eb[:, :].rearrange("p (t s) -> p t s", t=2), q3, ALU.mult)
                    tt(kend[:, :].rearrange("p (t s) -> p t s", t=2), e1[:, :].rearrange("p (t s) -> p t s", t=2), hk[:, d, :, tk(c)], ALU.mult)
                    wait("e_ready", u + 1, l)
                    par_view = lambda ap: ap.rearrange("p (a b) t -> p b a t", b=2)
                    kk = ps[:, 1:3, 0:HW].rearrange("p b (a t) -> p b a t", a=2)
                    qk = ps[:, 1:3, HW:2 * HW].rearrange("p b (a t) -> p b a t", a=2)
                    tt(par_view(AT[:, :, :]), kk, par_view(E[:, HS:NDEC, :]), ALU.mult)
                    tt(AT[:, :, :].rearrange("p h t -> p (h t)"), AT[:, :, :].rearrange("p h t -> p (h t)"), ps[:, 6, :], ALU.mult)
                    tt(par_view(E[:, HS:NDEC, :]), qk, par_view(E[:, HS:NDEC, :]), ALU.mult, "at_ready")
                    tt(E[:, 0:HS, :], E[:, 0:HS, :], dt_[:, c, d, 0:HS].unsqueeze(2).to_broadcast([P, HS, P]), ALU.mult)
                    tt(E[:, 0:HS, :].rearrange("p (g r) t -> p g r t", g=NG), E[:, 0:HS, :].rearrange("p (g r) t -> p g r t", g=NG),
                       ps[:, 0, 0:NG * P].rearrange("p (g t) -> p g t", g=NG).unsqueeze(2).to_broadcast([P, NG, HS // NG, P]), ALU.mult)
                    xs = cv[:, 0:4, tk(c)].rearrange("p a (b x) -> p a b x", b=2)
                    by_head = lambda ap: ap.rearrange("p (a b x) -> p a b x", a=4, b=2)
                    heads = lambda v: v.rearrange("p (a b) -> p a b", b=2).unsqueeze(3).to_broadcast([P, 4, 2, HD])
                    tt(by_head(xw[:, :]), xs, heads(wdt[:, c, d, 0:HS]), ALU.mult, "att_ready")
                    wait("kl_ready", u + 1, l)
                    tt(e7[:, :, :].rearrange("p j (t s) -> p j t s", t=2), e7[:, :, :].rearrange("p j (t s) -> p j t s", t=2),
                       q3.unsqueeze(1).to_broadcast([P, LEVELS, 2, P]), ALU.mult, "ql_ready")
                    for j in range(LEVELS):
                        wait("q_ps", u * LEVELS + j + 1, l)
                        if j < LEVELS - 1:
                            tt(T[:, :, :].rearrange("p h t -> p (h t)"), T[:, :, :].rearrange("p h t -> p (h t)"), ps[:, 2, :], ALU.subtract)
                        tt(TT[:, :, :].rearrange("p h t -> p (h t)"), TT[:, :, :].rearrange("p h t -> p (h t)"), ps[:, 3, :],
                           ALU.subtract, "t_ready")
                        if j < 4:
                            if j == 0:
                                wait("a_init", u + 1, l)
                            wait("h_ps", u * 4 + j + 1, l)
                            dve.sem_inc(S["past"], 1)
                            for r in range(2):
                                lv = 2 * j + r
                                m = lev[:, d, lv, :] if lv < LEVELS else ident[:, :]
                                do(V.copy_predicated(par_view(attH[:, :, :]),
                                                     m.bitcast(I32).unsqueeze(1).unsqueeze(1).to_broadcast([P, 2, 2, P]),
                                                     ps[:, 4:6, r * HW:(r + 1) * HW].rearrange("p b (a t) -> p b a t", a=2)),
                                   "h_cp" if r else None)
                        if j == 4:
                            wait("ssd_ps", u + 1, l)
                            tt(by_head(tmp[:, :]), by_head(ps[:, 6, :]), heads(eacs[:, c, d, 0:HS]), ALU.mult)
                            if first:
                                tt(yraw[:, c, 0:SW], tmp[:, :], ps[:, 7, :], ALU.add)
                                tt(by_head(tmp[:, :]), xs, heads(dsk[:, :]), ALU.mult)
                            else:
                                tt(tmp[:, :], tmp[:, :], ps[:, 7, :], ALU.add)
                            tt(yraw[:, c, 0:SW], yraw[:, c, 0:SW], tmp[:, :], ALU.add, "ssd_sb" if last_step else None)
                            if not last_step:
                                sv = Ss[:, d, :, :].rearrange("p g f -> p (g f)")
                                tt(by_head(sv), by_head(sv), heads(etot[:, c, d, 0:HS]), ALU.mult)
                                tt(sv, sv, ps[:, 0, :], ALU.add, "ssd_sb")
                    wait("gks_ps", u + 1, l)
                    r3 = rr[:, :].rearrange("p (h v) -> p h v", h=HH)
                    gdn = lambda v: v.unsqueeze(2).to_broadcast([P, HH, HD])
                    tt(r3, ps[:, 1, 0:HW].rearrange("p (h v) -> p h v", h=HH), gdn(eacs[:, c, d, HS:NDEC]), ALU.mult)
                    r22 = rr[:, :].rearrange("p (a f) -> p a f", a=2)
                    tt(r22, cv[:, 12:14, tk(c)], r22, ALU.subtract)
                    tt(r3, r3, gdn(beta[:, c, d, :]), ALU.mult, "r_ready")
                    wait("ho_ps", u + 1, l)
                    o = yraw[:, c, SW:SW + HW]
                    if first:
                        cp(o, ps[:, 4, 0:HW])
                    else:
                        tt(o, o, ps[:, 4, 0:HW], ALU.add)
                    if last_step:
                        dve.drain().then_inc(S["hgrn_done"], 1)
                    else:
                        tt(tmp[:, 0:2 * P].rearrange("p (t v) -> p t v", t=2), ps[:, 5, 2 * P:4 * P].rearrange("p (t v) -> p t v", t=2),
                           bd[:, :].unsqueeze(1).to_broadcast([P, 2, P]), ALU.mult)
                        for t in range(2):
                            stt(Sh[:, d, t, :], Sh[:, d, t, :], hdec[:, t:t + 1], tmp[:, t * P:(t + 1) * P], ALU.mult, ALU.add)
                        dve.drain().then_inc(S["hgrn_done"], 1)
                    wait("go_ps", u + 1, l)
                    t3 = tmp[:, 0:HW].rearrange("p (h v) -> p h v", h=HH)
                    tt(t3, ps[:, 2, 0:HW].rearrange("p (h v) -> p h v", h=HH), gdn(eacs[:, c, d, HS:NDEC]), ALU.mult)
                    o = yraw[:, c, SW + HW:DM]
                    if first:
                        tt(o, tmp[:, 0:HW], ps[:, 2, HW:2 * HW], ALU.add)
                    else:
                        tt(tmp[:, 0:HW], tmp[:, 0:HW], ps[:, 2, HW:2 * HW], ALU.add)
                        tt(o, o, tmp[:, 0:HW], ALU.add)
                    if not last_step:
                        tt(tmp[:, 0:2 * P].rearrange("p (t v) -> p t v", t=2), ps[:, 3, 0:2 * P].rearrange("p (t v) -> p t v", t=2),
                           bd[:, :].unsqueeze(1).to_broadcast([P, 2, P]), ALU.mult)
                        for t in range(2):
                            stt(Sg[:, d, t, :], Sg[:, d, t, :], dcol[:, 2 * c + d, t:t + 1], tmp[:, t * P:(t + 1) * P], ALU.mult, ALU.add)
                    dve.drain().then_inc(S["gdn_done"], 1)
                for c in range(NT):
                    tt(yraw[:, c, 0:SW], yraw[:, c, 0:SW], gates[:, c, 0:SW], ALU.mult)
                    tt(sqo[:, 0, :], yraw[:, c, :], yraw[:, c, :], ALU.mult)
                    do(V.tensor_reduce(ssq[:, c, 0:2], sqo[:, 0, 0:SW].rearrange("p (g f) -> p g f", g=2), AX.X, ALU.add))
                    do(V.tensor_reduce(ssq[:, c, 2:10], sqo[:, 0, SW:DM].rearrange("p (g f) -> p g f", g=8), AX.X, ALU.add))
                dve.drain().then_inc(S["y_sq"], 1)
                wait("nrow_loaded", 16 * NROW_DMAS, l)
                for base in (SW, SW + HW):
                    cp(nrow[:, base + HD:base + 2 * HD], nrow[:, base:base + HD])
                    cp(nrow[:, base + 2 * HD:base + 4 * HD], nrow[:, base:base + 2 * HD])
                wait("y_rstd", 1, l)
                for c in range(NT):
                    y = yraw[:, c, :]
                    v2 = y[:, 0:SW].rearrange("p (g f) -> p g f", g=2)
                    tt(v2, v2, ssq[:, c, 0:2].unsqueeze(2).to_broadcast([P, 2, HW]), ALU.mult)
                    v8_ = y[:, SW:DM].rearrange("p (g f) -> p g f", g=8)
                    tt(v8_, v8_, ssq[:, c, 2:10].unsqueeze(2).to_broadcast([P, 8, HD]), ALU.mult)
                    tt(y, y, nrow, ALU.mult)
                    tt(y[:, SW:DM], y[:, SW:DM], gates[:, c, SW:DM], ALU.mult, "y_ready")
                wait("grow_sb", 2, l)
                for n in range(N_OUT):
                    wait("wo_ps", n + 1, l)
                    b0 = 4 + 2 * (n % 2)
                    cols = slice(n * BW, (n + 1) * BW)
                    for j in range(2):
                        o = X[:, 0, 0:2 * BW].rearrange("p (c f) -> p c f", c=2)
                        tt(o, ps[:, b0 + j, :].rearrange("p (c f) -> p c f", c=2), grow[:, j, cols].unsqueeze(1).to_broadcast([P, 2, BW]), ALU.mult)
                        tt(h[:, 2 * j:2 * j + 2, cols], h[:, 2 * j:2 * j + 2, cols], o, ALU.add, "wo_sb" if j else None)
                norm_turn(1, l)
                for c in range(NT):
                    wait("ftok_ps", c + 1, l)
                    if c >= 2:
                        wait(f"ftok_dram{c % 2}", 16 * (c // 2), l)
                    cp(X[:, c % 2, :], bank(4 + 2 * (c % 2), 2), "ftok_sb")
                wait("lg_exp", 1, l)
                do(V.memset(blank[:, :, 1:2], 0.0))
                do(V.memset(blank[:, :, 0:1].bitcast(I32), SKIP), "blank_ready")
                ts(scor[:, :, :], scor[:, :, :], 1.0, None, ALU.add)
                do(V.reciprocal(scor[:, :, :], scor[:, :, :]))
                tt(sel[:, :, :], scor[:, :, :], rbias[:, :].unsqueeze(1).to_broadcast([P, NT, NE]), ALU.add)
                for c in range(NT):
                    do(V.max(v8[:, c, :], sel[:, c, :]))
                    do(V.max_index(i8[:, c, :], v8[:, c, :], sel[:, c, :]))
                cp(if8[:, :, :], i8[:, :, :])
                eight = lambda ap: ap.unsqueeze(1).to_broadcast([P, TOPK, NE])
                for c in range(NT):
                    hv = hots[:, c, :].rearrange("p (k e) -> p k e", k=TOPK)
                    tt(hv, eight(iota_e[:, :]), if8[:, c, :].unsqueeze(2).to_broadcast([P, TOPK, NE]), ALU.is_equal)
                    do(V.tensor_reduce(mask[:, c, :], hots[:, c, :].rearrange("p (k e) -> p e k", k=TOPK), AX.X, ALU.add))
                cp(lcur[:, :], live[:, L1, :].rearrange("p o c -> p (o c)"))
                tt(mask[:, :, :], mask[:, :, :], lcur[:, :].unsqueeze(2).to_broadcast([P, NT, NE]), ALU.mult)
                ts(lcur[:, :], lcur[:, :], -float(SKIP), float(SKIP), ALU.mult, ALU.add)
                dve.drain().then_inc(S["mask_ready"], 1)
                for c in range(NT):
                    hv = hots[:, c, :].rearrange("p (k e) -> p k e", k=TOPK)
                    tt(hot2[:, :, :], hv, eight(scor[:, c, :]), ALU.mult)
                    do(V.tensor_reduce(s8[:, c, :], hot2[:, :, :], AX.X, ALU.add))
                do(V.tensor_reduce(gsum[:, :], s8[:, :, :], AX.X, ALU.add))
                do(V.reciprocal(gsum[:, :], gsum[:, :]))
                tt(s8[:, :, :], s8[:, :, :], gsum[:, :].unsqueeze(2).to_broadcast([P, NT, TOPK]), ALU.mult)
                ts(pay[:, :, 1], s8[:, :, :].rearrange("p c k -> p (c k)"), ROUTED_SCALE, None, ALU.mult)
                cp(pay[:, :, 0].bitcast(I32).rearrange("p (c k) -> p c k", c=NT), tokid[:, :].unsqueeze(2).to_broadcast([P, NT, TOPK]))
                wait("pos_ps", 1, l)
                cp(pos[:, :, :].rearrange("p c e -> p (c e)"), ps[:, 7, 0:NT * NE])
                for c in range(NT):
                    hv = hots[:, c, :].rearrange("p (k e) -> p k e", k=TOPK)
                    tt(hot2[:, :, :], hv, eight(pos[:, c, :]), ALU.mult)
                    do(V.tensor_reduce(p8[:, c, :], hot2[:, :, :], AX.X, ALU.add))
                stt(dst8[:, :, :], p8[:, :, :], float(NE), if8[:, :, :], ALU.mult, ALU.add)
                tt(dst8[:, :, :], dst8[:, :, :], lcur[:, :].unsqueeze(2).to_broadcast([P, NT, TOPK]), ALU.add)
                cp(dsti[:, :, 0], dst8[:, :, :].rearrange("p c k -> p (c k)"), "pay_ready")
                do(V.tensor_reduce(flag[0:1, 0:1], ps[0:1, 7, NT * NE:(NT + 1) * NE], AX.X, ALU.max))
                ts(flag[0:1, 1:2], flag[0:1, 0:1], float(P), None, ALU.is_gt)
                do(V.tensor_copy(flagi[0:1, 0:1], flag[0:1, 1:2]), "flag_ready")
                wait("sh_silu", 1, l)
                wait("sh_ps", 2, l)
                tt(hsh[:, :, :], sgT[:, :, :], ps[:, 2:4, :], ALU.mult, "sh_mul")
                for c in range(NT):
                    wait("shd_ps", c + 1, l)
                    wait(f"ftok_dram{c % 2}", 32, l) if c < 2 else wait(f"acc_dram{c % 2}", 16, l)
                    cp(X[:, c % 2, :], bank(4 + 2 * (c % 2), 2), "shd_sb")

                def x_half(e, b):
                    dve.wait_ge(S["xt_ps"], e + 1)
                    cp(xgT[b][:, 4:8, :].rearrange("p k t -> p (k t)"), ps[:, 1, :], "xt_sb")

                def gate_up(e, b):
                    dve.wait_ge(S["gu_silu"], e + 1)
                    tt(hgu[b], sg[b], ps[:, 2 + b, ED:2 * ED], ALU.mult, "gu_mul")

                def dve_step(i, s, more):
                    e = l * NE + i * NSLOT + s
                    if more > 1:
                        gate_up(e + 1, (s + 1) % 2)
                    if more > 2:
                        x_half(e + 2, s % 2)
                    dve.wait_ge(S["dn_ps"], e + 1)
                    if not (isinstance(i, int) and i == 0 and s < 2):
                        dve.wait_ge(S["scattered"], e * 16 - 16)
                    ts(oe[s % 2][:, 512:DM], ps[:, 6, :], idxS[s][:, 1:2], None, ALU.mult, name="oe_ready")

                x_half(l * NE, 0)
                gate_up(l * NE, 0)
                x_half(l * NE + 1, 1)
                for s in range(NSLOT):
                    dve_step(0, s, 5)
                with dve.Fori(1, NE // NSLOT - 1) as i:
                    for s in range(NSLOT):
                        dve_step(i, s, 5)
                for s in range(NSLOT):
                    dve_step(NE // NSLOT - 1, s, NSLOT - s)
                over = dve.value_load(flagi[0:1, 0:1], min_val=0, max_val=1)
                with dve.If(over > 0):
                    with dve.Fori(0, OVER) as n_:
                        n = l * OVER + n_
                        dve.wait_ge(S["ov_xt"], n + 1)
                        cp(xgT[0].rearrange("p k t -> p (k t)"), bank(0, 2), "ov_xs")
                        dve.wait_ge(S["ov_sl"], n + 1)
                        tt(hgu[0], sg[0], ps[:, 2, ED:2 * ED], ALU.mult, "ov_mu")
                        dve.wait_ge(S["ov_ht"], n + 1)
                        cp(hTe[0].rearrange("p k t -> p (k t)"), ps[:, 4, 0:2 * P], "ov_hs")
                        dve.wait_ge(S["ov_dn"], n + 1)
                        ts(oe[0], bank(5, 2), idxS[0][:, 1:2], None, ALU.mult, name="ov_oe")
                with dve.Else():
                    for name in ("ov_xs", "ov_mu", "ov_hs", "ov_oe"):
                        dve.sem_inc(S[name], OVER)
                wait("gf_ps", 1, l)
                for c in range(NT):
                    wait(f"acc_loaded{c % 2}", 16 * (c // 2 + 1), l)
                    tt(X[:, c % 2, :], X[:, c % 2, :], bank(2 * (c // 2), 2), ALU.mult)
                    tt(h[:, c, :], h[:, c, :], X[:, c % 2, :], ALU.add, "acc_added")
                dve.drain().then_inc(S["h_ready"], 1)
            for c in range(2):
                V.tensor_tensor_reduce(out=X[:, c, :], in0=h[:, 2 + c, :], in1=h[:, 2 + c, :], scale=1.0, scalar=0.0,
                                       op0=ALU.mult, op1=ALU.add, accum_out=st[:, c:c + 1])
                dve.drain()
            dve.drain().then_inc(S["out_sq"], 1)
            dve.wait_ge(S["out_ln"], 1)
            dve.wait_ge(S["out_loaded"], 16)
            for c in range(2):
                ts(X[:, c, :], h[:, 2 + c, :], st[:, 8 + c:9 + c], None, ALU.mult)
                tt(X[:, c, :], X[:, c, :], grow[:, 0, :], ALU.mult, "out_ready")


        @block.tensor
        def _(pe):
            MM = nc.tensor.matmul

            def wait(name, n, l):
                pe.wait_ge(S[name], l * PER[name] + n)

            def mm(out_, lhsT, rhs, start=True, stop=True):
                return MM(out_, lhsT, rhs, start=start, stop=stop)

            def turn(out_, in_):
                k = in_.shape[0]
                return nc.tensor.transpose(out_, in_, ident[0:k, 0:k])

            def column(ap):
                return ap.to_broadcast([P, P])

            def ring_wait(m, l):
                pe.wait_ge(S[f"ring_full{m % 2}"], l * (16 * RING // 2) + 16 * (m // 2 + 1))

            pe.wait_ge(S["const_ready"], 1)
            pe.wait_ge(S["head_loaded"], 16 * 5)
            turn(ps[:, 0, 0:2 * KT], stage[0:2 * KT, 0, :])
            turn(ps[:, 3, 0:4], stage[0:4, 1, :]).then_inc(S["cond_ps"], 1)

            def norm_turn(q, l):
                for c in range(NT):
                    wait("xn", q * NT + c + 1, l)
                    if c >= 2:
                        wait("feat_d", q * NT + c - 1, l)
                        wait("feat_a", q * NT + c - 1, l)
                    for k in range(KT):
                        ins = turn(bank(4 + 2 * (c % 2), 2)[:, tk(k)], X[:, c % 2, tk(k)])
                    ins.then_inc(S["xT_ps"], 1)

            with pe.Fori(0, DEPTH) as l:
                wait("h_ready", 1, l)
                wait("prm_loaded", 16 * PRM_DMAS, l)
                pe.sem_inc(S["past"], 1)
                turn(ps[:, 1, 0:64], stage[0:64, 0, :])
                turn(ps[:, 1, 64:N_PRM], stage[0:N_PRM - 64, 1, :]).then_inc(S["prm_ps"], 1)
                with pe.Fori(0, N_MOD // 2) as i:
                    for s in range(2):
                        pe.wait_ge(S[f"ring_full{s}"], l * (16 * RING // 2) + i * 16 + 16)
                        for half in range(2):
                            for k in range(KT):
                                ins = mm(ps[:, 2, bass.ds(i * 8 + (s * 4 + half * 2), 2)], ring[:, s, k, tk(half)], condT[:, :, k],
                                         k == 0, k == KT - 1)
                        ins.then_inc(S["ring_used"], 1)
                pe.drain().then_inc(S["mod_ps"], 1)
                wait("mod_sb", 1, l)
                norm_turn(0, l)
                wait("feat_d", NT, l)
                wait("feat_a", NT, l)
                wait("small_loaded", 32, l)
                for c in range(NT):
                    for k in range(KT):
                        ins = mm(ps[:, 3, 32 * c:32 * c + 32], featT[:, k, tk(c)], wsm[:, k, :], k == 0, k == KT - 1)
                ins.then_inc(S["sm_ps"], 1)
                for n, (kind, _, _) in enumerate(IN_BLOCKS):
                    m = N_MOD + n
                    b0 = UB[n % 3]
                    ring_wait(m, l)
                    if n >= 3:
                        wait("u_dve", n - 2, l) if n - 3 < N_CONV else wait("u_act", n - 2 - N_CONV, l)
                    if kind in ("conv", "hq", "hf"):
                        for half in range(2):
                            for k in range(KT):
                                ins = mm(ps[:, b0 + half, :], ring[:, m % 2, k, tk(half)], featT[:, k, :], k == 0, k == KT - 1)
                    else:
                        for c in range(NT):
                            for k in range(KT):
                                ins = mm(bank(b0, 2)[:, c * BW:(c + 1) * BW], featT[:, k, tk(c)], ring[:, m % 2, k, :], k == 0, k == KT - 1)
                    ins.then_inc(S["u_ps"], 1)
                    pe.drain().then_inc(S["ring_used"], 1)
                wait("sp_done", 1, l)
                for d in range(2):
                    mm(ps[:, 2, 48 * d:48 * d + 48], tri[:, d, :], da[:, :, d, :])
                mm(ps[:, 2, 96:192], ones[:, :], da[:, :, :, :].rearrange("p c d h -> p (c d h)")).then_inc(S["cum_ps"], 1)
                wait("u_act", N_IN - N_CONV, l)
                for t in range(4):
                    wait("l2_sq", t + 1, l)
                    if t >= 2:
                        wait("l2_act", t - 1, l)
                    mm(ps[:, t % 2, :], bd[:, :], sqw[:, t % 2, :]).then_inc(S["l2_ps"], 1)
                wait("l2_done", 4, l)
                wait("cum_dve", 1, l)
                wait("silu_out", CT, l)
                for c in range(NT):
                    b0 = 4 * (c % 2)
                    if c >= 2:
                        wait("tok_d", c - 1, l)
                        wait("tok_a", c - 1, l)
                    for t in range(4):
                        turn(ps[:, b0, tk(t)], cv[:, t, tk(c)])
                    for t in range(2):
                        turn(ps[:, b0 + 1, tk(t)], cv[:, 4 + t, tk(c)])
                        turn(ps[:, b0 + 1, HW + t * P:HW + (t + 1) * P], cv[:, 10 + t, tk(c)])
                        ins = turn(ps[:, b0 + 2, tk(t)], cv[:, 12 + t, tk(c)])
                    ins.then_inc(S["tok_ps"], 1)
                wait("small_done", 1, l)
                wait("tok_d", NT, l)
                wait("tok_a", NT, l)
                wait("s_init", 1, l)
                for u, (i, d, c) in enumerate(UNITS):
                    last_step = i == NT - 1
                    if u:
                        wait("gdn_done", u, l)
                        wait("ssd_sb", u, l)
                    for g in range(NG):
                        mm(ps[:, 0, tk(g)], cv[:, 4 + g, tk(c)], cv[:, 6 + g, tk(c)])
                    for par in range(2):
                        rows = slice(par * HD, (par + 1) * HD)
                        for a in range(2):
                            mm(ps[:, 1 + par, tk(a)], cv[rows, 10 + a, tk(c)], cv[rows, 10 + a, tk(c)])
                            mm(ps[:, 1 + par, tk(2 + a)], cv[rows, 10 + a, tk(c)], cv[rows, 8 + a, tk(c)])
                    for j in range(NDEC):
                        mm(ps[:, 3 + j // 4, tk(j % 4)], column(da[:, c, d, j:j + 1]), tri[:, d, :])
                    for j in range(HH):
                        ins = mm(ps[:, 6, tk(j)], column(beta[:, c, d, j:j + 1]), ident[:, :])
                    ins.then_inc(S["pre_ps"], 1)
                    wait("at_ready", u + 1, l)
                    for j in range(LEVELS):
                        wait("nt_ready", u * LEVELS + j + 1, l)
                        wait("t_init", u + 1, l) if j == 0 else wait("t_ready", u * LEVELS + j, l)
                        for q in range(HH):
                            ins = mm(ps[:, 1, tk(q)], NTm[:, q, :], T[:, q, :])
                        ins.then_inc(S["p_ps"], 1)
                        if j < 4:
                            if j == 0:
                                wait("ql_ready", u + 1, l)
                            else:
                                wait("h_cp", u * 4 + j, l)
                            for r in range(2):
                                lv = 2 * j + r
                                for par in range(2):
                                    rows = slice(par * HD, (par + 1) * HD)
                                    for a in range(2):
                                        k_, q_ = (kL[rows, lv, tk(a)], e7[rows, lv, tk(a)]) if lv < LEVELS else \
                                            (hk[rows, d, a, tk(c)], hq[rows, a, tk(c)])
                                        ins = mm(ps[:, 4 + par, tk(2 * r + a)], k_, q_)
                            ins.then_inc(S["h_ps"], 1)
                        if j == 4:
                            wait("h_cp", u * 4 + 4, l)
                            for a in range(2):
                                ins = turn(ps[:, 5, tk(a)], kend[:, tk(a)])
                            ins.then_inc(S["ke_ps"], 1)
                        wait("p_sb", u * LEVELS + j + 1, l)
                        if j < LEVELS - 1:
                            for q in range(HH):
                                mm(ps[:, 2, tk(q)], TT[:, q, :], Pm[:, q, :])
                        for q in range(HH):
                            ins = mm(ps[:, 3, tk(q)], Pm[:, q, :], TT[:, q, :])
                        ins.then_inc(S["q_ps"], 1)
                        if j == 2:
                            wait("att_ready", u + 1, l)
                            for q in range(HS):
                                mm(ps[:, 7, q * HD:(q + 1) * HD], E[:, q, :], cv[:, q // 2, c * P + (q % 2) * HD:c * P + (q % 2 + 1) * HD])
                            for g in range(NG):
                                ins = mm(ps[:, 6, g * HW:(g + 1) * HW], cv[:, 6 + g, tk(c)], Ss[:, d, g, :])
                                if not last_step:
                                    ins = mm(ps[:, 0, g * HW:(g + 1) * HW], Btok[:, c, tk(g)], xw[:, g * HW:(g + 1) * HW])
                            ins.then_inc(S["ssd_ps"], 1)
                    for a in range(2):
                        mm(ps[:, 4, tk(a)], eb[:, tk(a)], Sh[:, d, a, :], True, False)
                        for par in range(2):
                            q = 2 * a + par
                            mm(ps[:, 4, q * HD:(q + 1) * HD], attH[:, q, :], val[:, c, q * HD:(q + 1) * HD], False, par == 1)
                    wait("ke_sb", u + 1, l)
                    for a in range(2):
                        ins = mm(ps[:, 5, tk(2 + a)], kendT[:, tk(a)], val[:, c, tk(a)])
                    ins.then_inc(S["ho_ps"], 1)
                    wait("t_ready", (u + 1) * LEVELS, l)
                    for a in range(2):
                        ins = mm(ps[:, 1, tk(a)], cv[:, 10 + a, tk(c)], Sg[:, d, a, :])
                    ins.then_inc(S["gks_ps"], 1)
                    for a in range(2):
                        mm(ps[:, 2, tk(a)], cv[:, 8 + a, tk(c)], Sg[:, d, a, :])
                    wait("r_ready", u + 1, l)
                    for q in range(HH):
                        ins = mm(ps[:, 1, HW + q * HD:HW + (q + 1) * HD], TT[:, q, :], rr[:, q * HD:(q + 1) * HD])
                    ins.then_inc(S["vn_ps"], 1)
                    wait("vn_sb", u + 1, l)
                    wait("kw_ready", u + 1, l)
                    for q in range(HH):
                        mm(ps[:, 2, HW + q * HD:HW + (q + 1) * HD], E[:, HS + q, :], vn[:, q * HD:(q + 1) * HD])
                    for a in range(2):
                        ins = mm(ps[:, 3, tk(a)], kw[:, tk(a)], vn[:, tk(a)])
                    ins.then_inc(S["go_ps"], 1)
                wait("gdn_done", U, l)
                wait("ssd_sb", U, l)
                def gate_rows(first, name, b0):
                    for j in range(2):
                        for k in range(KT):
                            ins = mm(bank(b0 + 2 * j, 2)[:, tk(k)], column(mod[:, first + k, j:j + 1]), ident[:, :])
                        if name:
                            ins.then_inc(S[name], 1)
                    return ins

                gate_rows(16, "grow_ps", 0)
                for c in range(NT):
                    wait("y_ready", c + 1, l)
                    if c >= 2:
                        wait("yT_sb", c - 1, l)
                    for k in range(KT):
                        ins = turn(bank(4 + 2 * (c % 2), 2)[:, tk(k)], yraw[:, c, tk(k)])
                    ins.then_inc(S["yT_ps"], 1)
                wait("yT_sb", NT, l)
                for n in range(N_OUT):
                    m = N_MOD + N_IN + n
                    ring_wait(m, l)
                    if n >= 2:
                        wait("wo_sb", n - 1, l)
                    for c in range(NT):
                        for k in range(KT):
                            ins = mm(bank(4 + 2 * (n % 2), 2)[:, c * BW:(c + 1) * BW], yT[:, k, tk(c)], ring[:, m % 2, k, :], k == 0, k == KT - 1)
                    ins.then_inc(S["wo_ps"], 1)
                    pe.drain().then_inc(S["ring_used"], 1)
                norm_turn(1, l)
                wait("feat_d", 2 * NT, l)
                wait("feat_a", 2 * NT, l)
                for c in range(NT):
                    if c >= 2:
                        wait("ftok_sb", c - 1, l)
                    for k in range(KT):
                        ins = turn(bank(4 + 2 * (c % 2), 2)[:, tk(k)], featT[:, k, tk(c)])
                    ins.then_inc(S["ftok_ps"], 1)
                wait("rw_loaded", 16, l)
                wait("grow_sb", 2, l)
                for c in range(NT):
                    for k in range(KT):
                        ins = mm(ps[:, 0, c * NE:(c + 1) * NE], featT[:, k, tk(c)], rw[:, k, :], k == 0, k == KT - 1)
                ins.then_inc(S["lg_ps"], 1)
                wait("ftok_sb", NT, l)
                wait("lg_exp", 1, l)
                for n in range(2):
                    m = N_MOD + N_IN + N_OUT + n
                    ring_wait(m, l)
                    for half in range(2):
                        for k in range(KT):
                            ins = mm(ps[:, 2 * n + half, :], ring[:, m % 2, k, tk(half)], featT[:, k, :], k == 0, k == KT - 1)
                    ins.then_inc(S["sh_ps"], 1)
                    pe.drain().then_inc(S["ring_used"], 1)
                wait("mask_ready", 1, l)
                for c in range(NT + 1):
                    for c2 in range(min(c + 1, NT)):
                        w = triS if c2 == c else ones
                        ins = mm(ps[:, 7, c * NE:(c + 1) * NE], w[:, :], mask[:, c2, :], c2 == 0, c2 == min(c, NT - 1))
                ins.then_inc(S["pos_ps"], 1)
                m = N_MOD + N_IN + N_OUT + 2
                wait("sh_mul", 1, l)
                wait("flag_ready", 1, l)
                ring_wait(m, l)
                down = ring[:, m % 2, :, :].rearrange("p (a b) n -> p a (b n)", a=2)
                for c in range(NT):
                    if c:
                        wait("shd_sb", c - 1, l) if c > 1 else None
                    for half in range(2):
                        for k in range(2):
                            ins = mm(ps[:, 4 + 2 * (c % 2) + half, :], hsh[:, k, tk(c)], down[:, k, half * 512:(half + 1) * 512], k == 0, k == 1)
                    ins.then_inc(S["shd_ps"], 1)
                pe.drain().then_inc(S["ring_used"], 1)
                wait("shd_sb", NT, l)

                def rows_T(s, n):
                    b = s % 2
                    pe.wait_ge(S[f"gathered{s}"], n)
                    for k in range(KT):
                        ins = turn(bank(0, 2)[:, tk(k)], xg[b][:, tk(k)])
                    ins.then_inc(S["xt_ps"], 1)

                def gate_up(e, s, ws):
                    b = s % 2
                    pe.wait_ge(S["xt_sb"], e * 2 + 2)
                    pe.wait_ge(S[f"w{s}"], ws)
                    for k in range(KT):
                        ins = mm(ps[:, 2 + b, :], xgT[b][:, k, :], wgu[s][:, k, :], k == 0, k == KT - 1)
                    ins.then_inc(S["gu_ps"], 1)

                def pe_step(i, s, more):
                    e = l * NE + i * NSLOT + s
                    weights = l * PER["w0"] + i * 48 + 48
                    if more > 1:
                        gate_up(e + 1, (s + 1) % NSLOT, weights if s < NSLOT - 1 else weights + 48)
                    pe.wait_ge(S["gu_mul"], e + 1)
                    for k in range(2):
                        ins = turn(ps[:, 4, tk(k)], hgu[s % 2][:, tk(k)])
                    ins.then_inc(S["hT_ps"], 1)
                    if more > 2:
                        rows_T((s + 2) % NSLOT, l * (4 * NE) + i * 16 + (16 if s < 2 else 32))
                    pe.wait_ge(S["hT_sb"], e + 1)
                    if not (isinstance(i, int) and i == 0 and s == 0):
                        pe.wait_ge(S["oe_ready"], e * 2)
                    for half in range(2):
                        for k in range(2):
                            ins = mm(ps[:, 5 + half, :], hTe[s % 2][:, k, :], wdn[s][:, k, half * 512:(half + 1) * 512], k == 0, k == 1)
                    ins.then_inc(S["dn_ps"], 1)

                wait("xg_init", 1, l)
                rows_T(0, l * (4 * NE) + 16)
                gate_up(l * NE, 0, l * PER["w0"] + 48)
                rows_T(1, l * (4 * NE) + 16)
                for s in range(NSLOT):
                    pe_step(0, s, 5)
                with pe.Fori(1, NE // NSLOT - 1) as i:
                    for s in range(NSLOT):
                        pe_step(i, s, 5)
                for s in range(NSLOT):
                    pe_step(NE // NSLOT - 1, s, NSLOT - s)
                wait("oe_ready", 2 * NE, l)
                pe.sem_inc(S["past"], 1)
                pe.wait_ge(S["flag_ready"], l + 1)
                pe.sem_inc(S["past"], 1)
                over = pe.value_load(flagi[0:1, 0:1], min_val=0, max_val=1)
                with pe.If(over > 0):
                    with pe.Fori(0, OVER) as n_:
                        n = l * OVER + n_
                        pe.wait_ge(S["ov_g"], n + 1)
                        for k in range(KT):
                            ins = turn(bank(0, 2)[:, tk(k)], xg[0][:, tk(k)])
                        ins.then_inc(S["ov_xt"], 1)
                        pe.wait_ge(S["ov_xs"], n + 1)
                        pe.wait_ge(S["ov_w"], n * 48 + 48)
                        for k in range(KT):
                            ins = mm(ps[:, 2, :], xgT[0][:, k, :], wgu[0][:, k, :], k == 0, k == KT - 1)
                        ins.then_inc(S["ov_gu"], 1)
                        pe.wait_ge(S["ov_mu"], n + 1)
                        for k in range(2):
                            ins = turn(ps[:, 4, tk(k)], hgu[0][:, tk(k)])
                        ins.then_inc(S["ov_ht"], 1)
                        pe.wait_ge(S["ov_hs"], n + 1)
                        for half in range(2):
                            for k in range(2):
                                ins = mm(ps[:, 5 + half, :], hTe[0][:, k, :], wdn[0][:, k, half * 512:(half + 1) * 512], k == 0, k == 1)
                        ins.then_inc(S["ov_dn"], 1)
                with pe.Else():
                    for name in ("ov_xt", "ov_gu", "ov_ht", "ov_dn"):
                        pe.sem_inc(S[name], OVER)
                pe.wait_ge(S["ov_oe"], l * OVER + OVER)
                gate_rows(40, None, 0).then_inc(S["gf_ps"], 1)


_INS = ["x", "c", "ctx", "c_ctx", "w_mod", "b_mod", "norm_mix", "w_in", "ssd_conv_w", "ssd_conv_b", "ssd_dt_bias",
        "ssd_a_log", "ssd_d", "ssd_norm", "hgrn_lb", "hgrn_norm", "gdn_conv_w", "gdn_dt_bias", "gdn_a_log", "gdn_norm",
        "w_out", "norm_ffn", "router_w", "router_bias", "exp_gate", "exp_up", "exp_down", "sh_gate", "sh_up", "sh_down",
        "norm_final"]


def kernel(**inputs):
    import concourse.bacc as bacc
    from concourse.bass_utils import run_bass_kernel_spmd

    nc = bacc.Bacc("TRN2", target_bir_lowering=False, num_devices=1)
    arrays, A = {}, {}
    for name in _INS:
        a = np.ascontiguousarray(inputs[name])
        arrays[f"in_{name}"] = a
        A[name] = nc.dram_tensor(f"in_{name}", a.shape, mybir.dt.from_np(a.dtype), kind="ExternalInput").ap()
    out = nc.dram_tensor("out", (1, SEQ, DM), F32, kind="ExternalOutput").ap()
    scratch = (nc.dram_tensor("ffn_rows", (TOK, DM), F32, kind="Internal").ap(),
               nc.dram_tensor("ffn_sum", (TOK, DM), F32, kind="Internal").ap(),
               nc.dram_tensor("slots", (CAP, NE, 2), F32, kind="Internal").ap())
    build(nc, A, out, scratch)
    r = run_bass_kernel_spmd(nc, [arrays], core_ids=[0])
    return r.results[0]["out"]
```

```python
import math
from contextlib import ExitStack

import numpy as np

import concourse.bass as bass
from concourse import mybir

F32 = mybir.dt.float32
I32 = mybir.dt.int32
U32 = mybir.dt.uint32
ALU = mybir.AluOpType
ACT = mybir.ActivationFunctionType
AX = mybir.AxisListType

P = 128
DEPTH = 2
DM = 1024
KT = DM // P
CTX = 256
SEQ = 256
TOK = CTX + SEQ
NT = TOK // P
GRID_W = 64
ROWS = SEQ // GRID_W
TAPS = 5
HALF = TAPS // 2
EPS = 1e-6

HS, NG, NSTATE = 8, 2, 128
HH = 4
HD = 64
SW = HS * HD
HW = HH * HD
NDEC = HS + HH
SSD_IN = SW + SW + 2 * NG * NSTATE + 2 * HS
HGRN_IN = 5 * HW
GDN_IN = 3 * HW + 4 * HH + HW
COL_HGRN = SSD_IN
COL_GDN = SSD_IN + HGRN_IN
CT = 14
LEVELS = 7
NE, TOPK, ED = 64, 8, 256
ROUTED_SCALE = 2.5
CAP = TOK
NBLK = CAP // P
NSLOT = 4
BW = 256
RSIZE = 33700
NEG = -1e30
SKIP = 1 << 20

CPAD = CTX + 2 * HALF
RPAD = GRID_W + 2 * HALF
LINE = CPAD + ROWS * RPAD
CONV = LINE - 2 * HALF

IN_BLOCKS = (
    [("conv", SW + BW * i, i) for i in range(4)]
    + [("conv", COL_GDN + BW * i, 4 + i) for i in range(3)]
    + [("hq", COL_HGRN, 0), ("gate", 0, 0), ("gate", BW, 1),
       ("gate", COL_HGRN + 4 * HW, 2), ("gate", COL_GDN + 3 * HW + 4 * HH, 3)]
    + [("val", COL_HGRN + 3 * HW, 0), ("hf", COL_HGRN + HW, 0), ("hf", COL_HGRN + 2 * HW, 1)]
)
N_CONV = 7
N_IN = len(IN_BLOCKS)
MW = 512
N_MOD = 6 * DM // MW
N_OUT = DM // BW
RING = N_IN + N_OUT + 3

R_BMOD, R_NMIX, R_NFFN = 0, 48, 56
R_CWS, R_CBS, R_CWG = 64, 104, 112
N_PRM = 142

UB = (0, 4, 6)
PRM_DMAS = 12
NROW_DMAS = 3
OVER = (NBLK - 1) * NE

ORDER = ((0, 1, 2, 3), (1, 0, 3, 2))
UNITS = [(i, d, ORDER[d][i]) for i in range(NT) for d in range(2)]
SEEN = {}
for _n, (_i, _d, _c) in enumerate(UNITS):
    SEEN.setdefault(_c, _n)


def line_rows(ap):
    return ap[:, CPAD:CPAD + (ROWS - 1) * RPAD + RPAD].rearrange("p (r x) -> p r x", r=ROWS)[:, :, 0:GRID_W]


def build(nc, A, out, scratch):
    f_dram, acc_dram, acc_odd, tab_dram = scratch
    with ExitStack() as ctx:
        def sb(name, shape, dt=F32):
            return ctx.enter_context(nc.sbuf_tensor(name, shape, dt))

        def sem(name):
            return ctx.enter_context(nc.semaphore(name))

        h = sb("h", [P, NT, DM])
        featT = sb("featT", [P, KT, TOK])
        yraw = featT[:, :, :].rearrange("p k t -> p (k t)").rearrange("p (c f) -> p c f", c=NT)
        X = sb("X", [P, 2, DM])
        ring = sb("ring", [P, 2, KT, BW])
        ident = sb("ident", [P, P])
        tri = sb("tri", [P, 2, P])
        negm = sb("negm", [P, 2, P])
        triS = sb("triS", [P, P])
        ones = sb("ones", [P, P])
        bd = sb("bd", [P, P])
        lev = sb("lev", [P, 2, LEVELS, P])
        iota_e = sb("iota_e", [P, NE])
        tokid = sb("tokid", [P, NT], I32)
        cst = sb("cst", [P, 4])
        condT = sb("condT", [P, 2, KT])
        stage = sb("stage", [P, 2, P])
        prm = sb("prm", [P, N_PRM])
        low = sb("low", [P, DEPTH, 2])
        lowv = sb("lowv", [P, 3, 2])
        mod = sb("mod", [P, 48, 2])
        amul = sb("amul", [P, 2, KT, 2])
        nrow = X[:, 1, :]
        dtb = sb("dtb", [P, 2, NDEC])
        alog = sb("alog", [P, 2, NDEC])
        nega = sb("nega", [P, 2, NDEC])
        dsk = sb("dsk", [P, HS])
        rbias = sb("rbias", [P, NE])
        wsm = sb("wsm", [P, KT, 32])
        rw = sb("rw", [P, KT, NE])
        st = sb("st", [P, 16])
        live = sb("live", [P, DEPTH, NT])
        lcur = sb("lcur", [P, NT])
        hdec = sb("hdec", [P, 2])
        ssq = sb("ssq", [P, NT, 10])
        R = sb("R", [P, RSIZE])
        at = [0]

        def cut(*shape):
            n = math.prod(shape)
            v = R[:, at[0]:at[0] + n]
            at[0] += n
            if len(shape) == 2:
                v = v.rearrange("p (a b) -> p a b", a=shape[0])
            if len(shape) == 3:
                v = v.rearrange("p (a b c) -> p a b c", a=shape[0], b=shape[1])
            return v

        cv = cut(CT, TOK)
        hq = cut(2, TOK)
        logf = cut(2, 2, TOK)
        hk = cut(2, 2, TOK)
        gates = cut(NT, DM)
        val = cut(NT, HW)
        Btok = cut(NT, NG * NSTATE)
        Ktok = cut(NT, HW)
        wk = at[0]
        line = cut(2, LINE)
        cvo = cut(2, LINE)
        hwt = cut(2 * 2, TOK)
        hwx = cut(2 * 2, TOK)
        lnw = cut(TOK)
        lnx = cut(TOK)
        sqw = cut(2, TOK)
        sm = cut(NT, 32)
        spw = cut(4, NT * 2 * NDEC)
        at[0] = wk
        E = cut(NDEC, P)
        AT = cut(HH, P)
        NTm = cut(HH, P)
        T = cut(HH, P)
        TT = cut(HH, P)
        Pm = cut(HH, P)
        e7 = cut(LEVELS, 2 * P)
        kL = cut(LEVELS, 2 * P)
        bh = cut(2 * P)
        eb = cut(2 * P)
        e1 = cut(2 * P)
        kend = cut(2 * P)
        kendT = cut(2 * P)
        attH = cut(HH, P)
        xw = cut(SW)
        rr = cut(HW)
        vn = cut(HW)
        kw = cut(HW)
        tmp = cut(SW)
        Ss = cut(2, NG, SW // NG)
        Sh = cut(2, 2, P)
        Sg = cut(2, 2, P)
        wdt = cut(NT, 2, NDEC)
        dt_ = cut(NT, 2, NDEC)
        da = cut(NT, 2, NDEC)
        acs = cut(NT, 2, NDEC)
        eacs = cut(NT, 2, NDEC)
        wend = cut(NT, 2, NDEC)
        etot = cut(NT, 2, NDEC)
        beta = cut(NT, 2, HH)
        dcol = cut(NT * 2, 2)
        assert at[0] <= RSIZE
        levt = e7[:, 0:1, :].bitcast(I32).rearrange("p a (b t) -> p (a b) t", b=2)
        at[0] = 0
        yT = cut(KT, TOK)
        sqo = cut(2, DM)
        grow = cut(2, DM)
        at[0] = 0
        wgu, wdn = [], []
        for _ in range(NSLOT):
            wgu.append(cut(KT, 2 * ED))
            wdn.append(cut(2, DM))
        ex = at[0]
        xg = [yraw[:, s, :] for s in range(NSLOT)]
        xgT = [cut(KT, P) for _ in range(2)]
        oe = [cut(DM) for _ in range(2)]
        sg = [cut(2, P) for _ in range(2)]
        hTe = [cut(2, P) for _ in range(2)]
        tabA = cut(NE, 2)
        assert at[0] <= RSIZE
        at[0] = ex
        scor = cut(NT, NE)
        sel = cut(NT, NE)
        mask = cut(NT, NE)
        pos = cut(NT, NE)
        hot2 = cut(TOPK, NE)
        hots = cut(NT, TOPK * NE)
        v8 = cut(NT, TOPK)
        i8 = cut(NT, TOPK).bitcast(U32)
        if8 = cut(NT, TOPK)
        s8 = cut(NT, TOPK)
        p8 = cut(NT, TOPK)
        dst8 = cut(NT, TOPK)
        dsti = cut(NT * TOPK, 1).bitcast(I32)
        pay = cut(NT * TOPK, 2)
        gsum = cut(NT)
        blank = cut(CAP * NE // P, 2)
        sgT = cut(2, TOK)
        hsh = cut(2, TOK)
        idxG = [sb(f"idx_in{i}", [P, 2]) for i in range(NSLOT)]
        idxS = [sb(f"idx_out{i}", [P, 2]) for i in range(NSLOT)]
        flag = sb("flag", [1, 4])
        flagi = sb("flagi", [1, 1], I32)
        moref = sb("moref", [1, NBLK, NE])
        more = sb("more", [1, NBLK * NE], I32)
        zero = sb("zero", [P, P])

        ps = ctx.enter_context(nc.psum_tensor("ps", [P, 8, 512], F32))


        PER = {}

        def signal(name, per_layer=0):
            PER[name] = per_layer
            S[name] = sem(name)

        S = {}
        for name in ("const_pool", "const_ready", "head_loaded", "cond_ps", "cond_sb", "out_loaded",
                     "low_a", "low_b",
                     "past", "ov_dma", "out_ready", "out_stored"):
            signal(name)
        U = len(UNITS)
        for name, n in (
            ("h_ready", 1), ("prm_loaded", 16 * PRM_DMAS), ("prm_ps", 1), ("small_loaded", 32), ("rw_loaded", 16),
            ("ring_full0", 16 * RING // 2), ("ring_full1", 16 * RING // 2), ("ring_used", RING),
            ("mod_used", N_MOD), ("mod_row", N_MOD), ("mod_ps", 1), ("mod_sb", 1),
            ("sumsq", 2), ("rstd", 2), ("xn", 2 * NT), ("xT_ps", 2 * NT), ("feat_d", 2 * NT), ("feat_a", 2 * NT),
            ("u_ps", N_IN), ("u_dve", N_CONV), ("u_act", N_IN - N_CONV), ("conv_out", CT), ("silu_out", CT),
            ("sm_ps", 1), ("sp_x", 1), ("sp_exp", 1), ("sp_done", 1), ("cum_ps", 1), ("cum_dve", 1),
            ("cum_act", 1), ("small_done", 1),
            ("l2_sq", 4), ("l2_ps", 4), ("l2_act", 4), ("l2_done", 4),
            ("low_c", 1), ("lowl", 1), ("hg_b", 1), ("hg_c", 1), ("hg_d", 1), ("hg_e", 1), ("hg_f", 1),
            ("tok_ps", NT), ("tok_d", NT), ("tok_a", NT), ("s_init", 1),
            ("pre_ps", U), ("dm_ready", U), ("e_ready", U), ("b_ready", U), ("hexp", U), ("kl_ready", U),
            ("ql_ready", U), ("a_init", U), ("t_init", U), ("kw_ready", U), ("at_ready", U), ("att_ready", U),
            ("ssd_ps", U), ("ssd_sb", U), ("nt_ready", U * LEVELS), ("p_ps", U * LEVELS), ("p_sb", U * LEVELS),
            ("q_ps", U * LEVELS), ("t_ready", U * LEVELS), ("h_ps", U * 4), ("h_cp", U * 4),
            ("ke_ps", U), ("ke_sb", U), ("ho_ps", U), ("hgrn_done", U),
            ("gks_ps", U), ("r_ready", U), ("vn_ps", U), ("vn_sb", U), ("go_ps", U), ("gdn_done", U),
            ("nrow_loaded", 16 * NROW_DMAS), ("y_sq", 1), ("y_rstd", 1), ("y_ready", NT), ("yT_ps", NT), ("yT_sb", NT),
            ("grow_ps", 2), ("grow_sb", 2), ("wo_ps", N_OUT), ("wo_sb", N_OUT),
            ("ftok_ps", NT), ("ftok_sb", NT), ("x_stored0", 64), ("x_stored1", 64), ("lg_ps", 1), ("lg_exp", 1),
            ("mask_ready", 1), ("pos_ps", 1), ("blank_ready", 1), ("blank_dram", 16), ("pay_ready", 1),
            ("tab_dram", 16 * NT * TOPK), ("tab_loaded", 16), ("flag_ready", 1),
            ("sh_ps", 2), ("sh_silu", 1), ("sh_mul", 1), ("shd_ps", NT), ("shd_sb", NT), ("acc_zeroed", 16 * NT),
            ("w0", 32 * 24), ("w1", 32 * 24), ("w2", 32 * 24), ("w3", 32 * 24), 
            ("gathered0", 4 * NE), ("gathered1", 4 * NE), ("gathered2", 4 * NE), ("gathered3", 4 * NE), ("xt_ps", NE), ("xt_sb", 2 * NE), ("gu_ps", NE), ("gu_silu", NE), ("gu_mul", NE),
            ("dn_ps", NE), ("oe_act", NE), ("oe_dve", NE), ("idx_in", NE), ("idx_out", NE), ("scattered0", 8 * NE), ("scattered1", 8 * NE), ("xg_init", 1),
            ("acc_loaded0", 32), ("acc_loaded1", 32), ("odd_loaded", 16), ("acc_added", NT), ("gf_ps", 1),
            ("ov_w", 48 * OVER), ("ov_tab", 16 * OVER), ("ov_g", OVER), ("ov_xt", OVER), ("ov_xs", OVER),
            ("ov_gu", OVER), ("ov_sl", OVER), ("ov_mu", OVER), ("ov_dn", OVER),
            ("ov_oe", OVER), ("ov_sc", OVER),
        ):
            signal(name, n)
        for s in range(NSLOT):
            PER[f"w{s}"] = 16 * N_MOD // NSLOT + 48 * NE // NSLOT

        block = ctx.enter_context(nc.Block())

        def tk(c):
            return slice(c * P, (c + 1) * P)

        def bank(b, n=1):
            return ps[:, b:b + n, :].rearrange("p b f -> p (b f)")

        def bc(ap, *shape):
            return ap.to_broadcast([P, *shape])

        @block.sync
        def _(sp):
            def past():
                sp.sem_inc(S["past"], 1)

            def wait(name, n, l):
                sp.wait_ge(S[name], l * PER[name] + n)
                past()

            sp.dma_start(h[:, 0:2, :], A["ctx"][0].rearrange("(c p) f -> p c f", p=P)).then_inc(S["head_loaded"], 16)
            sp.dma_start(h[:, 2:4, :], A["x"][0].rearrange("(c p) f -> p c f", p=P)).then_inc(S["head_loaded"], 16)
            sp.dma_start(stage[0:KT, 0, :], A["c_ctx"].rearrange("(k p) -> k p", p=P)).then_inc(S["head_loaded"], 16)
            sp.dma_start(stage[KT:2 * KT, 0, :], A["c"].rearrange("o (k p) -> (o k) p", p=P)).then_inc(S["head_loaded"], 16)
            sp.dma_start(stage[0:4, 1, :], A["hgrn_lb"].rearrange("l (t p) -> (l t) p", p=P)).then_inc(S["head_loaded"], 16)
            with sp.Fori(0, DEPTH) as l:
                L1 = bass.ds(l, 1)
                wmod = A["w_mod"][L1].rearrange("o (k p) n -> p (o k) n", p=P)
                for s in range(NSLOT):
                    sp.dma_start(wgu[s][:, :, :], wmod[:, :, s * MW:(s + 1) * MW]).then_inc(S[f"w{s}"], 16)
                wait("h_ready", 1, l)
                def param(dst, src):
                    sp.dma_start(dst, src).then_inc(S["prm_loaded"], 16)
                param(stage[R_BMOD:R_BMOD + 48, 0, :], A["b_mod"][L1].rearrange("o (r p) -> (o r) p", p=P))
                param(stage[R_NMIX:R_NMIX + 8, 0, :], A["norm_mix"][L1].rearrange("o (r p) -> (o r) p", p=P))
                param(stage[R_NFFN:R_NFFN + 8, 0, :], A["norm_ffn"][L1].rearrange("o (r p) -> (o r) p", p=P))
                param(stage[0:40, 1, :], A["ssd_conv_w"][L1].rearrange("o j (t p) -> (o j t) p", p=P))
                param(stage[40:48, 1, :], A["ssd_conv_b"][L1].rearrange("o (t p) -> (o t) p", p=P))
                param(stage[48:78, 1, :], A["gdn_conv_w"][L1].rearrange("o j (t p) -> (o j t) p", p=P))
                param(dtb[:, :, 0:HS], A["ssd_dt_bias"][L1].to_broadcast([P, 2, HS]))
                param(dtb[:, :, HS:NDEC], A["gdn_dt_bias"][L1].to_broadcast([P, 2, HH]))
                param(alog[:, :, 0:HS], A["ssd_a_log"][L1].to_broadcast([P, 2, HS]))
                param(alog[:, :, HS:NDEC], A["gdn_a_log"][L1].to_broadcast([P, 2, HH]))
                param(dsk[:, :], A["ssd_d"][L1].to_broadcast([P, HS]))
                param(rbias[:, :], A["router_bias"][L1].to_broadcast([P, NE]))

                def ring_block(n, dst, src):
                    wait("ring_used", n + 1, l)
                    sp.dma_start(dst, src).then_inc(S[f"ring_full{n % 2}"], 16)

                with sp.Fori(1, N_MOD // NSLOT) as i:
                    for s in range(NSLOT):
                        sp.wait_ge(S["mod_used"], l * N_MOD + i * NSLOT + (s + 1 - NSLOT))
                        past()
                        sp.dma_start(wgu[s][:, :, :], wmod[:, :, bass.ds(i * (NSLOT * MW) + s * MW, MW)]).then_inc(S[f"w{s}"], 16)
                win = A["w_in"][L1].rearrange("o (k p) n -> p (o k) n", p=P)
                sp.dma_start(wsm[:, :, 0:16], win[:, :, 3 * SW:3 * SW + 16]).then_inc(S["small_loaded"], 16)
                sp.dma_start(wsm[:, :, 16:32], win[:, :, COL_GDN + 3 * HW:COL_GDN + 3 * HW + 16]).then_inc(S["small_loaded"], 16)
                for n, (_, col, _) in enumerate(IN_BLOCKS):
                    m = n
                    ring_block(m, ring[:, m % 2, :, :], win[:, :, col:col + BW])
                for c in range(NT):
                    sp.dma_start(acc_odd[tk(c), :].rearrange("p (a b) -> p a b", b=P),
                                 zero[:, :].unsqueeze(1).to_broadcast([P, KT, P])).then_inc(S["acc_zeroed"], 16)
                sp.dma_start(rw[:, :, :], A["router_w"][L1].rearrange("o (k p) n -> p (o k) n", p=P)).then_inc(S["rw_loaded"], 16)
                wout = A["w_out"][L1].rearrange("o (k p) n -> p (o k) n", p=P)
                for n in range(N_OUT):
                    m = N_IN + n
                    ring_block(m, ring[:, m % 2, :, :], wout[:, :, n * BW:(n + 1) * BW])
                    if n == 0:
                        wait("hgrn_done", U, l)
                        for q in range(1):
                            sp.dma_start(nrow[:, 0:SW], A["ssd_norm"][L1].to_broadcast([P, SW])).then_inc(S["nrow_loaded"], 16)
                            sp.dma_start(nrow[:, SW:SW + HD], A["hgrn_norm"][L1].to_broadcast([P, HD])).then_inc(S["nrow_loaded"], 16)
                            sp.dma_start(nrow[:, SW + HW:SW + HW + HD], A["gdn_norm"][L1].to_broadcast([P, HD])).then_inc(S["nrow_loaded"], 16)
                for n, name in enumerate(("sh_gate", "sh_up")):
                    m = N_IN + N_OUT + n
                    ring_block(m, ring[:, m % 2, :, :], A[name][L1].rearrange("o (k p) n -> p (o k) n", p=P))
                wait("wo_sb", N_OUT, l)
                gate_w = A["exp_gate"][L1].rearrange("o e (k p) n -> p (o e) k n", p=P)
                up_w = A["exp_up"][L1].rearrange("o e (k p) n -> p (o e) k n", p=P)
                down_w = A["exp_down"][L1].rearrange("o e (k p) n -> p (o e) k n", p=P)

                def expert(s, e):
                    one = bass.ds(e, 1)
                    sp.dma_start(wgu[s][:, :, 0:ED], gate_w[:, one].rearrange("p e k n -> p (e k) n")).then_inc(S[f"w{s}"], 16)
                    sp.dma_start(wgu[s][:, :, ED:2 * ED], up_w[:, one].rearrange("p e k n -> p (e k) n")).then_inc(S[f"w{s}"], 16)
                    sp.dma_start(wdn[s][:, :, :], down_w[:, one].rearrange("p e k n -> p (e k) n")).then_inc(S[f"w{s}"], 16)

                for s in range(NSLOT):
                    expert(s, s)
                for c in range(NT):
                    wait("ftok_sb", c + 1, l)
                    sp.dma_start(f_dram[tk(c), :], X[:, c % 2, :]).then_inc(S[f"x_stored{c % 2}"], 16)
                m = N_IN + N_OUT + 2
                ring_block(m, ring[:, m % 2, :, :].rearrange("p (a b) n -> p a (b n)", a=2),
                           A["sh_down"][L1].rearrange("o (k p) n -> p (o k) n", p=P))
                for c in range(NT):
                    wait("shd_sb", c + 1, l)
                    sp.dma_start(acc_dram[tk(c), :], X[:, c % 2, :]).then_inc(S[f"x_stored{c % 2}"], 16)
                with sp.Fori(1, NE // NSLOT) as i:
                    for s in range(NSLOT):
                        sp.wait_ge(S["dn_ps"], l * NE + i * NSLOT + (s - NSLOT + 1))
                        past()
                        expert(s, i * NSLOT + s)
                wait("oe_act", NE, l)
                wait("oe_dve", NE, l)
                sp.wait_ge(S["flag_ready"], l + 1)
                sp.sem_inc(S["past"], 1)
                over = sp.value_load(flagi[0:1, 0:1], min_val=0, max_val=1)
                with sp.If(over > 0):
                    with sp.Fori(1, NBLK) as b:
                        with sp.Fori(0, NE) as e:
                            one = bass.ds(e, 1)
                            sp.wait_ge(S["ov_sc"], l * OVER + b * NE + e + (1 - NE))
                            past()
                            need = sp.value_load(more[0:1, bass.ds(b * NE + e, 1)], min_val=0, max_val=1)
                            with sp.If(need > 0):
                                sp.dma_start(wgu[0][:, :, 0:ED], gate_w[:, one].rearrange("p e k n -> p (e k) n")).then_inc(S["ov_w"], 16)
                                sp.dma_start(wgu[0][:, :, ED:2 * ED], up_w[:, one].rearrange("p e k n -> p (e k) n")).then_inc(S["ov_w"], 16)
                                sp.dma_start(wdn[0][:, :, :], down_w[:, one].rearrange("p e k n -> p (e k) n")).then_inc(S["ov_w"], 16)
                                sp.dma_start(idxS[0][:, :], tab_dram[bass.ds(b * P, P), one, :].rearrange("p o t -> p (o t)")).then_inc(S["ov_tab"], 16)
                            with sp.Else():
                                sp.sem_inc(S["ov_w"], 48)
                                sp.sem_inc(S["ov_tab"], 16)
                with sp.Else():
                    sp.sem_inc(S["ov_w"], PER["ov_w"])
                    sp.sem_inc(S["ov_tab"], PER["ov_tab"])
                wait("ov_sc", OVER + 1, l)
                for b in range(2):
                    wait(f"scattered{b}", 8 * NE, l)
                sp.dma_start(yraw[:, :, :], acc_odd.rearrange("(c p) f -> p c f", p=P)).then_inc(S["odd_loaded"], 16)
                for c in range(NT):
                    if c >= 2:
                        wait("acc_added", c - 1, l)
                    sp.dma_start(X[:, c % 2, :], acc_dram[tk(c), :]).then_inc(S[f"acc_loaded{c % 2}"], 16)
            sp.wait_ge(S["h_ready"], DEPTH + 1)
            sp.dma_start(grow[:, 0, :], A["norm_final"].rearrange("(o f) -> o f", o=1).to_broadcast([P, DM])).then_inc(S["out_loaded"], 16)
            for c in range(2):
                sp.wait_ge(S["out_ready"], c + 1)
                sp.dma_start(out[0, tk(c), :], X[:, c, :]).then_inc(S["out_stored"], 16)
            sp.wait_ge(S["out_stored"], 32)

        @block.gpsimd
        def _(pool):
            G = nc.gpsimd

            def wait(name, n, l):
                pool.wait_ge(S[name], l * PER[name] + n)
                pool.sem_inc(S["past"], 1)

            def do(ins, name=None, n=1):
                if name:
                    ins.then_inc(S[name], n)
                pool.drain()

            do(G.memset(ones[:, :], 1.0))
            do(G.memset(bd[:, :], 0.0))
            do(G.memset(zero[:, :], 0.0))
            do(G.memset(bd[0:HD, 0:HD], 1.0))
            do(G.memset(bd[HD:P, HD:P], 1.0))
            do(G.affine_select(tri[:, 0, :], ones[:, :], [[1, P]], ALU.is_ge, 0.0, base=0, channel_multiplier=-1))
            do(G.affine_select(tri[:, 1, :], ones[:, :], [[-1, P]], ALU.is_ge, 0.0, base=0, channel_multiplier=1))
            do(G.affine_select(triS[:, :], ones[:, :], [[1, P]], ALU.is_gt, 0.0, base=0, channel_multiplier=-1))
            do(G.affine_select(ident[:, :], ones[:, :], [[1, P]], ALU.is_equal, 0.0, base=0, channel_multiplier=-1))
            do(G.iota(levt[:, 0, :], pattern=[[0, P]], base=0, channel_multiplier=1))
            do(G.iota(levt[:, 1, :], pattern=[[1, P]], base=0, channel_multiplier=0))
            do(G.iota(tokid[:, :], pattern=[[P, NT]], base=0, channel_multiplier=1))
            do(G.iota(iota_e[:, :], pattern=[[1, NE]], base=0, channel_multiplier=0, allow_small_or_imprecise_dtypes=True))
            do(G.memset(live[:, :, :], 1.0))
            do(G.memset(live[:, DEPTH - 1, 0:CTX // P], 0.0))
            do(G.memset(cst[:, 0:1], EPS))
            do(G.memset(cst[:, 1:2], -math.log(math.sqrt(HD))))
            do(G.memset(cst[:, 2:3], -40.0 * math.log(2.0)))
            do(G.memset(cst[:, 3:4], 0.0))
            pool.sem_inc(S["ring_used"], 2)
            pool.sem_inc(S["ov_sc"], 1)
            pool.drain().then_inc(S["const_pool"], 1)
            with pool.Fori(0, DEPTH) as l:
                wait("h_ready", 1, l)
                do(G.memset(Ss[:, :, :, :], 0.0))
                do(G.memset(Sh[:, :, :, :], 0.0))
                do(G.memset(Sg[:, :, :, :], 0.0), "s_init")
                wait("tok_d", NT, l)
                for u, (i, d, c) in enumerate(UNITS):
                    wait("small_done", 1, l) if u == 0 else wait("ho_ps", u, l)
                    if u:
                        wait("go_ps", u, l)
                    do(G.memset(attH[:, :, :], 0.0), "a_init")
                    do(G.tensor_copy(T[:, :, :], ident[:, :].unsqueeze(1).to_broadcast([P, HH, P])))
                    do(G.tensor_copy(TT[:, :, :], ident[:, :].unsqueeze(1).to_broadcast([P, HH, P])), "t_init")
                    wait("hexp", u + 1, l)
                    do(G.tensor_tensor(kL[:, :, :].rearrange("p j (t s) -> p j t s", t=2),
                                       e7[:, :, :].rearrange("p j (t s) -> p j t s", t=2),
                                       hk[:, d, :, tk(c)].unsqueeze(1).to_broadcast([P, LEVELS, 2, P]), ALU.mult), "kl_ready")
                    do(G.tensor_tensor(kw[:, :].rearrange("p (h k) -> p h k", h=HH),
                                       Ktok[:, c, :].rearrange("p (h k) -> p h k", h=HH),
                                       wend[:, c, d, HS:NDEC].unsqueeze(2).to_broadcast([P, HH, HD]), ALU.mult), "kw_ready")
                    for j in range(LEVELS):
                        if j == 0:
                            wait("at_ready", u + 1, l)
                        else:
                            wait("p_ps", u * LEVELS + j, l)
                        do(G.tensor_tensor(NTm[:, :, :], AT[:, :, :],
                                           lev[:, d, j, :].unsqueeze(1).to_broadcast([P, HH, P]), ALU.mult), "nt_ready")
                wait("blank_ready", 1, l)
                pool.dma_start(tab_dram.rearrange("a e t -> (a e t)").rearrange("(p n) -> p n", p=P),
                               blank[:, :, :].rearrange("p a b -> p (a b)")).then_inc(S["blank_dram"], 16)
                wait("blank_dram", 16, l)
                wait("pay_ready", 1, l)
                rows = tab_dram.rearrange("a e t -> (a e) t")
                for n in range(NT * TOPK):
                    pool.indirect_dma_start(rows, bass.IndirectOffsetOnAxis(dsti[:, n, :].bitcast(U32), 0), pay[:, n, :], None,
                                            bounds_check=CAP * NE - 1, oob_is_err=False).then_inc(S["tab_dram"], 16)
                wait("tab_dram", 16 * NT * TOPK, l)
                wait("shd_ps", NT, l)
                wait("shd_sb", NT, l)
                pool.dma_start(tabA[:, :, :], tab_dram[0:P, :, :]).then_inc(S["tab_loaded"], 16)
                for s in range(NSLOT - 1):
                    do(G.memset(xg[s], 0.0))
                do(G.memset(xg[NSLOT - 1], 0.0), "xg_init")
                wait("tab_loaded", 16, l)
                wait("acc_zeroed", 16 * NT, l)
                for b in range(2):
                    wait(f"x_stored{b}", 64, l)

                def gather(s, e):
                    pool.wait_ge(S["idx_in"], l * NE + e + 1)
                    pool.sem_inc(S["past"], 1)
                    pool.indirect_dma_start(xg[s], None, f_dram, bass.IndirectOffsetOnAxis(idxG[s][:, 0:1].bitcast(U32), 0),
                                            bounds_check=TOK - 1, oob_is_err=False).then_inc(S[f"gathered{s}"], 16)

                def pool_step(i, s, ahead):
                    e = l * NE + i * NSLOT + s
                    first = isinstance(i, int) and i == 0
                    if ahead > 3:
                        if not (first and s == 0):
                            pool.wait_ge(S["xt_ps"], e)
                            pool.sem_inc(S["past"], 1)
                        gather((s + 3) % NSLOT, i * NSLOT + s + 3)
                    pool.wait_ge(S["oe_act"], e + 1)
                    pool.wait_ge(S["oe_dve"], e + 1)
                    pool.sem_inc(S["past"], 1)
                    if not (first and s < 2):
                        pool.wait_ge(S[f"scattered{s % 2}"], l * (8 * NE) + i * 32 + (s // 2) * 16)
                        pool.sem_inc(S["past"], 1)
                    pool.indirect_dma_start((acc_dram, acc_odd)[s % 2], bass.IndirectOffsetOnAxis(idxS[s][:, 0:1].bitcast(U32), 0),
                                            oe[s % 2], None, bounds_check=TOK - 1, oob_is_err=False,
                                            compute_op=ALU.add).then_inc(S[f"scattered{s % 2}"], 16)

                for s in range(3):
                    gather(s, s)
                for s in range(NSLOT):
                    pool_step(0, s, NSLOT + 1)
                with pool.Fori(1, NE // NSLOT - 1) as i:
                    for s in range(NSLOT):
                        pool_step(i, s, NSLOT + 1)
                for s in range(NSLOT):
                    pool_step(NE // NSLOT - 1, s, NSLOT - s)
                for b in range(2):
                    wait(f"scattered{b}", 8 * NE, l)
                over = pool.value_load(flagi[0:1, 0:1], min_val=0, max_val=1)
                with pool.If(over > 0):
                    with pool.Fori(0, OVER) as n_:
                        n = l * OVER + n_
                        pool.wait_ge(S["ov_tab"], n * 16 + 16)
                        pool.sem_inc(S["past"], 1)
                        need = pool.value_load(more[0:1, bass.ds(n_ + NE, 1)], min_val=0, max_val=1)
                        with pool.If(need > 0):
                            pool.indirect_dma_start(xg[0], None, f_dram, bass.IndirectOffsetOnAxis(idxS[0][:, 0:1].bitcast(U32), 0),
                                                    bounds_check=TOK - 1, oob_is_err=False).then_inc(S["ov_dma"], 16)
                            pool.wait_ge(S["ov_dma"], 16)
                            pool.dma_reset(range(S["ov_dma"].num, S["ov_dma"].num + 1))
                            pool.sem_clear(S["ov_dma"])
                            pool.drain().then_inc(S["ov_g"], 1)
                            pool.wait_ge(S["ov_oe"], n + 1)
                            pool.sem_inc(S["past"], 1)
                            pool.indirect_dma_start(acc_dram, bass.IndirectOffsetOnAxis(idxS[0][:, 0:1].bitcast(U32), 0), oe[0], None,
                                                    bounds_check=TOK - 1, oob_is_err=False, compute_op=ALU.add).then_inc(S["ov_dma"], 16)
                            pool.wait_ge(S["ov_dma"], 16)
                            pool.dma_reset(range(S["ov_dma"].num, S["ov_dma"].num + 1))
                            pool.sem_clear(S["ov_dma"])
                            pool.drain().then_inc(S["ov_sc"], 1)
                        with pool.Else():
                            pool.sem_inc(S["ov_g"], 1)
                            pool.sem_inc(S["ov_sc"], 1)
                with pool.Else():
                    pool.sem_inc(S["ov_g"], PER["ov_g"])
                    pool.sem_inc(S["ov_sc"], PER["ov_sc"])

        @block.scalar
        def _(act):
            C = nc.scalar

            def wait(name, n, l):
                act.wait_ge(S[name], l * PER[name] + n)

            def do(ins, name=None):
                if name:
                    ins.then_inc(S[name], 1)
                act.drain()

            def f(out_, in_, func, name=None, **kw):
                do(C.activation(out_, in_, func, **kw), name)

            act.wait_ge(S["const_pool"], 1)
            act.wait_ge(S["cond_ps"], 1)
            f(condT[:, :, :].rearrange("p a k -> p (a k)"), ps[:, 0, 0:2 * KT], ACT.Silu, "cond_sb")
            act.wait_ge(S["low_a"], 1)
            f(low[:, :, :], low[:, :, :], ACT.Exp, "low_b")

            def norm_turn(q, l):
                wait("sumsq", q + 1, l)
                f(st[:, 4:8], st[:, 0:4], ACT.Ln, scale=1.0 / DM, bias=cst[:, 0:1])
                f(st[:, 8:12], st[:, 4:8], ACT.Exp, "rstd", scale=-0.5)
                for c in range(NT):
                    wait("xT_ps", q * NT + c + 1, l)
                    for k in range(KT // 2, KT):
                        ins = C.activation(featT[:, k, tk(c)], bank(4 + 2 * (c % 2), 2)[:, tk(k)], ACT.Identity,
                                           scale=amul[:, q, k, c // 2:c // 2 + 1], bias=mod[:, 24 * q + k, c // 2:c // 2 + 1])
                    do(ins, "feat_a")

            with act.Fori(0, DEPTH) as l:
                wait("h_ready", 1, l)
                with act.Fori(0, N_MOD // NSLOT) as i:
                    for s in range(NSLOT):
                        act.wait_ge(S["mod_used"], l * N_MOD + i * NSLOT + (s + 1))
                        f(X[0:2, s % 2, 0:MW], ps[0:2, 4 + s % 2, :], ACT.Identity, "mod_row")
                wait("mod_sb", 1, l)
                norm_turn(0, l)
                for n in range(N_CONV):
                    for half in range(2):
                        t = 2 * n + half
                        wait("conv_out", t + 1, l)
                        b = prm[:, R_CBS + t:R_CBS + t + 1] if t < 8 else cst[:, 3:4]
                        C.activation(cv[:, t, 0:CTX], cvo[:, half, 0:CTX], ACT.Silu, bias=b)
                        do(C.activation(cv[:, t, CTX:TOK].rearrange("p (r x) -> p r x", r=ROWS),
                                        line_rows(cvo[:, half, :]), ACT.Silu, bias=b), "silu_out")
                for n in range(N_CONV, N_IN):
                    kind, _, i = IN_BLOCKS[n]
                    b0 = UB[n % 3]
                    wait("u_ps", n + 1, l)
                    if kind == "hq":
                        f(hq[:, :, :], ps[:, b0:b0 + 2, :], ACT.Silu, "u_act")
                    elif kind == "gate":
                        f(gates[:, :, i * BW:(i + 1) * BW], bank(b0, 2).rearrange("p (c f) -> p c f", c=NT), ACT.Silu, "u_act")
                    elif kind == "val":
                        f(val[:, :, :], bank(b0, 2).rearrange("p (c f) -> p c f", c=NT), ACT.Identity, "u_act")
                    else:
                        f(logf[:, i, :, :], ps[:, b0:b0 + 2, :], ACT.Identity, "u_act")
                wait("sp_x", 1, l)
                f(nega[:, :, :], alog[:, :, :], ACT.Exp)
                f(beta[:, :, :, :], beta[:, :, :, :], ACT.Exp, scale=-1.0)
                f(spw[:, 1, :], spw[:, 0, :], ACT.Abs)
                f(spw[:, 1, :], spw[:, 1, :], ACT.Exp, scale=-1.0)
                f(spw[:, 2, :], spw[:, 1, :], ACT.Ln, "sp_exp", bias=ones[:, 0:1])
                wait("low_c", 1, l)
                f(lowv[:, 1, :], lowv[:, 1, :], ACT.Ln)
                f(lowv[:, 1, :], lowv[:, 1, :], ACT.Identity, "lowl", bias=cst[:, 2:3])
                f(hwt[:, :, :], logf[:, :, :, :].rearrange("p a b t -> p (a b) t"), ACT.Abs)
                f(hwt[:, :, :], hwt[:, :, :], ACT.Exp, scale=-1.0)
                f(hwt[:, :, :], hwt[:, :, :], ACT.Ln, "hg_b", bias=ones[:, 0:1])
                wait("hg_c", 1, l)
                f(hwt[:, :, :], hwx[:, :, :], ACT.Abs)
                f(hwt[:, :, :], hwt[:, :, :], ACT.Exp, scale=-1.0)
                f(hwt[:, :, :], hwt[:, :, :], ACT.Ln, "hg_d", bias=ones[:, 0:1])
                wait("hg_e", 1, l)
                f(hk[:, :, :, :].rearrange("p a b t -> p (a b) t"), hwt[:, :, :], ACT.Exp, "hg_f")
                wait("cum_dve", 1, l)
                f(eacs[:, :, :, :], acs[:, :, :, :], ACT.Exp)
                f(wend[:, :, :, :], wend[:, :, :, :], ACT.Exp)
                f(etot[:, :, :, :], etot[:, :, :, :], ACT.Exp, "cum_act")
                for t in range(4):
                    wait("l2_ps", t + 1, l)
                    f(lnw[:, :], ps[:, t % 2, :], ACT.Ln, bias=cst[:, 0:1])
                    if t:
                        wait("l2_done", t, l)
                    f(lnx[:, :], lnw[:, :], ACT.Exp, "l2_act", scale=-0.5, bias=cst[:, 1:2] if t < 2 else cst[:, 3:4])
                for c in range(NT):
                    wait("tok_ps", c + 1, l)
                    b0 = 4 * (c % 2)
                    C.activation(Btok[:, c, :], ps[:, b0 + 1, 0:HW], ACT.Identity)
                    do(C.activation(Ktok[:, c, :], ps[:, b0 + 1, HW:2 * HW], ACT.Identity), "tok_a")
                for u, (i, d, c) in enumerate(UNITS):
                    wait("b_ready", u + 1, l)
                    f(e7[:, :, :], e7[:, :, :], ACT.Abs)
                    f(e7[:, :, :], e7[:, :, :], ACT.Exp, scale=-1.0)
                    f(eb[:, :], bh[:, :], ACT.Exp)
                    f(e1[:, :], e1[:, :], ACT.Exp, "hexp", scale=-1.0)
                    wait("dm_ready", u + 1, l)
                    f(E[:, :, :], E[:, :, :], ACT.Exp, "e_ready")
                    for j in range(LEVELS):
                        wait("p_ps", u * LEVELS + j + 1, l)
                        f(Pm[:, :, :].rearrange("p h t -> p (h t)"), ps[:, 1, :], ACT.Identity, "p_sb")
                        if j == 5:
                            wait("ke_ps", u + 1, l)
                            f(kendT[:, :], ps[:, 5, 0:2 * P], ACT.Identity, "ke_sb")
                    wait("vn_ps", u + 1, l)
                    f(vn[:, :], ps[:, 1, HW:2 * HW], ACT.Identity, "vn_sb")
                wait("y_sq", 1, l)
                f(ssq[:, :, 0:2], ssq[:, :, 0:2], ACT.Ln, scale=1.0 / HW, bias=cst[:, 0:1])
                f(ssq[:, :, 2:10], ssq[:, :, 2:10], ACT.Ln, scale=1.0 / HD, bias=cst[:, 0:1])
                f(ssq[:, :, :], ssq[:, :, :], ACT.Exp, "y_rstd", scale=-0.5)
                for j in range(2):
                    wait("grow_ps", j + 1, l)
                    f(grow[:, j, :], bank(2 * j, 2), ACT.Identity, "grow_sb")
                for c in range(NT):
                    wait("yT_ps", c + 1, l)
                    f(yT[:, :, tk(c)], bank(4 + 2 * (c % 2), 2).rearrange("p (k t) -> p k t", k=KT), ACT.Identity, "yT_sb")
                norm_turn(1, l)
                wait("lg_ps", 1, l)
                f(scor[:, :, :], ps[:, 0, 0:NT * NE].rearrange("p (c e) -> p c e", c=NT), ACT.Exp, "lg_exp", scale=-1.0)
                wait("sh_ps", 1, l)
                f(sgT[:, :, :], ps[:, 0:2, :], ACT.Silu, "sh_silu")
                def turned(e, b):
                    act.wait_ge(S["xt_ps"], e + 1)
                    do(C.activation(xgT[b][:, 0:4, :].rearrange("p k t -> p (k t)"), ps[:, 0, :], ACT.Identity), "xt_sb")

                def silu(e, b):
                    act.wait_ge(S["gu_ps"], e + 1)
                    f(sg[b].rearrange("p k t -> p (k t)"), ps[:, 2 + b, 0:ED], ACT.Silu, "gu_silu")

                def act_step(i, s, ahead):
                    e = l * NE + i * NSLOT + s
                    if ahead > 1:
                        silu(e + 1, (s + 1) % 2)
                    if ahead > 2:
                        turned(e + 2, s % 2)
                    act.wait_ge(S["idx_out"], e + 1)
                    if not (isinstance(i, int) and i == 0 and s < 2):
                        act.wait_ge(S[f"scattered{s % 2}"], l * (8 * NE) + i * 32 + (s // 2) * 16)
                    act.wait_ge(S["dn_ps"], e + 1)
                    f(oe[s % 2][:, 0:512], ps[:, 4 + 2 * (s % 2), :], ACT.Identity, "oe_act", scale=idxS[s][:, 1:2])

                turned(l * NE, 0)
                silu(l * NE, 0)
                turned(l * NE + 1, 1)
                for s in range(NSLOT):
                    act_step(0, s, NSLOT + 1)
                with act.Fori(1, NE // NSLOT - 1) as i:
                    for s in range(NSLOT):
                        act_step(i, s, NSLOT + 1)
                for s in range(NSLOT):
                    act_step(NE // NSLOT - 1, s, NSLOT - s)
                act.wait_ge(S["flag_ready"], l + 1)
                act.sem_inc(S["past"], 1)
                over = act.value_load(flagi[0:1, 0:1], min_val=0, max_val=1)
                with act.If(over > 0):
                    with act.Fori(0, OVER) as n_:
                        need = act.value_load(more[0:1, bass.ds(n_ + NE, 1)], min_val=0, max_val=1)
                        with act.If(need > 0):
                            act.wait_ge(S["ov_gu"], l * OVER + n_ + 1)
                            f(sg[0].rearrange("p k t -> p (k t)"), ps[:, 2, 0:ED], ACT.Silu, "ov_sl")
                        with act.Else():
                            act.sem_inc(S["ov_sl"], 1)
                with act.Else():
                    act.sem_inc(S["ov_sl"], OVER)
            wait("sumsq", 1, DEPTH)
            f(st[:, 4:6], st[:, 0:2], ACT.Ln, scale=1.0 / DM, bias=cst[:, 0:1])
            f(st[:, 8:10], st[:, 4:6], ACT.Exp, "rstd", scale=-0.5)

        @block.vector
        def _(dve):
            V = nc.vector

            def wait(name, n, l):
                dve.wait_ge(S[name], l * PER[name] + n)

            def do(ins, name=None):
                if name:
                    ins.then_inc(S[name], 1)
                dve.drain()

            def tt(out_, a, b, op, name=None):
                do(V.tensor_tensor(out_, a, b, op), name)

            def ts(out_, a, s1, s2, op0, op1=None, name=None):
                do(V.tensor_scalar(out_, a, s1, s2, op0, *(() if op1 is None else (op1,))), name)

            def stt(out_, a, s_, b, op0, op1, name=None):
                do(V.scalar_tensor_tensor(out_, a, s_, b, op0, op1), name)

            def cp(out_, in_, name=None):
                do(V.tensor_copy(out_, in_), name)

            dve.wait_ge(S["const_pool"], 1)
            tt(levt[:, 0, :], levt[:, 0, :], levt[:, 1, :], ALU.bitwise_xor)
            for j in range(LEVELS):
                ts(levt[:, 1, :], levt[:, 0, :], j, None, ALU.logical_shift_right)
                cp(lev[:, 0, j, :], levt[:, 1, :])
                ts(lev[:, 0, j, :], lev[:, 0, j, :], 1.0, None, ALU.is_equal)
                tt(lev[:, 1, j, :], lev[:, 0, j, :], tri[:, 1, :], ALU.mult)
                tt(lev[:, 0, j, :], lev[:, 0, j, :], triS[:, :], ALU.mult)
            for d in range(2):
                ts(negm[:, d, :], tri[:, d, :], -1.0, -NEG, ALU.add, ALU.mult)
            dve.drain().then_inc(S["const_ready"], 1)
            dve.wait_ge(S["cond_ps"], 1)
            cp(low[:, :, :].rearrange("p l t -> p (l t)"), ps[:, 3, 0:4])
            tt(lowv[:, 0, :], low[:, 0, :], low[:, 1, :], ALU.max)
            tt(low[:, :, :], low[:, :, :], lowv[:, 0:1, :].to_broadcast([P, DEPTH, 2]), ALU.subtract, "low_a")
            dve.wait_ge(S["low_b"], 1)
            tt(lowv[:, 0, :], low[:, 0, :], low[:, 1, :], ALU.add)
            do(V.reciprocal(lowv[:, 1, :], lowv[:, 0, :]))
            tt(low[:, :, :], low[:, :, :], lowv[:, 1:2, :].to_broadcast([P, DEPTH, 2]), ALU.mult)
            tt(lowv[:, 0, :], low[:, 0, :], low[:, 1, :], ALU.add)
            tt(low[:, 1, :], lowv[:, 0, :], low[:, 0, :], ALU.subtract)
            tt(low[:, 0, :], low[:, 0, :], low[:, 0, :], ALU.subtract)
            dve.wait_ge(S["cond_sb"], 1)
            dve.wait_ge(S["head_loaded"], 16 * 5)
            dve.drain().then_inc(S["h_ready"], 1)

            def norm_turn(q, l):
                for c in range(NT):
                    V.tensor_tensor_reduce(out=X[:, c % 2, :], in0=h[:, c, :], in1=h[:, c, :], scale=1.0, scalar=0.0,
                                           op0=ALU.mult, op1=ALU.add, accum_out=st[:, c:c + 1])
                    dve.drain()
                dve.drain().then_inc(S["sumsq"], 1)
                wait("rstd", q + 1, l)
                for c in range(NT):
                    if c >= 2:
                        wait("xT_ps", q * NT + c - 1, l)
                    ts(X[:, c % 2, :], h[:, c, :], st[:, 8 + c:9 + c], None, ALU.mult, name="xn")
                    if c >= 1:
                        turned(q, c - 1, l)
                turned(q, NT - 1, l)

            def turned(q, c, l):
                wait("xT_ps", q * NT + c + 1, l)
                for k in range(KT // 2):
                    ins = V.tensor_scalar(featT[:, k, tk(c)], bank(4 + 2 * (c % 2), 2)[:, tk(k)],
                                          amul[:, q, k, c // 2:c // 2 + 1], mod[:, 24 * q + k, c // 2:c // 2 + 1],
                                          ALU.mult, ALU.add)
                do(ins, "feat_d")

            with dve.Fori(0, DEPTH) as l:
                L1 = bass.ds(l, 1)
                wait("prm_ps", 1, l)
                cp(prm[:, :], ps[:, 1, 0:N_PRM])
                cp(lowv[:, 0, :], low[:, L1, :].rearrange("p o t -> p (o t)"))
                ts(lowv[:, 2, :], lowv[:, 0, :], -1.0, 1.0, ALU.mult, ALU.add)
                ts(lowv[:, 1, :], lowv[:, 0, :], 1e-30, float(2.0 ** 40), ALU.max, ALU.mult, "low_c")
                wait("mod_ps", 1, l)
                tt(mod[:, :, :], ps[:, 2, 0:96].rearrange("p (r j) -> p r j", j=2),
                   prm[:, R_BMOD:R_BMOD + 48].unsqueeze(2).to_broadcast([P, 48, 2]), ALU.add)
                for q in range(2):
                    ts(amul[:, q, :, :], mod[:, 24 * q + 8:24 * q + 16, :], 1.0, None, ALU.add)
                    tt(amul[:, q, :, :], amul[:, q, :, :],
                       prm[:, R_NMIX + 8 * q:R_NMIX + 8 * q + 8].unsqueeze(2).to_broadcast([P, KT, 2]), ALU.mult)
                dve.drain().then_inc(S["mod_sb"], 1)
                norm_turn(0, l)
                do(V.memset(line[:, :, :], 0.0))
                for n in range(N_CONV):
                    wait("u_ps", n + 1, l)
                    for half in range(2):
                        src = ps[:, UB[n % 3] + half, :]
                        V.tensor_copy(line[:, half, HALF:HALF + CTX], src[:, 0:CTX])
                        V.tensor_copy(line[:, half, CPAD:LINE].rearrange("p (r x) -> p r x", r=ROWS)[:, :, HALF:HALF + GRID_W],
                                      src[:, CTX:TOK].rearrange("p (r x) -> p r x", r=ROWS))
                    dve.drain().then_inc(S["u_dve"], 1)
                    for half in range(2):
                        t = 2 * n + half
                        base, off, per = (R_CWS, t, 8) if t < 8 else (R_CWG, t - 8, 6)
                        if n:
                            wait("silu_out", t - 1, l)
                        for j in range(TAPS):
                            w = prm[:, base + j * per + off:base + j * per + off + 1]
                            o, s_ = cvo[:, half, 0:CONV], line[:, half, j:j + CONV]
                            if j == 0:
                                ts(o, s_, w, None, ALU.mult)
                            else:
                                stt(o, s_, w, o, ALU.mult, ALU.add, "conv_out" if j == TAPS - 1 else None)
                wait("sm_ps", 1, l)
                cp(sm[:, :, :].rearrange("p c f -> p (c f)"), ps[:, 3, 0:32 * NT])
                x3 = spw[:, 0, :].rearrange("p (c d h) -> p c d h", c=NT, d=2)
                for c in range(NT):
                    tt(x3[:, c, :, 0:HS], sm[:, c, 0:16].rearrange("p (d h) -> p d h", d=2), dtb[:, :, 0:HS], ALU.add)
                    tt(x3[:, c, :, HS:NDEC], sm[:, c, 16:24].rearrange("p (d h) -> p d h", d=2), dtb[:, :, HS:NDEC], ALU.add)
                    cp(beta[:, c, :, :].rearrange("p d h -> p (d h)"), sm[:, c, 24:32])
                dve.drain().then_inc(S["sp_x"], 1)
                wait("sp_exp", 1, l)
                ts(beta[:, :, :, :], beta[:, :, :, :], 1.0, None, ALU.add)
                do(V.reciprocal(beta[:, :, :, :], beta[:, :, :, :]))
                ts(spw[:, 3, :], spw[:, 1, :], 1.0, None, ALU.add)
                ts(spw[:, 3, :], spw[:, 3, :], -1.0, None, ALU.add)
                dtf = dt_[:, :, :, :].rearrange("p c d h -> p (c d h)")
                daf = da[:, :, :, :].rearrange("p c d h -> p (c d h)")
                ts(dtf, spw[:, 3, :], 0.0, None, ALU.is_equal)
                tt(spw[:, 2, :], spw[:, 2, :], dtf, ALU.add)
                tt(spw[:, 3, :], spw[:, 3, :], dtf, ALU.add)
                do(V.reciprocal(spw[:, 3, :], spw[:, 3, :]))
                tt(spw[:, 1, :], spw[:, 1, :], spw[:, 3, :], ALU.mult)
                tt(spw[:, 1, :], spw[:, 1, :], spw[:, 2, :], ALU.mult)
                stt(dtf, spw[:, 0, :], 0.0, spw[:, 1, :], ALU.max, ALU.add)
                stt(da[:, :, :, :].rearrange("p c d h -> p c (d h)"), dt_[:, :, :, :].rearrange("p c d h -> p c (d h)"), -1.0,
                    nega[:, :, :].rearrange("p d h -> p (d h)").unsqueeze(1).to_broadcast([P, NT, 2 * NDEC]),
                    ALU.mult, ALU.mult, "sp_done")
                wait("u_act", N_IN - N_CONV, l)
                wait("lowl", 1, l)
                raw = logf[:, :, :, :].rearrange("p a b t -> p (a b) t")
                ls = hk[:, :, :, :].rearrange("p a b t -> p (a b) t")
                for q in range(4):
                    V.tensor_scalar(hwx[:, q, :], raw[:, q, :], -1.0, lowv[:, 1, q % 2:q % 2 + 1], ALU.mult, ALU.add)
                dve.drain()
                wait("hg_b", 1, l)
                stt(ls, raw, 0.0, hwt[:, :, :], ALU.min, ALU.subtract)
                dve.drain().then_inc(S["hg_c"], 1)
                wait("cum_ps", 1, l)
                for d in range(2):
                    cp(acs[:, :, d, :], ps[:, 2, 48 * d:48 * d + 48].rearrange("p (c h) -> p c h", c=NT))
                cp(etot[:, :, :, :].rearrange("p c d h -> p (c d h)"), ps[:, 2, 96:192])
                tt(wend[:, :, :, :], etot[:, :, :, :], acs[:, :, :, :], ALU.subtract, "cum_dve")
                wait("hg_d", 1, l)
                stt(hwx[:, :, :], hwx[:, :, :], 0.0, hwt[:, :, :], ALU.max, ALU.add)
                tt(hwt[:, :, :], ls, raw, ALU.subtract)
                tt(raw, ls, hwx[:, :, :], ALU.add, "hg_e")
                for t in range(4):
                    if t >= 2:
                        wait("l2_ps", t - 1, l)
                    tt(sqw[:, t % 2, :], cv[:, 8 + t, :], cv[:, 8 + t, :], ALU.mult, "l2_sq")
                    if t >= 1:
                        wait("l2_act", t, l)
                        tt(cv[:, 7 + t, :], cv[:, 7 + t, :], lnx[:, :], ALU.mult, "l2_done")
                wait("l2_act", 4, l)
                tt(cv[:, 11, :], cv[:, 11, :], lnx[:, :], ALU.mult, "l2_done")
                wait("hg_f", 1, l)
                for t in range(2):
                    ts(hk[:, :, t, :], hk[:, :, t, :], lowv[:, 2, t:t + 1], None, ALU.mult)
                dve.drain()
                wait("cum_act", 1, l)
                tt(wdt[:, :, :, :], dt_[:, :, :, :], wend[:, :, :, :], ALU.mult)
                for t in range(2):
                    for par in range(2):
                        rows = slice(par * HD, (par + 1) * HD)
                        cp(dcol[rows, :, t], etot[rows, :, :, HS + 2 * t + par].rearrange("p c d -> p (c d)"))
                dve.drain().then_inc(S["small_done"], 1)
                for c in range(NT):
                    wait("tok_ps", c + 1, l)
                    b0 = 4 * (c % 2)
                    cp(cv[:, 0:4, tk(c)], ps[:, b0, :].rearrange("p (t f) -> p t f", t=4))
                    cp(cv[:, 12:14, tk(c)], ps[:, b0 + 2, 0:HW].rearrange("p (t f) -> p t f", t=2), "tok_d")
                wait("s_init", 1, l)
                for u, (i, d, c) in enumerate(UNITS):
                    first, last_step = SEEN[c] == u, i == NT - 1
                    end = P - 1 if d == 0 else 0
                    way = slice(None) if d == 0 else slice(None, None, -1)
                    b3 = bh[:, :].rearrange("p (t s) -> p t s", t=2)
                    for t in range(2):
                        V.tensor_tensor_scan(b3[:, t, way], ones[:, :], logf[:, d, t, tk(c)][:, way], 0.0, ALU.mult, ALU.add)
                    dve.drain()
                    for j in range(LEVELS):
                        w = 2 << j
                        mid = w // 2 - 1 if d == 0 else w // 2
                        v = bh[:, :].rearrange("p (n w) -> p n w", w=w)
                        V.tensor_tensor(e7[:, j, :].rearrange("p (n w) -> p n w", w=w), v,
                                        v[:, :, mid:mid + 1].to_broadcast([P, 2 * P // w, w]), ALU.subtract)
                    V.tensor_tensor(e1[:, :].rearrange("p (t s) -> p t s", t=2), b3, b3[:, :, end:end + 1].to_broadcast([P, 2, P]), ALU.subtract)
                    dve.drain().then_inc(S["b_ready"], 1)
                    wait("pre_ps", u + 1, l)
                    tt(E[:, :, :], bank(3, 3).rearrange("p (h t) -> p h t", h=NDEC),
                       acs[:, c, d, :].unsqueeze(2).to_broadcast([P, NDEC, P]), ALU.subtract)
                    tt(E[:, :, :], E[:, :, :], negm[:, d, :].unsqueeze(1).to_broadcast([P, NDEC, P]), ALU.add, "dm_ready")
                    wait("hexp", u + 1, l)
                    q3 = hq[:, :, tk(c)]
                    cp(hdec[:, :], eb[:, :].rearrange("p (t s) -> p t s", t=2)[:, :, end])
                    tt(eb[:, :].rearrange("p (t s) -> p t s", t=2), eb[:, :].rearrange("p (t s) -> p t s", t=2), q3, ALU.mult)
                    tt(kend[:, :].rearrange("p (t s) -> p t s", t=2), e1[:, :].rearrange("p (t s) -> p t s", t=2), hk[:, d, :, tk(c)], ALU.mult)
                    wait("e_ready", u + 1, l)
                    par_view = lambda ap: ap.rearrange("p (a b) t -> p b a t", b=2)
                    kk = ps[:, 1:3, 0:HW].rearrange("p b (a t) -> p b a t", a=2)
                    qk = ps[:, 1:3, HW:2 * HW].rearrange("p b (a t) -> p b a t", a=2)
                    tt(par_view(AT[:, :, :]), kk, par_view(E[:, HS:NDEC, :]), ALU.mult)
                    tt(AT[:, :, :].rearrange("p h t -> p (h t)"), AT[:, :, :].rearrange("p h t -> p (h t)"), ps[:, 6, :], ALU.mult)
                    tt(par_view(E[:, HS:NDEC, :]), qk, par_view(E[:, HS:NDEC, :]), ALU.mult, "at_ready")
                    tt(E[:, 0:HS, :], E[:, 0:HS, :], dt_[:, c, d, 0:HS].unsqueeze(2).to_broadcast([P, HS, P]), ALU.mult)
                    tt(E[:, 0:HS, :].rearrange("p (g r) t -> p g r t", g=NG), E[:, 0:HS, :].rearrange("p (g r) t -> p g r t", g=NG),
                       ps[:, 0, 0:NG * P].rearrange("p (g t) -> p g t", g=NG).unsqueeze(2).to_broadcast([P, NG, HS // NG, P]), ALU.mult)
                    xs = cv[:, 0:4, tk(c)].rearrange("p a (b x) -> p a b x", b=2)
                    by_head = lambda ap: ap.rearrange("p (a b x) -> p a b x", a=4, b=2)
                    heads = lambda v: v.rearrange("p (a b) -> p a b", b=2).unsqueeze(3).to_broadcast([P, 4, 2, HD])
                    tt(by_head(xw[:, :]), xs, heads(wdt[:, c, d, 0:HS]), ALU.mult, "att_ready")
                    wait("kl_ready", u + 1, l)
                    tt(e7[:, :, :].rearrange("p j (t s) -> p j t s", t=2), e7[:, :, :].rearrange("p j (t s) -> p j t s", t=2),
                       q3.unsqueeze(1).to_broadcast([P, LEVELS, 2, P]), ALU.mult, "ql_ready")
                    for j in range(LEVELS):
                        wait("q_ps", u * LEVELS + j + 1, l)
                        if j < LEVELS - 1:
                            tt(T[:, :, :].rearrange("p h t -> p (h t)"), T[:, :, :].rearrange("p h t -> p (h t)"), ps[:, 2, :], ALU.subtract)
                        tt(TT[:, :, :].rearrange("p h t -> p (h t)"), TT[:, :, :].rearrange("p h t -> p (h t)"), ps[:, 3, :],
                           ALU.subtract, "t_ready")
                        if j < 4:
                            if j == 0:
                                wait("a_init", u + 1, l)
                            wait("h_ps", u * 4 + j + 1, l)
                            dve.sem_inc(S["past"], 1)
                            for r in range(2):
                                lv = 2 * j + r
                                m = lev[:, d, lv, :] if lv < LEVELS else ident[:, :]
                                do(V.copy_predicated(par_view(attH[:, :, :]),
                                                     m.bitcast(I32).unsqueeze(1).unsqueeze(1).to_broadcast([P, 2, 2, P]),
                                                     ps[:, 4:6, r * HW:(r + 1) * HW].rearrange("p b (a t) -> p b a t", a=2)),
                                   "h_cp" if r else None)
                        if j == 4:
                            wait("ssd_ps", u + 1, l)
                            tt(by_head(tmp[:, :]), by_head(ps[:, 6, :]), heads(eacs[:, c, d, 0:HS]), ALU.mult)
                            if first:
                                tt(yraw[:, c, 0:SW], tmp[:, :], ps[:, 7, :], ALU.add)
                                tt(by_head(tmp[:, :]), xs, heads(dsk[:, :]), ALU.mult)
                            else:
                                tt(tmp[:, :], tmp[:, :], ps[:, 7, :], ALU.add)
                            tt(yraw[:, c, 0:SW], yraw[:, c, 0:SW], tmp[:, :], ALU.add, "ssd_sb" if last_step else None)
                            if not last_step:
                                sv = Ss[:, d, :, :].rearrange("p g f -> p (g f)")
                                tt(by_head(sv), by_head(sv), heads(etot[:, c, d, 0:HS]), ALU.mult)
                                tt(sv, sv, ps[:, 0, :], ALU.add, "ssd_sb")
                    wait("gks_ps", u + 1, l)
                    r3 = rr[:, :].rearrange("p (h v) -> p h v", h=HH)
                    gdn = lambda v: v.unsqueeze(2).to_broadcast([P, HH, HD])
                    tt(r3, ps[:, 1, 0:HW].rearrange("p (h v) -> p h v", h=HH), gdn(eacs[:, c, d, HS:NDEC]), ALU.mult)
                    r22 = rr[:, :].rearrange("p (a f) -> p a f", a=2)
                    tt(r22, cv[:, 12:14, tk(c)], r22, ALU.subtract)
                    tt(r3, r3, gdn(beta[:, c, d, :]), ALU.mult, "r_ready")
                    wait("ho_ps", u + 1, l)
                    o = yraw[:, c, SW:SW + HW]
                    if first:
                        cp(o, ps[:, 4, 0:HW])
                    else:
                        tt(o, o, ps[:, 4, 0:HW], ALU.add)
                    if last_step:
                        dve.drain().then_inc(S["hgrn_done"], 1)
                    else:
                        tt(tmp[:, 0:2 * P].rearrange("p (t v) -> p t v", t=2), ps[:, 5, 2 * P:4 * P].rearrange("p (t v) -> p t v", t=2),
                           bd[:, :].unsqueeze(1).to_broadcast([P, 2, P]), ALU.mult)
                        for t in range(2):
                            stt(Sh[:, d, t, :], Sh[:, d, t, :], hdec[:, t:t + 1], tmp[:, t * P:(t + 1) * P], ALU.mult, ALU.add)
                        dve.drain().then_inc(S["hgrn_done"], 1)
                    wait("go_ps", u + 1, l)
                    t3 = tmp[:, 0:HW].rearrange("p (h v) -> p h v", h=HH)
                    tt(t3, ps[:, 2, 0:HW].rearrange("p (h v) -> p h v", h=HH), gdn(eacs[:, c, d, HS:NDEC]), ALU.mult)
                    o = yraw[:, c, SW + HW:DM]
                    if first:
                        tt(o, tmp[:, 0:HW], ps[:, 2, HW:2 * HW], ALU.add)
                    else:
                        tt(tmp[:, 0:HW], tmp[:, 0:HW], ps[:, 2, HW:2 * HW], ALU.add)
                        tt(o, o, tmp[:, 0:HW], ALU.add)
                    if not last_step:
                        tt(tmp[:, 0:2 * P].rearrange("p (t v) -> p t v", t=2), ps[:, 3, 0:2 * P].rearrange("p (t v) -> p t v", t=2),
                           bd[:, :].unsqueeze(1).to_broadcast([P, 2, P]), ALU.mult)
                        for t in range(2):
                            stt(Sg[:, d, t, :], Sg[:, d, t, :], dcol[:, 2 * c + d, t:t + 1], tmp[:, t * P:(t + 1) * P], ALU.mult, ALU.add)
                    dve.drain().then_inc(S["gdn_done"], 1)
                for c in range(NT):
                    tt(yraw[:, c, 0:SW], yraw[:, c, 0:SW], gates[:, c, 0:SW], ALU.mult)
                    tt(sqo[:, 0, :], yraw[:, c, :], yraw[:, c, :], ALU.mult)
                    do(V.tensor_reduce(ssq[:, c, 0:2], sqo[:, 0, 0:SW].rearrange("p (g f) -> p g f", g=2), AX.X, ALU.add))
                    do(V.tensor_reduce(ssq[:, c, 2:10], sqo[:, 0, SW:DM].rearrange("p (g f) -> p g f", g=8), AX.X, ALU.add))
                dve.drain().then_inc(S["y_sq"], 1)
                wait("nrow_loaded", 16 * NROW_DMAS, l)
                for base in (SW, SW + HW):
                    cp(nrow[:, base + HD:base + 2 * HD], nrow[:, base:base + HD])
                    cp(nrow[:, base + 2 * HD:base + 4 * HD], nrow[:, base:base + 2 * HD])
                wait("y_rstd", 1, l)
                for c in range(NT):
                    y = yraw[:, c, :]
                    v2 = y[:, 0:SW].rearrange("p (g f) -> p g f", g=2)
                    tt(v2, v2, ssq[:, c, 0:2].unsqueeze(2).to_broadcast([P, 2, HW]), ALU.mult)
                    v8_ = y[:, SW:DM].rearrange("p (g f) -> p g f", g=8)
                    tt(v8_, v8_, ssq[:, c, 2:10].unsqueeze(2).to_broadcast([P, 8, HD]), ALU.mult)
                    tt(y, y, nrow, ALU.mult)
                    tt(y[:, SW:DM], y[:, SW:DM], gates[:, c, SW:DM], ALU.mult, "y_ready")
                wait("grow_sb", 2, l)
                for n in range(N_OUT):
                    wait("wo_ps", n + 1, l)
                    b0 = 4 + 2 * (n % 2)
                    cols = slice(n * BW, (n + 1) * BW)
                    for j in range(2):
                        o = X[:, 0, 0:2 * BW].rearrange("p (c f) -> p c f", c=2)
                        tt(o, ps[:, b0 + j, :].rearrange("p (c f) -> p c f", c=2), grow[:, j, cols].unsqueeze(1).to_broadcast([P, 2, BW]), ALU.mult)
                        tt(h[:, 2 * j:2 * j + 2, cols], h[:, 2 * j:2 * j + 2, cols], o, ALU.add, "wo_sb" if j else None)
                norm_turn(1, l)
                for c in range(NT):
                    wait("ftok_ps", c + 1, l)
                    if c >= 2:
                        wait(f"x_stored{c % 2}", 16 * (c // 2), l)
                    cp(X[:, c % 2, :], bank(4 + 2 * (c % 2), 2), "ftok_sb")
                wait("lg_exp", 1, l)
                do(V.memset(blank[:, :, 1:2], 0.0))
                do(V.memset(blank[:, :, 0:1].bitcast(I32), SKIP), "blank_ready")
                ts(scor[:, :, :], scor[:, :, :], 1.0, None, ALU.add)
                do(V.reciprocal(scor[:, :, :], scor[:, :, :]))
                tt(sel[:, :, :], scor[:, :, :], rbias[:, :].unsqueeze(1).to_broadcast([P, NT, NE]), ALU.add)
                for c in range(NT):
                    do(V.max(v8[:, c, :], sel[:, c, :]))
                    do(V.max_index(i8[:, c, :], v8[:, c, :], sel[:, c, :]))
                cp(if8[:, :, :], i8[:, :, :])
                eight = lambda ap: ap.unsqueeze(1).to_broadcast([P, TOPK, NE])
                for c in range(NT):
                    hv = hots[:, c, :].rearrange("p (k e) -> p k e", k=TOPK)
                    tt(hv, eight(iota_e[:, :]), if8[:, c, :].unsqueeze(2).to_broadcast([P, TOPK, NE]), ALU.is_equal)
                    do(V.tensor_reduce(mask[:, c, :], hots[:, c, :].rearrange("p (k e) -> p e k", k=TOPK), AX.X, ALU.add))
                cp(lcur[:, :], live[:, L1, :].rearrange("p o c -> p (o c)"))
                tt(mask[:, :, :], mask[:, :, :], lcur[:, :].unsqueeze(2).to_broadcast([P, NT, NE]), ALU.mult)
                ts(lcur[:, :], lcur[:, :], -float(SKIP), float(SKIP), ALU.mult, ALU.add)
                dve.drain().then_inc(S["mask_ready"], 1)
                for c in range(NT):
                    hv = hots[:, c, :].rearrange("p (k e) -> p k e", k=TOPK)
                    tt(hot2[:, :, :], hv, eight(scor[:, c, :]), ALU.mult)
                    do(V.tensor_reduce(s8[:, c, :], hot2[:, :, :], AX.X, ALU.add))
                do(V.tensor_reduce(gsum[:, :], s8[:, :, :], AX.X, ALU.add))
                do(V.reciprocal(gsum[:, :], gsum[:, :]))
                tt(s8[:, :, :], s8[:, :, :], gsum[:, :].unsqueeze(2).to_broadcast([P, NT, TOPK]), ALU.mult)
                ts(pay[:, :, 1], s8[:, :, :].rearrange("p c k -> p (c k)"), ROUTED_SCALE, None, ALU.mult)
                cp(pay[:, :, 0].bitcast(I32).rearrange("p (c k) -> p c k", c=NT), tokid[:, :].unsqueeze(2).to_broadcast([P, NT, TOPK]))
                wait("pos_ps", 1, l)
                cp(pos[:, :, :].rearrange("p c e -> p (c e)"), ps[:, 7, 0:NT * NE])
                for c in range(NT):
                    hv = hots[:, c, :].rearrange("p (k e) -> p k e", k=TOPK)
                    tt(hot2[:, :, :], hv, eight(pos[:, c, :]), ALU.mult)
                    do(V.tensor_reduce(p8[:, c, :], hot2[:, :, :], AX.X, ALU.add))
                stt(dst8[:, :, :], p8[:, :, :], float(NE), if8[:, :, :], ALU.mult, ALU.add)
                tt(dst8[:, :, :], dst8[:, :, :], lcur[:, :].unsqueeze(2).to_broadcast([P, NT, TOPK]), ALU.add)
                cp(dsti[:, :, 0], dst8[:, :, :].rearrange("p c k -> p (c k)"), "pay_ready")
                for b in range(NBLK):
                    ts(moref[:, b, :], ps[0:1, 7, NT * NE:(NT + 1) * NE], float(P * b if b else HD), None, ALU.is_gt)
                do(V.tensor_copy(more[:, :], moref[:, :, :].rearrange("p b e -> p (b e)")))
                do(V.tensor_reduce(flag[0:1, 0:1], ps[0:1, 7, NT * NE:(NT + 1) * NE], AX.X, ALU.max))
                ts(flag[0:1, 1:2], flag[0:1, 0:1], float(P), None, ALU.is_gt)
                do(V.tensor_copy(flagi[0:1, 0:1], flag[0:1, 1:2]), "flag_ready")
                wait("sh_silu", 1, l)
                wait("sh_ps", 2, l)
                tt(hsh[:, :, :], sgT[:, :, :], ps[:, 2:4, :], ALU.mult, "sh_mul")
                for c in range(NT):
                    wait("shd_ps", c + 1, l)
                    wait(f"x_stored{c % 2}", 32 if c < 2 else 48, l)
                    cp(X[:, c % 2, :], bank(4 + 2 * (c % 2), 2), "shd_sb")

                def x_half(e, b):
                    dve.wait_ge(S["xt_ps"], e + 1)
                    cp(xgT[b][:, 4:8, :].rearrange("p k t -> p (k t)"), ps[:, 1, :], "xt_sb")

                def gate_up(e, b):
                    dve.wait_ge(S["gu_silu"], e + 1)
                    tt(hTe[b].rearrange("p k t -> p (k t)"), sg[b].rearrange("p k t -> p (k t)"), ps[:, 2 + b, ED:2 * ED], ALU.mult, "gu_mul")

                def slots_of(idx, e, name):
                    at_ = slice(e, e + 1) if isinstance(e, int) else bass.ds(e, 1)
                    cp(idx[:, :].bitcast(I32), tabA[:, at_, :].rearrange("p a t -> p (a t)").bitcast(I32), name)

                def dve_step(i, s, ahead):
                    e = l * NE + i * NSLOT + s
                    if ahead > NSLOT:
                        slots_of(idxG[s], i * NSLOT + (s + NSLOT), "idx_in")
                    if ahead > 1:
                        gate_up(e + 1, (s + 1) % 2)
                    if ahead > 2:
                        x_half(e + 2, s % 2)
                    if not (isinstance(i, int) and i == 0 and s < 2):
                        dve.wait_ge(S[f"scattered{s % 2}"], l * (8 * NE) + i * 32 + (s // 2) * 16)
                    if ahead > 2:
                        dve.sem_inc(S["past"], 1)
                        slots_of(idxS[(s + 2) % NSLOT], i * NSLOT + (s + 2), "idx_out")
                    dve.wait_ge(S["dn_ps"], e + 1)
                    ts(oe[s % 2][:, 512:DM], ps[:, 5 + 2 * (s % 2), :], idxS[s][:, 1:2], None, ALU.mult, name="oe_dve")

                wait("tab_loaded", 16, l)
                for s in range(NSLOT):
                    slots_of(idxG[s], s, "idx_in")
                for s in range(2):
                    slots_of(idxS[s], s, "idx_out")
                x_half(l * NE, 0)
                gate_up(l * NE, 0)
                x_half(l * NE + 1, 1)
                for s in range(NSLOT):
                    dve_step(0, s, NSLOT + 1)
                with dve.Fori(1, NE // NSLOT - 1) as i:
                    for s in range(NSLOT):
                        dve_step(i, s, NSLOT + 1)
                for s in range(NSLOT):
                    dve_step(NE // NSLOT - 1, s, NSLOT - s)
                over = dve.value_load(flagi[0:1, 0:1], min_val=0, max_val=1)
                with dve.If(over > 0):
                    with dve.Fori(0, OVER) as n_:
                        n = l * OVER + n_
                        need = dve.value_load(more[0:1, bass.ds(n_ + NE, 1)], min_val=0, max_val=1)
                        with dve.If(need > 0):
                            dve.wait_ge(S["ov_xt"], n + 1)
                            cp(xgT[0].rearrange("p k t -> p (k t)"), bank(0, 2), "ov_xs")
                            dve.wait_ge(S["ov_sl"], n + 1)
                            tt(hTe[0].rearrange("p k t -> p (k t)"), sg[0].rearrange("p k t -> p (k t)"), ps[:, 2, ED:2 * ED], ALU.mult, "ov_mu")
                            dve.wait_ge(S["ov_dn"], n + 1)
                            ts(oe[0], bank(4, 2), idxS[0][:, 1:2], None, ALU.mult, name="ov_oe")
                        with dve.Else():
                            for name in ("ov_xs", "ov_mu", "ov_oe"):
                                dve.sem_inc(S[name], 1)
                with dve.Else():
                    for name in ("ov_xs", "ov_mu", "ov_oe"):
                        dve.sem_inc(S[name], OVER)
                wait("gf_ps", 1, l)
                wait("odd_loaded", 16, l)
                for c in range(NT):
                    wait(f"acc_loaded{c % 2}", 16 * (c // 2 + 1), l)
                    tt(X[:, c % 2, :], X[:, c % 2, :], yraw[:, c, :], ALU.add)
                    tt(X[:, c % 2, :], X[:, c % 2, :], bank(2 * (c // 2), 2), ALU.mult)
                    tt(h[:, c, :], h[:, c, :], X[:, c % 2, :], ALU.add, "acc_added")
                dve.drain().then_inc(S["h_ready"], 1)
            for c in range(2):
                V.tensor_tensor_reduce(out=X[:, c, :], in0=h[:, 2 + c, :], in1=h[:, 2 + c, :], scale=1.0, scalar=0.0,
                                       op0=ALU.mult, op1=ALU.add, accum_out=st[:, c:c + 1])
                dve.drain()
            dve.drain().then_inc(S["sumsq"], 1)
            wait("rstd", 1, DEPTH)
            dve.wait_ge(S["out_loaded"], 16)
            for c in range(2):
                ts(X[:, c, :], h[:, 2 + c, :], st[:, 8 + c:9 + c], None, ALU.mult)
                tt(X[:, c, :], X[:, c, :], grow[:, 0, :], ALU.mult, "out_ready")


        @block.tensor
        def _(pe):
            MM = nc.tensor.matmul

            def wait(name, n, l):
                pe.wait_ge(S[name], l * PER[name] + n)

            def mm(out_, lhsT, rhs, start=True, stop=True):
                return MM(out_, lhsT, rhs, start=start, stop=stop)

            def turn(out_, in_):
                k = in_.shape[0]
                return nc.tensor.transpose(out_, in_, ident[0:k, 0:k])

            def column(ap):
                return ap.to_broadcast([P, P])

            def ring_wait(m, l):
                pe.wait_ge(S[f"ring_full{m % 2}"], l * (16 * RING // 2) + 16 * (m // 2 + 1))

            W_MOD = 16 * N_MOD // NSLOT

            pe.wait_ge(S["const_ready"], 1)
            pe.wait_ge(S["head_loaded"], 16 * 5)
            turn(ps[:, 0, 0:2 * KT], stage[0:2 * KT, 0, :])
            turn(ps[:, 3, 0:4], stage[0:4, 1, :]).then_inc(S["cond_ps"], 1)

            def norm_turn(q, l):
                for c in range(NT):
                    wait("xn", q * NT + c + 1, l)
                    if c >= 2:
                        wait("feat_d", q * NT + c - 1, l)
                        wait("feat_a", q * NT + c - 1, l)
                    for k in range(KT):
                        ins = turn(bank(4 + 2 * (c % 2), 2)[:, tk(k)], X[:, c % 2, tk(k)])
                    ins.then_inc(S["xT_ps"], 1)

            with pe.Fori(0, DEPTH) as l:
                wait("h_ready", 1, l)
                wait("prm_loaded", 16 * PRM_DMAS, l)
                pe.sem_inc(S["past"], 1)
                turn(ps[:, 1, 0:64], stage[0:64, 0, :])
                turn(ps[:, 1, 64:N_PRM], stage[0:N_PRM - 64, 1, :]).then_inc(S["prm_ps"], 1)
                with pe.Fori(0, N_MOD // NSLOT) as i:
                    def mod_turn(s):
                        pe.wait_ge(S["mod_row"], l * N_MOD + i * NSLOT + (s + 1))
                        pe.sem_inc(S["past"], 1)
                        for q in range(MW // P):
                            mm(ps[:, 2, bass.ds(i * (NSLOT * 8) + (s * 8 + q * 2), 2)], X[0:2, s % 2, tk(q)], ident[0:2, 0:2])

                    for s in range(NSLOT):
                        pe.wait_ge(S[f"w{s}"], l * PER["w0"] + i * 16 + 16)
                        for k in range(KT):
                            ins = mm(ps[0:2, 4 + s % 2, :], condT[:, :, k], wgu[s][:, k, :], k == 0, k == KT - 1)
                        ins.then_inc(S["mod_used"], 1)
                        if s:
                            mod_turn(s - 1)
                    mod_turn(NSLOT - 1)
                pe.drain().then_inc(S["mod_ps"], 1)
                wait("mod_sb", 1, l)
                norm_turn(0, l)
                wait("feat_d", NT, l)
                wait("feat_a", NT, l)
                wait("small_loaded", 32, l)
                for c in range(NT):
                    for k in range(KT):
                        ins = mm(ps[:, 3, 32 * c:32 * c + 32], featT[:, k, tk(c)], wsm[:, k, :], k == 0, k == KT - 1)
                ins.then_inc(S["sm_ps"], 1)
                for n, (kind, _, _) in enumerate(IN_BLOCKS):
                    m = n
                    b0 = UB[n % 3]
                    ring_wait(m, l)
                    if n >= 3:
                        wait("u_dve", n - 2, l) if n - 3 < N_CONV else wait("u_act", n - 2 - N_CONV, l)
                    if kind in ("conv", "hq", "hf"):
                        for half in range(2):
                            for k in range(KT):
                                ins = mm(ps[:, b0 + half, :], ring[:, m % 2, k, tk(half)], featT[:, k, :], k == 0, k == KT - 1)
                    else:
                        for c in range(NT):
                            for k in range(KT):
                                ins = mm(bank(b0, 2)[:, c * BW:(c + 1) * BW], featT[:, k, tk(c)], ring[:, m % 2, k, :], k == 0, k == KT - 1)
                    ins.then_inc(S["u_ps"], 1)
                    pe.drain().then_inc(S["ring_used"], 1)
                wait("sp_done", 1, l)
                for d in range(2):
                    mm(ps[:, 2, 48 * d:48 * d + 48], tri[:, d, :], da[:, :, d, :])
                mm(ps[:, 2, 96:192], ones[:, :], da[:, :, :, :].rearrange("p c d h -> p (c d h)")).then_inc(S["cum_ps"], 1)
                wait("u_act", N_IN - N_CONV, l)
                for t in range(4):
                    wait("l2_sq", t + 1, l)
                    if t >= 2:
                        wait("l2_act", t - 1, l)
                    mm(ps[:, t % 2, :], bd[:, :], sqw[:, t % 2, :]).then_inc(S["l2_ps"], 1)
                wait("l2_done", 4, l)
                wait("cum_dve", 1, l)
                wait("silu_out", CT, l)
                for c in range(NT):
                    b0 = 4 * (c % 2)
                    if c >= 2:
                        wait("tok_d", c - 1, l)
                        wait("tok_a", c - 1, l)
                    for t in range(4):
                        turn(ps[:, b0, tk(t)], cv[:, t, tk(c)])
                    for t in range(2):
                        turn(ps[:, b0 + 1, tk(t)], cv[:, 4 + t, tk(c)])
                        turn(ps[:, b0 + 1, HW + t * P:HW + (t + 1) * P], cv[:, 10 + t, tk(c)])
                        ins = turn(ps[:, b0 + 2, tk(t)], cv[:, 12 + t, tk(c)])
                    ins.then_inc(S["tok_ps"], 1)
                wait("small_done", 1, l)
                wait("tok_d", NT, l)
                wait("tok_a", NT, l)
                wait("s_init", 1, l)
                for u, (i, d, c) in enumerate(UNITS):
                    last_step = i == NT - 1
                    if u:
                        wait("gdn_done", u, l)
                        wait("ssd_sb", u, l)
                    for g in range(NG):
                        mm(ps[:, 0, tk(g)], cv[:, 4 + g, tk(c)], cv[:, 6 + g, tk(c)])
                    for par in range(2):
                        rows = slice(par * HD, (par + 1) * HD)
                        for a in range(2):
                            mm(ps[:, 1 + par, tk(a)], cv[rows, 10 + a, tk(c)], cv[rows, 10 + a, tk(c)])
                            mm(ps[:, 1 + par, tk(2 + a)], cv[rows, 10 + a, tk(c)], cv[rows, 8 + a, tk(c)])
                    for j in range(NDEC):
                        mm(ps[:, 3 + j // 4, tk(j % 4)], column(da[:, c, d, j:j + 1]), tri[:, d, :])
                    for j in range(HH):
                        ins = mm(ps[:, 6, tk(j)], column(beta[:, c, d, j:j + 1]), ident[:, :])
                    ins.then_inc(S["pre_ps"], 1)
                    wait("at_ready", u + 1, l)
                    for j in range(LEVELS):
                        wait("nt_ready", u * LEVELS + j + 1, l)
                        wait("t_init", u + 1, l) if j == 0 else wait("t_ready", u * LEVELS + j, l)
                        for q in range(HH):
                            ins = mm(ps[:, 1, tk(q)], NTm[:, q, :], T[:, q, :])
                        ins.then_inc(S["p_ps"], 1)
                        if j < 4:
                            if j == 0:
                                wait("ql_ready", u + 1, l)
                            else:
                                wait("h_cp", u * 4 + j, l)
                            for r in range(2):
                                lv = 2 * j + r
                                for par in range(2):
                                    rows = slice(par * HD, (par + 1) * HD)
                                    for a in range(2):
                                        k_, q_ = (kL[rows, lv, tk(a)], e7[rows, lv, tk(a)]) if lv < LEVELS else \
                                            (hk[rows, d, a, tk(c)], hq[rows, a, tk(c)])
                                        ins = mm(ps[:, 4 + par, tk(2 * r + a)], k_, q_)
                            ins.then_inc(S["h_ps"], 1)
                        if j == 4:
                            wait("h_cp", u * 4 + 4, l)
                            for a in range(2):
                                ins = turn(ps[:, 5, tk(a)], kend[:, tk(a)])
                            ins.then_inc(S["ke_ps"], 1)
                        wait("p_sb", u * LEVELS + j + 1, l)
                        if j < LEVELS - 1:
                            for q in range(HH):
                                mm(ps[:, 2, tk(q)], TT[:, q, :], Pm[:, q, :])
                        for q in range(HH):
                            ins = mm(ps[:, 3, tk(q)], Pm[:, q, :], TT[:, q, :])
                        ins.then_inc(S["q_ps"], 1)
                        if j == 2:
                            wait("att_ready", u + 1, l)
                            for q in range(HS):
                                mm(ps[:, 7, q * HD:(q + 1) * HD], E[:, q, :], cv[:, q // 2, c * P + (q % 2) * HD:c * P + (q % 2 + 1) * HD])
                            for g in range(NG):
                                ins = mm(ps[:, 6, g * HW:(g + 1) * HW], cv[:, 6 + g, tk(c)], Ss[:, d, g, :])
                                if not last_step:
                                    ins = mm(ps[:, 0, g * HW:(g + 1) * HW], Btok[:, c, tk(g)], xw[:, g * HW:(g + 1) * HW])
                            ins.then_inc(S["ssd_ps"], 1)
                    for a in range(2):
                        mm(ps[:, 4, tk(a)], eb[:, tk(a)], Sh[:, d, a, :], True, False)
                        for par in range(2):
                            q = 2 * a + par
                            mm(ps[:, 4, q * HD:(q + 1) * HD], attH[:, q, :], val[:, c, q * HD:(q + 1) * HD], False, par == 1)
                    wait("ke_sb", u + 1, l)
                    for a in range(2):
                        ins = mm(ps[:, 5, tk(2 + a)], kendT[:, tk(a)], val[:, c, tk(a)])
                    ins.then_inc(S["ho_ps"], 1)
                    wait("t_ready", (u + 1) * LEVELS, l)
                    for a in range(2):
                        ins = mm(ps[:, 1, tk(a)], cv[:, 10 + a, tk(c)], Sg[:, d, a, :])
                    ins.then_inc(S["gks_ps"], 1)
                    for a in range(2):
                        mm(ps[:, 2, tk(a)], cv[:, 8 + a, tk(c)], Sg[:, d, a, :])
                    wait("r_ready", u + 1, l)
                    for q in range(HH):
                        ins = mm(ps[:, 1, HW + q * HD:HW + (q + 1) * HD], TT[:, q, :], rr[:, q * HD:(q + 1) * HD])
                    ins.then_inc(S["vn_ps"], 1)
                    wait("vn_sb", u + 1, l)
                    wait("kw_ready", u + 1, l)
                    for q in range(HH):
                        mm(ps[:, 2, HW + q * HD:HW + (q + 1) * HD], E[:, HS + q, :], vn[:, q * HD:(q + 1) * HD])
                    for a in range(2):
                        ins = mm(ps[:, 3, tk(a)], kw[:, tk(a)], vn[:, tk(a)])
                    ins.then_inc(S["go_ps"], 1)
                wait("gdn_done", U, l)
                wait("ssd_sb", U, l)
                def gate_rows(first, name, b0):
                    for j in range(2):
                        for k in range(KT):
                            ins = mm(bank(b0 + 2 * j, 2)[:, tk(k)], column(mod[:, first + k, j:j + 1]), ident[:, :])
                        if name:
                            ins.then_inc(S[name], 1)
                    return ins

                gate_rows(16, "grow_ps", 0)
                for c in range(NT):
                    wait("y_ready", c + 1, l)
                    if c >= 2:
                        wait("yT_sb", c - 1, l)
                    for k in range(KT):
                        ins = turn(bank(4 + 2 * (c % 2), 2)[:, tk(k)], yraw[:, c, tk(k)])
                    ins.then_inc(S["yT_ps"], 1)
                wait("yT_sb", NT, l)
                for n in range(N_OUT):
                    m = N_IN + n
                    ring_wait(m, l)
                    if n >= 2:
                        wait("wo_sb", n - 1, l)
                    for c in range(NT):
                        for k in range(KT):
                            ins = mm(bank(4 + 2 * (n % 2), 2)[:, c * BW:(c + 1) * BW], yT[:, k, tk(c)], ring[:, m % 2, k, :], k == 0, k == KT - 1)
                    ins.then_inc(S["wo_ps"], 1)
                    pe.drain().then_inc(S["ring_used"], 1)
                norm_turn(1, l)
                wait("feat_d", 2 * NT, l)
                wait("feat_a", 2 * NT, l)
                for c in range(NT):
                    if c >= 2:
                        wait("ftok_sb", c - 1, l)
                    for k in range(KT):
                        ins = turn(bank(4 + 2 * (c % 2), 2)[:, tk(k)], featT[:, k, tk(c)])
                    ins.then_inc(S["ftok_ps"], 1)
                wait("rw_loaded", 16, l)
                wait("grow_sb", 2, l)
                for c in range(NT):
                    for k in range(KT):
                        ins = mm(ps[:, 0, c * NE:(c + 1) * NE], featT[:, k, tk(c)], rw[:, k, :], k == 0, k == KT - 1)
                ins.then_inc(S["lg_ps"], 1)
                wait("ftok_sb", NT, l)
                wait("lg_exp", 1, l)
                for n in range(2):
                    m = N_IN + N_OUT + n
                    ring_wait(m, l)
                    for half in range(2):
                        for k in range(KT):
                            ins = mm(ps[:, 2 * n + half, :], ring[:, m % 2, k, tk(half)], featT[:, k, :], k == 0, k == KT - 1)
                    ins.then_inc(S["sh_ps"], 1)
                    pe.drain().then_inc(S["ring_used"], 1)
                wait("mask_ready", 1, l)
                for c in range(NT + 1):
                    for c2 in range(min(c + 1, NT)):
                        w = triS if c2 == c else ones
                        ins = mm(ps[:, 7, c * NE:(c + 1) * NE], w[:, :], mask[:, c2, :], c2 == 0, c2 == min(c, NT - 1))
                ins.then_inc(S["pos_ps"], 1)
                m = N_IN + N_OUT + 2
                wait("sh_mul", 1, l)
                wait("flag_ready", 1, l)
                ring_wait(m, l)
                down = ring[:, m % 2, :, :].rearrange("p (a b) n -> p a (b n)", a=2)
                for c in range(NT):
                    if c:
                        wait("shd_sb", c - 1, l) if c > 1 else None
                    for half in range(2):
                        for k in range(2):
                            ins = mm(ps[:, 4 + 2 * (c % 2) + half, :], hsh[:, k, tk(c)], down[:, k, half * 512:(half + 1) * 512], k == 0, k == 1)
                    ins.then_inc(S["shd_ps"], 1)
                pe.drain().then_inc(S["ring_used"], 1)
                wait("shd_sb", NT, l)

                def rows_T(s, n):
                    pe.wait_ge(S[f"gathered{s}"], n)
                    for k in range(KT):
                        ins = turn(bank(0, 2)[:, tk(k)], xg[s][:, tk(k)])
                    ins.then_inc(S["xt_ps"], 1)

                def gate_up_T(b, s, n):
                    for q in range(4):
                        for k in range(KT):
                            ins = mm(ps[:, 2 + b, q * P:q * P + n], wgu[s][:, k, tk(q)], xgT[b][:, k, 0:n], k == 0, k == KT - 1)
                    return ins

                def gate_up(e, at_, s, ws):
                    b = s % 2
                    pe.wait_ge(S["xt_sb"], e * 2 + 2)
                    pe.wait_ge(S[f"w{s}"], ws)
                    pe.sem_inc(S["past"], 1)
                    wide = pe.value_load(more[0:1, at_], min_val=0, max_val=1)
                    with pe.If(wide > 0):
                        gate_up_T(b, s, P).then_inc(S["gu_ps"], 1)
                    with pe.Else():
                        gate_up_T(b, s, HD).then_inc(S["gu_ps"], 1)

                def pe_step(i, s, ahead):
                    e = l * NE + i * NSLOT + s
                    weights = l * PER["w0"] + i * 48 + (W_MOD + 48)
                    if ahead > 1:
                        j = i * NSLOT + s + 1
                        gate_up(e + 1, slice(j, j + 1) if isinstance(i, int) else bass.ds(j, 1), (s + 1) % NSLOT,
                                weights if s < NSLOT - 1 else weights + 48)
                    if ahead > 2:
                        rows_T((s + 2) % NSLOT, l * (4 * NE) + i * 16 + (16 if s < 2 else 32))
                    pe.wait_ge(S["gu_mul"], e + 1)
                    if not (isinstance(i, int) and i == 0 and s < 2):
                        pe.wait_ge(S["oe_act"], e - 1)
                        pe.wait_ge(S["oe_dve"], e - 1)
                    for half in range(2):
                        for k in range(2):
                            ins = mm(ps[:, 4 + 2 * (s % 2) + half, :], hTe[s % 2][:, k, :], wdn[s][:, k, half * 512:(half + 1) * 512], k == 0, k == 1)
                    ins.then_inc(S["dn_ps"], 1)

                wait("xg_init", 1, l)
                rows_T(0, l * (4 * NE) + 16)
                gate_up(l * NE, slice(0, 1), 0, l * PER["w0"] + W_MOD + 48)
                rows_T(1, l * (4 * NE) + 16)
                for s in range(NSLOT):
                    pe_step(0, s, NSLOT + 1)
                with pe.Fori(1, NE // NSLOT - 1) as i:
                    for s in range(NSLOT):
                        pe_step(i, s, NSLOT + 1)
                for s in range(NSLOT):
                    pe_step(NE // NSLOT - 1, s, NSLOT - s)
                wait("oe_act", NE, l)
                wait("oe_dve", NE, l)
                pe.sem_inc(S["past"], 1)
                over = pe.value_load(flagi[0:1, 0:1], min_val=0, max_val=1)
                with pe.If(over > 0):
                    with pe.Fori(0, OVER) as n_:
                        n = l * OVER + n_
                        need = pe.value_load(more[0:1, bass.ds(n_ + NE, 1)], min_val=0, max_val=1)
                        with pe.If(need > 0):
                            pe.wait_ge(S["ov_g"], n + 1)
                            for k in range(KT):
                                ins = turn(bank(0, 2)[:, tk(k)], xg[0][:, tk(k)])
                            ins.then_inc(S["ov_xt"], 1)
                            pe.wait_ge(S["ov_xs"], n + 1)
                            pe.wait_ge(S["ov_w"], n * 48 + 48)
                            gate_up_T(0, 0, P).then_inc(S["ov_gu"], 1)
                            pe.wait_ge(S["ov_mu"], n + 1)
                            for half in range(2):
                                for k in range(2):
                                    ins = mm(ps[:, 4 + half, :], hTe[0][:, k, :], wdn[0][:, k, half * 512:(half + 1) * 512], k == 0, k == 1)
                            ins.then_inc(S["ov_dn"], 1)
                        with pe.Else():
                            for name in ("ov_xt", "ov_gu", "ov_dn"):
                                pe.sem_inc(S[name], 1)
                with pe.Else():
                    for name in ("ov_xt", "ov_gu", "ov_dn"):
                        pe.sem_inc(S[name], OVER)
                pe.wait_ge(S["ov_oe"], l * OVER + OVER)
                gate_rows(40, None, 0).then_inc(S["gf_ps"], 1)


_INS = ["x", "c", "ctx", "c_ctx", "w_mod", "b_mod", "norm_mix", "w_in", "ssd_conv_w", "ssd_conv_b", "ssd_dt_bias",
        "ssd_a_log", "ssd_d", "ssd_norm", "hgrn_lb", "hgrn_norm", "gdn_conv_w", "gdn_dt_bias", "gdn_a_log", "gdn_norm",
        "w_out", "norm_ffn", "router_w", "router_bias", "exp_gate", "exp_up", "exp_down", "sh_gate", "sh_up", "sh_down",
        "norm_final"]


def kernel(**inputs):
    import concourse.bacc as bacc
    from concourse.bass_utils import run_bass_kernel_spmd

    nc = bacc.Bacc("TRN2", target_bir_lowering=False, num_devices=1)
    arrays, A = {}, {}
    for name in _INS:
        a = np.ascontiguousarray(inputs[name])
        arrays[f"in_{name}"] = a
        A[name] = nc.dram_tensor(f"in_{name}", a.shape, mybir.dt.from_np(a.dtype), kind="ExternalInput").ap()
    out = nc.dram_tensor("out", (1, SEQ, DM), F32, kind="ExternalOutput").ap()
    scratch = (nc.dram_tensor("ffn_rows", (TOK, DM), F32, kind="Internal").ap(),
               nc.dram_tensor("ffn_sum_even", (TOK, DM), F32, kind="Internal").ap(),
               nc.dram_tensor("ffn_sum_odd", (TOK, DM), F32, kind="Internal").ap(),
               nc.dram_tensor("slots", (CAP, NE, 2), F32, kind="Internal").ap())
    build(nc, A, out, scratch)
    r = run_bass_kernel_spmd(nc, [arrays], core_ids=[0])
    return r.results[0]["out"]
```

```python
import math
from contextlib import ExitStack

import numpy as np

import concourse.bass as bass
from concourse import mybir

F32 = mybir.dt.float32
I32 = mybir.dt.int32
U32 = mybir.dt.uint32
ALU = mybir.AluOpType
ACT = mybir.ActivationFunctionType
AX = mybir.AxisListType

P = 128
DEPTH = 2
DM = 1024
KT = DM // P
CTX = 256
SEQ = 256
TOK = CTX + SEQ
NT = TOK // P
GRID_W = 64
ROWS = SEQ // GRID_W
TAPS = 5
HALF = TAPS // 2
EPS = 1e-6

HS, NG, NSTATE = 8, 2, 128
HH = 4
HD = 64
SW = HS * HD
HW = HH * HD
NDEC = HS + HH
SSD_IN = SW + SW + 2 * NG * NSTATE + 2 * HS
HGRN_IN = 5 * HW
GDN_IN = 3 * HW + 4 * HH + HW
COL_HGRN = SSD_IN
COL_GDN = SSD_IN + HGRN_IN
CT = 14
LEVELS = 7
NE, TOPK, ED = 64, 8, 256
ROUTED_SCALE = 2.5
CAP = TOK
NBLK = CAP // P
NSLOT = 4
BW = 256
RSIZE = 33700
NEG = -1e30
SKIP = 1 << 20

CPAD = CTX + 2 * HALF
RPAD = GRID_W + 2 * HALF
LINE = CPAD + ROWS * RPAD
CONV = LINE - 2 * HALF

IN_BLOCKS = (
    [("conv", SW + BW * i, i) for i in range(4)]
    + [("conv", COL_GDN + BW * i, 4 + i) for i in range(3)]
    + [("hf", COL_HGRN + HW, 0), ("hf", COL_HGRN + 2 * HW, 1), ("hq", COL_HGRN, 0), ("val", COL_HGRN + 3 * HW, 0)]
    + [("gate", 0, 0), ("gate", BW, 1), ("gate", COL_HGRN + 4 * HW, 2), ("gate", COL_GDN + 3 * HW + 4 * HH, 3)]
)
N_CONV = 7
N_IN = len(IN_BLOCKS)
MW = 512
N_MOD = 6 * DM // MW
N_OUT = DM // BW
RING = N_IN + N_OUT + 3

R_BMOD, R_NMIX, R_NFFN = 0, 48, 56
R_CWS, R_CBS, R_CWG = 64, 104, 112
N_PRM = 142

UB = (0, 4, 6)
PRM_DMAS = 12
NROW_DMAS = 3
OVER = (NBLK - 1) * NE

ORDER = ((0, 1, 2, 3), (1, 0, 3, 2))
UNITS = [(i, d, ORDER[d][i]) for i in range(NT) for d in range(2)]
SEEN = {}
for _n, (_i, _d, _c) in enumerate(UNITS):
    SEEN.setdefault(_c, _n)


def late(ap, w, d):
    half = slice(w // 2, w) if d == 0 else slice(0, w // 2)
    return ap.rearrange("p t (n w) -> p t n w", w=w)[:, :, :, half]


def early(ap, w, d):
    return late(ap, w, 1 - d)


def line_rows(ap):
    return ap[:, CPAD:CPAD + (ROWS - 1) * RPAD + RPAD].rearrange("p (r x) -> p r x", r=ROWS)[:, :, 0:GRID_W]


def build(nc, A, out, scratch):
    f_dram, acc_dram, acc_odd, tab_dram = scratch
    with ExitStack() as ctx:
        def sb(name, shape, dt=F32):
            return ctx.enter_context(nc.sbuf_tensor(name, shape, dt))

        def sem(name):
            return ctx.enter_context(nc.semaphore(name))

        h = sb("h", [P, NT, DM])
        featT = sb("featT", [P, KT, TOK])
        yraw = featT[:, :, :].rearrange("p k t -> p (k t)").rearrange("p (c f) -> p c f", c=NT)
        X = sb("X", [P, 2, DM])
        ring = sb("ring", [P, 2, KT, BW])
        ident = sb("ident", [P, P])
        tri = sb("tri", [P, 2, P])
        negm = sb("negm", [P, 2, P])
        triS = sb("triS", [P, P])
        ones = sb("ones", [P, P])
        bd = sb("bd", [P, P])
        lev = sb("lev", [P, 2, LEVELS, P])
        iota_e = sb("iota_e", [P, NE])
        tokid = sb("tokid", [P, NT], I32)
        cst = sb("cst", [P, 4])
        condT = sb("condT", [P, 2, KT])
        stage = sb("stage", [P, 2, P])
        prm = sb("prm", [P, N_PRM])
        low = sb("low", [P, DEPTH, 2])
        lowv = sb("lowv", [P, 3, 2])
        mod = sb("mod", [P, 48, 2])
        amul = sb("amul", [P, 2, KT, 2])
        nrow = X[:, 1, :]
        dtb = sb("dtb", [P, 2, NDEC])
        alog = sb("alog", [P, 2, NDEC])
        nega = sb("nega", [P, 2, NDEC])
        dsk = sb("dsk", [P, HS])
        rbias = sb("rbias", [P, NE])
        wsm = sb("wsm", [P, KT, 32])
        rw = sb("rw", [P, KT, NE])
        st = sb("st", [P, 16])
        live = sb("live", [P, DEPTH, NT])
        lcur = sb("lcur", [P, NT])
        hdec = sb("hdec", [P, 2])
        ssq = sb("ssq", [P, NT, 10])
        R = sb("R", [P, RSIZE])
        at = [0]

        def cut(*shape):
            n = math.prod(shape)
            v = R[:, at[0]:at[0] + n]
            at[0] += n
            if len(shape) == 2:
                v = v.rearrange("p (a b) -> p a b", a=shape[0])
            if len(shape) == 3:
                v = v.rearrange("p (a b c) -> p a b c", a=shape[0], b=shape[1])
            return v

        cv = cut(CT, TOK)
        hq = cut(2, TOK)
        logf = cut(2, 2, TOK)
        hk = cut(2, 2, TOK)
        gates = cut(NT, DM)
        val = cut(NT, HW)
        Btok = cut(NT, NG * NSTATE)
        Ktok = cut(NT, HW)
        wk = at[0]
        line = cut(2, LINE)
        cvo = cut(2, LINE)
        hwt = cut(2 * 2, TOK)
        hwx = cut(2 * 2, TOK)
        lnw = cut(TOK)
        lnx = cut(TOK)
        sqw = cut(2, TOK)
        sm = cut(NT, 32)
        spw = cut(4, NT * 2 * NDEC)
        at[0] = wk
        E = cut(NDEC, P)
        AT = cut(HH, P)
        NTm = cut(2, HH, P)
        W = cut(2, 4, P)
        Pm = cut(HH, P)
        e7 = cut(LEVELS, 2 * P)
        bh = cut(2 * P)
        eb = cut(2 * P)
        e1 = cut(2 * P)
        kend = cut(2 * P)
        kendT = cut(2 * P)
        attH = cut(HH, P)
        xw = cut(SW)
        rr = cut(HW)
        vn = cut(HW)
        kw = cut(HW)
        tmp = cut(SW)
        Ss = cut(2, NG, SW // NG)
        Sh = cut(2, 2, P)
        Sg = cut(2, 2, P)
        wdt = cut(NT, 2, NDEC)
        dt_ = cut(NT, 2, NDEC)
        da = cut(NT, 2, NDEC)
        acs = cut(NT, 2, NDEC)
        eacs = cut(NT, 2, NDEC)
        wend = cut(NT, 2, NDEC)
        etot = cut(NT, 2, NDEC)
        beta = cut(NT, 2, HH)
        dcol = cut(NT * 2, 2)
        assert at[0] <= RSIZE
        levt = e7[:, 0:1, :].bitcast(I32).rearrange("p a (b t) -> p (a b) t", b=2)
        at[0] = 0
        yT = cut(KT, TOK)
        sqo = cut(2, DM)
        grow = cut(2, DM)
        at[0] = 0
        wgu, wdn = [], []
        for _ in range(NSLOT):
            wgu.append(cut(KT, 2 * ED))
            wdn.append(cut(2, DM))
        ex = at[0]
        xg = [yraw[:, s, :] for s in range(NSLOT)]
        xgT = [cut(KT, P) for _ in range(2)]
        oe = [cut(DM) for _ in range(2)]
        sg = [cut(2, P) for _ in range(2)]
        hTe = [cut(2, P) for _ in range(2)]
        tabA = cut(NE, 2)
        sums = R[:, ex:ex + NT * DM].rearrange("p (c f) -> p c f", c=NT)
        assert at[0] <= RSIZE
        at[0] = ex
        scor = cut(NT, NE)
        sel = cut(NT, NE)
        mask = cut(NT, NE)
        pos = cut(NT, NE)
        hot2 = cut(TOPK, NE)
        hots = cut(NT, TOPK * NE)
        v8 = cut(NT, TOPK)
        i8 = cut(NT, TOPK).bitcast(U32)
        if8 = cut(NT, TOPK)
        s8 = cut(NT, TOPK)
        p8 = cut(NT, TOPK)
        dst8 = cut(NT, TOPK)
        dsti = cut(NT * TOPK, 1).bitcast(I32)
        pay = cut(NT * TOPK, 2)
        gsum = cut(NT)
        blank = cut(CAP * NE // P, 2)
        sgT = cut(2, TOK)
        hsh = cut(2, TOK)
        idxG = [sb(f"idx_in{i}", [P, 2]) for i in range(NSLOT)]
        idxS = [sb(f"idx_out{i}", [P, 2]) for i in range(NSLOT)]
        flag = sb("flag", [1, 4])
        flagi = sb("flagi", [1, 2], I32)
        moref = sb("moref", [1, NBLK, NE])
        more = sb("more", [1, NBLK * NE], I32)
        zero = sb("zero", [P, P])

        ps = ctx.enter_context(nc.psum_tensor("ps", [P, 8, 512], F32))


        PER = {}

        def signal(name, per_layer=0):
            PER[name] = per_layer
            S[name] = sem(name)

        S = {}
        for name in ("const_pool", "const_ready", "head_loaded", "cond_ps", "cond_sb",
                     "past", "ov_dma", "out_ready", "out_stored"):
            signal(name)
        U = len(UNITS)
        for name, n in (
            ("h_ready", 1), ("prm_loaded", 16 * PRM_DMAS), ("prm_ps", 1), ("small_loaded", 32), ("rw_loaded", 16),
            ("ring_full0", 16 * RING // 2), ("ring_full1", 16 * RING // 2), ("ring_used", RING),
            ("mod_used", N_MOD), ("mod_row", N_MOD), ("mod_ps", 1), ("mod_sb", 1),
            ("sumsq", 2), ("rstd", 2), ("xn", 2 * NT), ("xT_ps", 2 * NT), ("feat_d", 2 * NT), ("feat_a", 2 * NT),
            ("u_ps", N_IN), ("u_dve", N_CONV), ("u_act", N_IN - N_CONV), ("conv_out", CT), ("silu_out", CT),
            ("sm_ps", 1), ("sp_x", 1), ("sp_exp", 1), ("sp_done", 1), ("cum_ps", 1), ("cum_dve", 1),
            ("cum_act", 1), ("small_done", 1),
            ("l2_sq", 4), ("l2_ps", 4), ("l2_act", 4), ("l2_done", 4),
            ("low_c", 1), ("lowl", 1), ("hg_b", 1), ("hg_c", 1), ("hg_d", 1), ("hg_e", 1), ("hg_f", 1),
            ("tok_ps", NT), ("tok_d", NT), ("tok_a", NT), ("s_init", 1),
            ("pre_ps", U), ("ssd_pre", U), ("dm_gdn", U), ("e_gdn", U), ("dm_ssd", U), ("e_ssd", U), ("cb_ps", U), ("b_ready", U), ("hexp", U), ("eb_ready", U), ("kl_ready", U),
            ("ql_ready", U), ("a_init", U), ("kw_ready", U), ("at_ready", U), ("att_ready", U),
            ("ssd_ps", U), ("ssd_sb", U), ("nt_ready", U * LEVELS), ("p_ps", 2 * U * LEVELS), ("p_sb", 2 * U * (LEVELS - 1)),
            ("q_ps", 2 * U * (LEVELS - 1)), ("t_ready", 2 * U * LEVELS), ("h_ps", U * 4), ("h_cp", U * 4),
            ("ke_ps", U), ("ke_sb", U), ("ho_ps", U), ("hgrn_done", U),
            ("gks_ps", U), ("r_ready", U), ("vn_ps", U), ("vn_sb", U), ("go_ps", U), ("gdn_done", U),
            ("nrow_loaded", 16 * NROW_DMAS), ("y_sq", 1), ("y_rstd", 1), ("y_ready", NT), ("yT_ps", NT), ("yT_sb", NT),
            ("grow_ps", 2), ("grow_sb", 2), ("wo_ps", N_OUT), ("wo_sb", N_OUT),
            ("ftok_ps", NT), ("ftok_sb", NT), ("x_stored0", 64), ("x_stored1", 64), ("lg_ps", 1), ("lg_exp", 1),
            ("mask_ready", 1), ("pos_ps", 1), ("blank_ready", 1), ("blank_dram", 16), ("pay_ready", 1),
            ("tab_dram", 16 * NT * TOPK), ("tab_loaded", 16), ("flag_ready", 1),
            ("sh_ps", 2), ("sh_silu", 1), ("sh_mul", 1), ("shd_ps", NT), ("shd_sb", NT), ("acc_zeroed", 16 * NT),
            ("w0", 0), ("w1", 0), ("w2", 0), ("w3", 0),
            ("gathered0", 4 * NE), ("gathered1", 4 * NE), ("gathered2", 4 * NE), ("gathered3", 4 * NE), ("xt_ps", NE), ("xt_sb", 2 * NE), ("gu_ps", NE), ("gu_silu", NE), ("gu_mul", NE),
            ("dn_ps", NE), ("oe_act", NE), ("oe_dve", NE), ("idx_in", NE), ("idx_out", NE), ("scattered0", 8 * NE), ("scattered1", 8 * NE),
            ("even_loaded", 16), ("odd_loaded", 16), ("gf_ps", 1),
            ("ov_w", 48 * OVER), ("ov_tab", 16 * OVER), ("ov_g", OVER), ("ov_xt", OVER), ("ov_xs", OVER),
            ("ov_gu", OVER), ("ov_sl", OVER), ("ov_mu", OVER), ("ov_dn", OVER),
            ("ov_oe", OVER), ("ov_sc", OVER),
        ):
            signal(name, n)
        for s in range(NSLOT):
            PER[f"w{s}"] = 16 * N_MOD // NSLOT + 48 * NE // NSLOT

        block = ctx.enter_context(nc.Block())

        def tk(c):
            return slice(c * P, (c + 1) * P)

        def bank(b, n=1):
            return ps[:, b:b + n, :].rearrange("p b f -> p (b f)")

        def bc(ap, *shape):
            return ap.to_broadcast([P, *shape])

        @block.sync
        def _(sp):
            def past():
                sp.sem_inc(S["past"], 1)

            def wait(name, n, l):
                sp.wait_ge(S[name], l * PER[name] + n)
                past()

            sp.dma_start(h[:, 0:2, :], A["ctx"][0].rearrange("(c p) f -> p c f", p=P)).then_inc(S["head_loaded"], 16)
            sp.dma_start(h[:, 2:4, :], A["x"][0].rearrange("(c p) f -> p c f", p=P)).then_inc(S["head_loaded"], 16)
            sp.dma_start(stage[0:KT, 0, :], A["c_ctx"].rearrange("(k p) -> k p", p=P)).then_inc(S["head_loaded"], 16)
            sp.dma_start(stage[KT:2 * KT, 0, :], A["c"].rearrange("o (k p) -> (o k) p", p=P)).then_inc(S["head_loaded"], 16)
            sp.dma_start(stage[0:4, 1, :], A["hgrn_lb"].rearrange("l (t p) -> (l t) p", p=P)).then_inc(S["head_loaded"], 16)
            with sp.Fori(0, DEPTH) as l:
                L1 = bass.ds(l, 1)
                wmod = A["w_mod"][L1].rearrange("o (k p) n -> p (o k) n", p=P)
                for s in range(NSLOT):
                    sp.dma_start(wgu[s][:, :, :], wmod[:, :, s * MW:(s + 1) * MW]).then_inc(S[f"w{s}"], 16)
                sp.wait_ge(S["cond_ps"], 1)
                def param(dst, src):
                    sp.dma_start(dst, src).then_inc(S["prm_loaded"], 16)
                param(stage[R_BMOD:R_BMOD + 48, 0, :], A["b_mod"][L1].rearrange("o (r p) -> (o r) p", p=P))
                param(stage[R_NMIX:R_NMIX + 8, 0, :], A["norm_mix"][L1].rearrange("o (r p) -> (o r) p", p=P))
                param(stage[R_NFFN:R_NFFN + 8, 0, :], A["norm_ffn"][L1].rearrange("o (r p) -> (o r) p", p=P))
                param(stage[0:40, 1, :], A["ssd_conv_w"][L1].rearrange("o j (t p) -> (o j t) p", p=P))
                param(stage[40:48, 1, :], A["ssd_conv_b"][L1].rearrange("o (t p) -> (o t) p", p=P))
                param(stage[48:78, 1, :], A["gdn_conv_w"][L1].rearrange("o j (t p) -> (o j t) p", p=P))
                param(dtb[:, :, 0:HS], A["ssd_dt_bias"][L1].to_broadcast([P, 2, HS]))
                param(dtb[:, :, HS:NDEC], A["gdn_dt_bias"][L1].to_broadcast([P, 2, HH]))
                param(alog[:, :, 0:HS], A["ssd_a_log"][L1].to_broadcast([P, 2, HS]))
                param(alog[:, :, HS:NDEC], A["gdn_a_log"][L1].to_broadcast([P, 2, HH]))
                param(dsk[:, :], A["ssd_d"][L1].to_broadcast([P, HS]))
                param(rbias[:, :], A["router_bias"][L1].to_broadcast([P, NE]))

                def ring_block(n, dst, src):
                    wait("ring_used", n + 1, l)
                    sp.dma_start(dst, src).then_inc(S[f"ring_full{n % 2}"], 16)

                with sp.Fori(1, N_MOD // NSLOT) as i:
                    for s in range(NSLOT):
                        sp.wait_ge(S["mod_used"], l * N_MOD + i * NSLOT + (s + 1 - NSLOT))
                        past()
                        sp.dma_start(wgu[s][:, :, :], wmod[:, :, bass.ds(i * (NSLOT * MW) + s * MW, MW)]).then_inc(S[f"w{s}"], 16)
                win = A["w_in"][L1].rearrange("o (k p) n -> p (o k) n", p=P)
                sp.dma_start(wsm[:, :, 0:16], win[:, :, 3 * SW:3 * SW + 16]).then_inc(S["small_loaded"], 16)
                sp.dma_start(wsm[:, :, 16:32], win[:, :, COL_GDN + 3 * HW:COL_GDN + 3 * HW + 16]).then_inc(S["small_loaded"], 16)
                for n, (_, col, _) in enumerate(IN_BLOCKS):
                    m = n
                    ring_block(m, ring[:, m % 2, :, :], win[:, :, col:col + BW])
                for c in range(NT):
                    sp.dma_start(acc_odd[tk(c), :].rearrange("p (a b) -> p a b", b=P),
                                 zero[:, :].unsqueeze(1).to_broadcast([P, KT, P])).then_inc(S["acc_zeroed"], 16)
                sp.dma_start(rw[:, :, :], A["router_w"][L1].rearrange("o (k p) n -> p (o k) n", p=P)).then_inc(S["rw_loaded"], 16)
                wout = A["w_out"][L1].rearrange("o (k p) n -> p (o k) n", p=P)
                for n in range(N_OUT):
                    m = N_IN + n
                    ring_block(m, ring[:, m % 2, :, :], wout[:, :, n * BW:(n + 1) * BW])
                    if n == 0:
                        wait("hgrn_done", U, l)
                        sp.dma_start(nrow[:, 0:SW], A["ssd_norm"][L1].to_broadcast([P, SW])).then_inc(S["nrow_loaded"], 16)
                        sp.dma_start(nrow[:, SW:SW + HD], A["hgrn_norm"][L1].to_broadcast([P, HD])).then_inc(S["nrow_loaded"], 16)
                        sp.dma_start(nrow[:, SW + HW:SW + HW + HD], A["gdn_norm"][L1].to_broadcast([P, HD])).then_inc(S["nrow_loaded"], 16)
                for n, name in enumerate(("sh_gate", "sh_up")):
                    m = N_IN + N_OUT + n
                    ring_block(m, ring[:, m % 2, :, :], A[name][L1].rearrange("o (k p) n -> p (o k) n", p=P))
                wait("wo_sb", N_OUT, l)
                gate_w = A["exp_gate"][L1].rearrange("o e (k p) n -> p (o e) k n", p=P)
                up_w = A["exp_up"][L1].rearrange("o e (k p) n -> p (o e) k n", p=P)
                down_w = A["exp_down"][L1].rearrange("o e (k p) n -> p (o e) k n", p=P)

                def expert(s, e):
                    one = bass.ds(e, 1)
                    sp.dma_start(wgu[s][:, :, 0:ED], gate_w[:, one].rearrange("p e k n -> p (e k) n")).then_inc(S[f"w{s}"], 16)
                    sp.dma_start(wgu[s][:, :, ED:2 * ED], up_w[:, one].rearrange("p e k n -> p (e k) n")).then_inc(S[f"w{s}"], 16)
                    sp.dma_start(wdn[s][:, :, :], down_w[:, one].rearrange("p e k n -> p (e k) n")).then_inc(S[f"w{s}"], 16)

                for s in range(NSLOT):
                    expert(s, s)
                for c in range(NT):
                    wait("ftok_sb", c + 1, l)
                    sp.dma_start(f_dram[tk(c), :], X[:, c % 2, :]).then_inc(S[f"x_stored{c % 2}"], 16)
                m = N_IN + N_OUT + 2
                ring_block(m, ring[:, m % 2, :, :].rearrange("p (a b) n -> p a (b n)", a=2),
                           A["sh_down"][L1].rearrange("o (k p) n -> p (o k) n", p=P))
                for c in range(NT):
                    wait("shd_sb", c + 1, l)
                    sp.dma_start(acc_dram[tk(c), :], X[:, c % 2, :]).then_inc(S[f"x_stored{c % 2}"], 16)
                with sp.Fori(1, NE // NSLOT) as i:
                    for s in range(NSLOT):
                        sp.wait_ge(S["dn_ps"], l * NE + i * NSLOT + (s - NSLOT + 1))
                        past()
                        expert(s, i * NSLOT + s)
                wait("oe_act", NE, l)
                wait("oe_dve", NE, l)
                sp.wait_ge(S["flag_ready"], l + 1)
                sp.sem_inc(S["past"], 1)
                over = sp.value_load(flagi[0:1, 0:1], min_val=0, max_val=1)
                with sp.If(over > 0):
                    with sp.Fori(1, NBLK) as b:
                        with sp.Fori(0, NE) as e:
                            one = bass.ds(e, 1)
                            sp.wait_ge(S["ov_sc"], l * OVER + b * NE + e + (1 - NE))
                            past()
                            need = sp.value_load(more[0:1, bass.ds(b * NE + e, 1)], min_val=0, max_val=1)
                            with sp.If(need > 0):
                                sp.dma_start(wgu[0][:, :, 0:ED], gate_w[:, one].rearrange("p e k n -> p (e k) n")).then_inc(S["ov_w"], 16)
                                sp.dma_start(wgu[0][:, :, ED:2 * ED], up_w[:, one].rearrange("p e k n -> p (e k) n")).then_inc(S["ov_w"], 16)
                                sp.dma_start(wdn[0][:, :, :], down_w[:, one].rearrange("p e k n -> p (e k) n")).then_inc(S["ov_w"], 16)
                                sp.dma_start(idxS[0][:, :], tab_dram[bass.ds(b * P, P), one, :].rearrange("p o t -> p (o t)")).then_inc(S["ov_tab"], 16)
                            with sp.Else():
                                sp.sem_inc(S["ov_w"], 48)
                                sp.sem_inc(S["ov_tab"], 16)
                none = sp.value_load(flagi[0:1, 1:2], min_val=0, max_val=1)
                with sp.If(none > 0):
                    sp.sem_inc(S["ov_w"], PER["ov_w"])
                    sp.sem_inc(S["ov_tab"], PER["ov_tab"])
                wait("ov_sc", OVER + 1, l)
                for b in range(2):
                    wait(f"scattered{b}", 8 * NE, l)
                sp.dma_start(yraw[:, :, :], acc_odd.rearrange("(c p) f -> p c f", p=P)).then_inc(S["odd_loaded"], 16)
                sp.dma_start(sums, acc_dram.rearrange("(c p) f -> p c f", p=P)).then_inc(S["even_loaded"], 16)
            sp.wait_ge(S["h_ready"], DEPTH + 1)
            sp.dma_start(grow[:, 0, :], A["norm_final"].rearrange("(o f) -> o f", o=1).to_broadcast([P, DM])).then_inc(S["head_loaded"], 16)
            for c in range(2):
                sp.wait_ge(S["out_ready"], c + 1)
                sp.dma_start(out[0, tk(c), :], X[:, c, :]).then_inc(S["out_stored"], 16)
            sp.wait_ge(S["out_stored"], 32)

        @block.gpsimd
        def _(pool):
            G = nc.gpsimd

            def wait(name, n, l):
                pool.wait_ge(S[name], l * PER[name] + n)
                pool.sem_inc(S["past"], 1)

            def do(ins, name=None, n=1):
                if name:
                    ins.then_inc(S[name], n)
                pool.drain()

            do(G.memset(ones[:, :], 1.0))
            do(G.memset(bd[:, :], 0.0))
            do(G.memset(zero[:, :], 0.0))
            do(G.memset(bd[0:HD, 0:HD], 1.0))
            do(G.memset(bd[HD:P, HD:P], 1.0))
            do(G.affine_select(tri[:, 0, :], ones[:, :], [[1, P]], ALU.is_ge, 0.0, base=0, channel_multiplier=-1))
            do(G.affine_select(tri[:, 1, :], ones[:, :], [[-1, P]], ALU.is_ge, 0.0, base=0, channel_multiplier=1))
            do(G.affine_select(triS[:, :], ones[:, :], [[1, P]], ALU.is_gt, 0.0, base=0, channel_multiplier=-1))
            do(G.affine_select(ident[:, :], ones[:, :], [[1, P]], ALU.is_equal, 0.0, base=0, channel_multiplier=-1))
            do(G.iota(levt[:, 0, :], pattern=[[0, P]], base=0, channel_multiplier=1))
            do(G.iota(levt[:, 1, :], pattern=[[1, P]], base=0, channel_multiplier=0))
            do(G.iota(tokid[:, :], pattern=[[P, NT]], base=0, channel_multiplier=1))
            do(G.iota(iota_e[:, :], pattern=[[1, NE]], base=0, channel_multiplier=0, allow_small_or_imprecise_dtypes=True))
            do(G.memset(live[:, :, :], 1.0))
            do(G.memset(live[:, DEPTH - 1, 0:CTX // P], 0.0))
            do(G.memset(cst[:, 0:1], EPS))
            do(G.memset(cst[:, 1:2], -math.log(math.sqrt(HD))))
            do(G.memset(cst[:, 2:3], -40.0 * math.log(2.0)))
            do(G.memset(cst[:, 3:4], 0.0))
            pool.sem_inc(S["ring_used"], 2)
            pool.sem_inc(S["ov_sc"], 1)
            pool.drain().then_inc(S["const_pool"], 1)
            with pool.Fori(0, DEPTH) as l:
                wait("h_ready", 1, l)
                do(G.memset(Ss[:, :, :, :], 0.0))
                do(G.memset(Sh[:, :, :, :], 0.0))
                do(G.memset(Sg[:, :, :, :], 0.0), "s_init")
                wait("tok_d", NT, l)
                for u, (i, d, c) in enumerate(UNITS):
                    wait("small_done", 1, l) if u == 0 else wait("ho_ps", u, l)
                    do(G.memset(attH[:, :, :], 0.0), "a_init")
                    wait("hexp", u + 1, l)
                    for j in range(LEVELS):
                        w = 2 << j
                        ej = e7[:, j, :].rearrange("p (t s) -> p t s", t=2)
                        ins = G.tensor_tensor(early(ej, w, d), early(ej, w, d), early(hk[:, d, :, tk(c)], w, d), ALU.mult)
                    do(ins, "kl_ready")
                    if u:
                        wait("go_ps", u, l)
                    do(G.tensor_tensor(kw[:, :].rearrange("p (h k) -> p h k", h=HH),
                                       Ktok[:, c, :].rearrange("p (h k) -> p h k", h=HH),
                                       wend[:, c, d, HS:NDEC].unsqueeze(2).to_broadcast([P, HH, HD]), ALU.mult), "kw_ready")
                    for j in range(LEVELS):
                        if j == 0:
                            wait("at_ready", u + 1, l)
                        if j == 2:
                            wait("t_ready", 2 * (u * LEVELS + 1), l)
                        if j >= 2:
                            wait("p_ps", 2 * (u * LEVELS + j - 1), l)
                        do(G.tensor_tensor(NTm[:, j % 2, :, :], AT[:, :, :],
                                           lev[:, d, j, :].unsqueeze(1).to_broadcast([P, HH, P]), ALU.mult), "nt_ready")
                wait("blank_ready", 1, l)
                pool.dma_start(tab_dram.rearrange("a e t -> (a e t)").rearrange("(p n) -> p n", p=P),
                               blank[:, :, :].rearrange("p a b -> p (a b)")).then_inc(S["blank_dram"], 16)
                wait("blank_dram", 16, l)
                wait("pay_ready", 1, l)
                rows = tab_dram.rearrange("a e t -> (a e) t")
                for n in range(NT * TOPK):
                    pool.indirect_dma_start(rows, bass.IndirectOffsetOnAxis(dsti[:, n, :].bitcast(U32), 0), pay[:, n, :], None,
                                            bounds_check=CAP * NE - 1, oob_is_err=False).then_inc(S["tab_dram"], 16)
                wait("tab_dram", 16 * NT * TOPK, l)
                wait("shd_ps", NT, l)
                wait("shd_sb", NT, l)
                pool.dma_start(tabA[:, :, :], tab_dram[0:P, :, :]).then_inc(S["tab_loaded"], 16)
                wait("tab_loaded", 16, l)
                wait("acc_zeroed", 16 * NT, l)
                for b in range(2):
                    wait(f"x_stored{b}", 64, l)

                def gather(s, e):
                    pool.wait_ge(S["idx_in"], l * NE + e + 1)
                    pool.sem_inc(S["past"], 1)
                    def rows(n):
                        pool.indirect_dma_start(xg[s][0:n, :], None, f_dram, bass.IndirectOffsetOnAxis(idxG[s][0:n, 0:1].bitcast(U32), 0),
                                                bounds_check=TOK - 1, oob_is_err=False).then_inc(S[f"gathered{s}"], 16)
                    by_count(e, rows)

                def by_count(e, rows):
                    at_ = slice(e, e + 1) if isinstance(e, int) else bass.ds(e, 1)
                    wide = pool.value_load(more[0:1, at_], min_val=0, max_val=1)
                    with pool.If(wide > 0):
                        rows(P)
                    with pool.Else():
                        rows(HD)

                def pool_step(i, s, ahead):
                    e = l * NE + i * NSLOT + s
                    first = isinstance(i, int) and i == 0
                    if ahead > 3:
                        if not (first and s == 0):
                            pool.wait_ge(S["xt_ps"], e)
                            pool.sem_inc(S["past"], 1)
                        gather((s + 3) % NSLOT, i * NSLOT + s + 3)
                    pool.wait_ge(S["oe_act"], e + 1)
                    pool.wait_ge(S["oe_dve"], e + 1)
                    pool.sem_inc(S["past"], 1)
                    if not (first and s < 2):
                        pool.wait_ge(S[f"scattered{s % 2}"], l * (8 * NE) + i * 32 + (s // 2) * 16)
                        pool.sem_inc(S["past"], 1)

                    def rows(n):
                        pool.indirect_dma_start((acc_dram, acc_odd)[s % 2], bass.IndirectOffsetOnAxis(idxS[s][0:n, 0:1].bitcast(U32), 0),
                                                oe[s % 2][0:n, :], None, bounds_check=TOK - 1, oob_is_err=False,
                                                compute_op=ALU.add).then_inc(S[f"scattered{s % 2}"], 16)
                    by_count(i * NSLOT + s, rows)

                for s in range(3):
                    gather(s, s)
                for s in range(NSLOT):
                    pool_step(0, s, NSLOT + 1)
                with pool.Fori(1, NE // NSLOT - 1) as i:
                    for s in range(NSLOT):
                        pool_step(i, s, NSLOT + 1)
                for s in range(NSLOT):
                    pool_step(NE // NSLOT - 1, s, NSLOT - s)
                for b in range(2):
                    wait(f"scattered{b}", 8 * NE, l)
                over = pool.value_load(flagi[0:1, 0:1], min_val=0, max_val=1)
                with pool.If(over > 0):
                    with pool.Fori(0, OVER) as n_:
                        n = l * OVER + n_
                        pool.wait_ge(S["ov_tab"], n * 16 + 16)
                        pool.sem_inc(S["past"], 1)
                        need = pool.value_load(more[0:1, bass.ds(n_ + NE, 1)], min_val=0, max_val=1)
                        with pool.If(need > 0):
                            pool.indirect_dma_start(xg[0], None, f_dram, bass.IndirectOffsetOnAxis(idxS[0][:, 0:1].bitcast(U32), 0),
                                                    bounds_check=TOK - 1, oob_is_err=False).then_inc(S["ov_dma"], 16)
                            pool.wait_ge(S["ov_dma"], 16)
                            pool.dma_reset(range(S["ov_dma"].num, S["ov_dma"].num + 1))
                            pool.sem_clear(S["ov_dma"])
                            pool.drain().then_inc(S["ov_g"], 1)
                            pool.wait_ge(S["ov_oe"], n + 1)
                            pool.sem_inc(S["past"], 1)
                            pool.indirect_dma_start(acc_dram, bass.IndirectOffsetOnAxis(idxS[0][:, 0:1].bitcast(U32), 0), oe[0], None,
                                                    bounds_check=TOK - 1, oob_is_err=False, compute_op=ALU.add).then_inc(S["ov_dma"], 16)
                            pool.wait_ge(S["ov_dma"], 16)
                            pool.dma_reset(range(S["ov_dma"].num, S["ov_dma"].num + 1))
                            pool.sem_clear(S["ov_dma"])
                            pool.drain().then_inc(S["ov_sc"], 1)
                        with pool.Else():
                            pool.sem_inc(S["ov_g"], 1)
                            pool.sem_inc(S["ov_sc"], 1)
                none = pool.value_load(flagi[0:1, 1:2], min_val=0, max_val=1)
                with pool.If(none > 0):
                    pool.sem_inc(S["ov_g"], PER["ov_g"])
                    pool.sem_inc(S["ov_sc"], PER["ov_sc"])

        @block.scalar
        def _(act):
            C = nc.scalar

            def wait(name, n, l):
                act.wait_ge(S[name], l * PER[name] + n)

            def do(ins, name=None):
                if name:
                    ins.then_inc(S[name], 1)
                act.drain()

            def f(out_, in_, func, name=None, **kw):
                do(C.activation(out_, in_, func, **kw), name)

            act.wait_ge(S["const_pool"], 1)
            act.wait_ge(S["cond_ps"], 1)
            f(condT[:, :, :].rearrange("p a k -> p (a k)"), ps[:, 0, 0:2 * KT], ACT.Silu, "cond_sb")
            act.wait_ge(S["const_ready"], 2)
            f(low[:, :, :], low[:, :, :], ACT.Exp, "cond_sb")

            def norm_turn(q, l):
                wait("sumsq", q + 1, l)
                f(st[:, 4:8], st[:, 0:4], ACT.Ln, scale=1.0 / DM, bias=cst[:, 0:1])
                f(st[:, 8:12], st[:, 4:8], ACT.Exp, "rstd", scale=-0.5)
                for c in range(NT):
                    wait("xT_ps", q * NT + c + 1, l)
                    for k in range(KT // 2, KT):
                        ins = C.activation(featT[:, k, tk(c)], bank(4 + 2 * (c % 2), 2)[:, tk(k)], ACT.Identity,
                                           scale=amul[:, q, k, c // 2:c // 2 + 1], bias=mod[:, 24 * q + k, c // 2:c // 2 + 1])
                    do(ins, "feat_a")

            with act.Fori(0, DEPTH) as l:
                with act.Fori(0, N_MOD // NSLOT) as i:
                    for s in range(NSLOT):
                        act.wait_ge(S["mod_used"], l * N_MOD + i * NSLOT + (s + 1))
                        f(X[0:2, s % 2, 0:MW], ps[0:2, 4 + s % 2, :], ACT.Identity, "mod_row")
                wait("mod_sb", 1, l)
                norm_turn(0, l)
                for n in range(N_CONV):
                    for half in range(2):
                        t = 2 * n + half
                        wait("conv_out", t + 1, l)
                        b = prm[:, R_CBS + t:R_CBS + t + 1] if t < 8 else cst[:, 3:4]
                        C.activation(cv[:, t, 0:CTX], cvo[:, half, 0:CTX], ACT.Silu, bias=b)
                        do(C.activation(cv[:, t, CTX:TOK].rearrange("p (r x) -> p r x", r=ROWS),
                                        line_rows(cvo[:, half, :]), ACT.Silu, bias=b), "silu_out")
                def u_copy(n):
                    kind, _, i = IN_BLOCKS[n]
                    b0 = UB[n % 3]
                    wait("u_ps", n + 1, l)
                    if kind == "hq":
                        f(hq[:, :, :], ps[:, b0:b0 + 2, :], ACT.Silu, "u_act")
                    elif kind == "gate":
                        f(gates[:, :, i * BW:(i + 1) * BW], bank(b0, 2).rearrange("p (c f) -> p c f", c=NT), ACT.Silu, "u_act")
                    elif kind == "val":
                        f(val[:, :, :], bank(b0, 2).rearrange("p (c f) -> p c f", c=NT), ACT.Identity, "u_act")
                    else:
                        f(logf[:, i, :, :], ps[:, b0:b0 + 2, :], ACT.Identity, "u_act")

                def l2_norms(t):
                    wait("l2_ps", t + 1, l)
                    f(lnw[:, :], ps[:, 2 + t % 2, :], ACT.Ln, bias=cst[:, 0:1])
                    if t:
                        wait("l2_done", t, l)
                    f(lnx[:, :], lnw[:, :], ACT.Exp, "l2_act", scale=-0.5, bias=cst[:, 1:2] if t < 2 else cst[:, 3:4])

                u_copy(N_CONV)
                u_copy(N_CONV + 1)
                wait("sp_x", 1, l)
                f(nega[:, :, :], alog[:, :, :], ACT.Exp)
                f(beta[:, :, :, :], beta[:, :, :, :], ACT.Exp, scale=-1.0)
                f(spw[:, 1, :], spw[:, 0, :], ACT.Abs)
                f(spw[:, 1, :], spw[:, 1, :], ACT.Exp, scale=-1.0)
                f(spw[:, 2, :], spw[:, 1, :], ACT.Ln, "sp_exp", bias=ones[:, 0:1])
                wait("low_c", 1, l)
                f(lowv[:, 1, :], lowv[:, 1, :], ACT.Ln)
                f(lowv[:, 1, :], lowv[:, 1, :], ACT.Identity, "lowl", bias=cst[:, 2:3])
                f(hwt[:, :, :], logf[:, :, :, :].rearrange("p a b t -> p (a b) t"), ACT.Abs)
                f(hwt[:, :, :], hwt[:, :, :], ACT.Exp, scale=-1.0)
                f(hwt[:, :, :], hwt[:, :, :], ACT.Ln, "hg_b", bias=ones[:, 0:1])
                u_copy(N_CONV + 2)
                wait("hg_c", 1, l)
                f(hwt[:, :, :], hwx[:, :, :], ACT.Abs)
                f(hwt[:, :, :], hwt[:, :, :], ACT.Exp, scale=-1.0)
                f(hwt[:, :, :], hwt[:, :, :], ACT.Ln, "hg_d", bias=ones[:, 0:1])
                u_copy(N_CONV + 3)
                wait("hg_e", 1, l)
                f(hk[:, :, :, :].rearrange("p a b t -> p (a b) t"), hwt[:, :, :], ACT.Exp, "hg_f")
                wait("cum_dve", 1, l)
                f(eacs[:, :, :, :], acs[:, :, :, :], ACT.Exp)
                f(wend[:, :, :, :], wend[:, :, :, :], ACT.Exp)
                f(etot[:, :, :, :], etot[:, :, :, :], ACT.Exp, "cum_act")
                u_copy(N_CONV + 4)
                l2_norms(0)
                l2_norms(1)
                u_copy(N_CONV + 5)
                l2_norms(2)
                l2_norms(3)
                u_copy(N_CONV + 6)
                u_copy(N_CONV + 7)
                for c in range(NT):
                    wait("tok_ps", c + 1, l)
                    b0 = 4 * (c % 2)
                    C.activation(Btok[:, c, :], ps[:, b0 + 1, 0:HW], ACT.Identity)
                    do(C.activation(Ktok[:, c, :], ps[:, b0 + 1, HW:2 * HW], ACT.Identity), "tok_a")
                def levels_exp(u):
                    wait("b_ready", u + 1, l)
                    f(e7[:, :, :], e7[:, :, :], ACT.Abs)
                    f(e7[:, :, :], e7[:, :, :], ACT.Exp, scale=-1.0)
                    f(e1[:, :], e1[:, :], ACT.Exp, "hexp", scale=-1.0)

                levels_exp(0)
                for u in range(U):
                    wait("dm_gdn", u + 1, l)
                    f(E[:, HS:NDEC, :], E[:, HS:NDEC, :], ACT.Exp, "e_gdn")
                    if u:
                        wait("ho_ps", u, l)
                    f(eb[:, :], bh[:, :], ACT.Exp, "eb_ready")
                    wait("dm_ssd", u + 1, l)
                    f(E[:, 0:HS, :], E[:, 0:HS, :], ACT.Exp, "e_ssd")
                    for j in range(1, LEVELS):
                        for hf in range(2):
                            wait("p_ps", 2 * (u * LEVELS + j) + hf + 1, l)
                            f(Pm[:, 2 * hf:2 * hf + 2, :].rearrange("p h t -> p (h t)"), ps[:, 1 + hf, 0:2 * P], ACT.Identity, "p_sb")
                        if j == 5:
                            wait("ke_ps", u + 1, l)
                            f(kendT[:, :], ps[:, 5, 0:2 * P], ACT.Identity, "ke_sb")
                    if u + 1 < U:
                        levels_exp(u + 1)
                    wait("vn_ps", u + 1, l)
                    f(vn[:, :], ps[:, 1, HW:2 * HW], ACT.Identity, "vn_sb")
                wait("y_sq", 1, l)
                f(ssq[:, :, 0:2], ssq[:, :, 0:2], ACT.Ln, scale=1.0 / HW, bias=cst[:, 0:1])
                f(ssq[:, :, 2:10], ssq[:, :, 2:10], ACT.Ln, scale=1.0 / HD, bias=cst[:, 0:1])
                f(ssq[:, :, :], ssq[:, :, :], ACT.Exp, "y_rstd", scale=-0.5)
                for j in range(2):
                    wait("grow_ps", j + 1, l)
                    f(grow[:, j, :], bank(2 * j, 2), ACT.Identity, "grow_sb")
                for c in range(NT):
                    wait("yT_ps", c + 1, l)
                    f(yT[:, :, tk(c)], bank(4 + 2 * (c % 2), 2).rearrange("p (k t) -> p k t", k=KT), ACT.Identity, "yT_sb")
                norm_turn(1, l)
                wait("lg_ps", 1, l)
                f(scor[:, :, :], ps[:, 0, 0:NT * NE].rearrange("p (c e) -> p c e", c=NT), ACT.Exp, "lg_exp", scale=-1.0)
                wait("sh_ps", 1, l)
                f(sgT[:, :, :], ps[:, 0:2, :], ACT.Silu, "sh_silu")
                def turned(e, b):
                    act.wait_ge(S["xt_ps"], e + 1)
                    do(C.activation(xgT[b][:, 0:4, :].rearrange("p k t -> p (k t)"), ps[:, 0, :], ACT.Identity), "xt_sb")

                def silu(e, b):
                    act.wait_ge(S["gu_ps"], e + 1)
                    f(sg[b].rearrange("p k t -> p (k t)"), ps[:, 2 + b, 0:ED], ACT.Silu, "gu_silu")

                def act_step(i, s, ahead):
                    e = l * NE + i * NSLOT + s
                    if ahead > 1:
                        silu(e + 1, (s + 1) % 2)
                    if ahead > 2:
                        turned(e + 2, s % 2)
                    act.wait_ge(S["idx_out"], e + 1)
                    if not (isinstance(i, int) and i == 0 and s < 2):
                        act.wait_ge(S[f"scattered{s % 2}"], l * (8 * NE) + i * 32 + (s // 2) * 16)
                    act.wait_ge(S["dn_ps"], e + 1)
                    f(oe[s % 2][:, 0:512], ps[:, 4 + 2 * (s % 2), :], ACT.Identity, "oe_act", scale=idxS[s][:, 1:2])

                turned(l * NE, 0)
                silu(l * NE, 0)
                turned(l * NE + 1, 1)
                for s in range(NSLOT):
                    act_step(0, s, NSLOT + 1)
                with act.Fori(1, NE // NSLOT - 1) as i:
                    for s in range(NSLOT):
                        act_step(i, s, NSLOT + 1)
                for s in range(NSLOT):
                    act_step(NE // NSLOT - 1, s, NSLOT - s)
                act.wait_ge(S["flag_ready"], l + 1)
                act.sem_inc(S["past"], 1)
                over = act.value_load(flagi[0:1, 0:1], min_val=0, max_val=1)
                with act.If(over > 0):
                    with act.Fori(0, OVER) as n_:
                        need = act.value_load(more[0:1, bass.ds(n_ + NE, 1)], min_val=0, max_val=1)
                        with act.If(need > 0):
                            act.wait_ge(S["ov_gu"], l * OVER + n_ + 1)
                            f(sg[0].rearrange("p k t -> p (k t)"), ps[:, 2, 0:ED], ACT.Silu, "ov_sl")
                        with act.Else():
                            act.sem_inc(S["ov_sl"], 1)
                none = act.value_load(flagi[0:1, 1:2], min_val=0, max_val=1)
                with act.If(none > 0):
                    act.sem_inc(S["ov_sl"], OVER)
            wait("sumsq", 1, DEPTH)
            f(st[:, 4:6], st[:, 0:2], ACT.Ln, scale=1.0 / DM, bias=cst[:, 0:1])
            f(st[:, 8:10], st[:, 4:6], ACT.Exp, "rstd", scale=-0.5)

        @block.vector
        def _(dve):
            V = nc.vector

            def wait(name, n, l):
                dve.wait_ge(S[name], l * PER[name] + n)

            def do(ins, name=None):
                if name:
                    ins.then_inc(S[name], 1)
                dve.drain()

            def tt(out_, a, b, op, name=None):
                do(V.tensor_tensor(out_, a, b, op), name)

            def ts(out_, a, s1, s2, op0, op1=None, name=None):
                do(V.tensor_scalar(out_, a, s1, s2, op0, *(() if op1 is None else (op1,))), name)

            def stt(out_, a, s_, b, op0, op1, name=None):
                do(V.scalar_tensor_tensor(out_, a, s_, b, op0, op1), name)

            def cp(out_, in_, name=None):
                do(V.tensor_copy(out_, in_), name)

            dve.wait_ge(S["const_pool"], 1)
            tt(levt[:, 0, :], levt[:, 0, :], levt[:, 1, :], ALU.bitwise_xor)
            for j in range(LEVELS):
                ts(levt[:, 1, :], levt[:, 0, :], j, None, ALU.logical_shift_right)
                cp(lev[:, 0, j, :], levt[:, 1, :])
                ts(lev[:, 0, j, :], lev[:, 0, j, :], 1.0, None, ALU.is_equal)
                tt(lev[:, 1, j, :], lev[:, 0, j, :], tri[:, 1, :], ALU.mult)
                tt(lev[:, 0, j, :], lev[:, 0, j, :], triS[:, :], ALU.mult)
            for d in range(2):
                ts(negm[:, d, :], tri[:, d, :], -1.0, -NEG, ALU.add, ALU.mult)
            dve.drain().then_inc(S["const_ready"], 1)
            dve.wait_ge(S["cond_ps"], 1)
            cp(low[:, :, :].rearrange("p l t -> p (l t)"), ps[:, 3, 0:4])
            tt(lowv[:, 0, :], low[:, 0, :], low[:, 1, :], ALU.max)
            tt(low[:, :, :], low[:, :, :], lowv[:, 0:1, :].to_broadcast([P, DEPTH, 2]), ALU.subtract, "const_ready")
            dve.wait_ge(S["cond_sb"], 2)
            tt(lowv[:, 0, :], low[:, 0, :], low[:, 1, :], ALU.add)
            do(V.reciprocal(lowv[:, 1, :], lowv[:, 0, :]))
            tt(low[:, :, :], low[:, :, :], lowv[:, 1:2, :].to_broadcast([P, DEPTH, 2]), ALU.mult)
            tt(lowv[:, 0, :], low[:, 0, :], low[:, 1, :], ALU.add)
            tt(low[:, 1, :], lowv[:, 0, :], low[:, 0, :], ALU.subtract)
            tt(low[:, 0, :], low[:, 0, :], low[:, 0, :], ALU.subtract)
            dve.wait_ge(S["head_loaded"], 16 * 5)
            dve.drain().then_inc(S["h_ready"], 1)

            def norm_turn(q, l):
                for c in range(NT):
                    V.tensor_tensor_reduce(out=X[:, c % 2, :], in0=h[:, c, :], in1=h[:, c, :], scale=1.0, scalar=0.0,
                                           op0=ALU.mult, op1=ALU.add, accum_out=st[:, c:c + 1])
                    dve.drain()
                dve.drain().then_inc(S["sumsq"], 1)
                wait("rstd", q + 1, l)
                for c in range(NT):
                    if c >= 2:
                        wait("xT_ps", q * NT + c - 1, l)
                    ts(X[:, c % 2, :], h[:, c, :], st[:, 8 + c:9 + c], None, ALU.mult, name="xn")
                    if c >= 1:
                        turned(q, c - 1, l)
                turned(q, NT - 1, l)

            def turned(q, c, l):
                wait("xT_ps", q * NT + c + 1, l)
                for k in range(KT // 2):
                    ins = V.tensor_scalar(featT[:, k, tk(c)], bank(4 + 2 * (c % 2), 2)[:, tk(k)],
                                          amul[:, q, k, c // 2:c // 2 + 1], mod[:, 24 * q + k, c // 2:c // 2 + 1],
                                          ALU.mult, ALU.add)
                do(ins, "feat_d")

            with dve.Fori(0, DEPTH) as l:
                L1 = bass.ds(l, 1)
                wait("prm_ps", 1, l)
                cp(prm[:, :], ps[:, 7, 0:N_PRM])
                cp(lowv[:, 0, :], low[:, L1, :].rearrange("p o t -> p (o t)"))
                ts(lowv[:, 2, :], lowv[:, 0, :], -1.0, 1.0, ALU.mult, ALU.add)
                ts(lowv[:, 1, :], lowv[:, 0, :], 1e-30, float(2.0 ** 40), ALU.max, ALU.mult, "low_c")
                wait("mod_ps", 1, l)
                tt(mod[:, :, :], ps[:, 6, 0:96].rearrange("p (r j) -> p r j", j=2),
                   prm[:, R_BMOD:R_BMOD + 48].unsqueeze(2).to_broadcast([P, 48, 2]), ALU.add)
                for q in range(2):
                    ts(amul[:, q, :, :], mod[:, 24 * q + 8:24 * q + 16, :], 1.0, None, ALU.add)
                    tt(amul[:, q, :, :], amul[:, q, :, :],
                       prm[:, R_NMIX + 8 * q:R_NMIX + 8 * q + 8].unsqueeze(2).to_broadcast([P, KT, 2]), ALU.mult)
                dve.drain().then_inc(S["mod_sb"], 1)
                norm_turn(0, l)
                do(V.memset(line[:, :, :], 0.0))
                for n in range(N_CONV):
                    wait("u_ps", n + 1, l)
                    for half in range(2):
                        src = ps[:, UB[n % 3] + half, :]
                        V.tensor_copy(line[:, half, HALF:HALF + CTX], src[:, 0:CTX])
                        V.tensor_copy(line[:, half, CPAD:LINE].rearrange("p (r x) -> p r x", r=ROWS)[:, :, HALF:HALF + GRID_W],
                                      src[:, CTX:TOK].rearrange("p (r x) -> p r x", r=ROWS))
                    dve.drain().then_inc(S["u_dve"], 1)
                    for half in range(2):
                        t = 2 * n + half
                        base, off, per = (R_CWS, t, 8) if t < 8 else (R_CWG, t - 8, 6)
                        if n:
                            wait("silu_out", t - 1, l)
                        for j in range(TAPS):
                            w = prm[:, base + j * per + off:base + j * per + off + 1]
                            o, s_ = cvo[:, half, 0:CONV], line[:, half, j:j + CONV]
                            if j == 0:
                                ts(o, s_, w, None, ALU.mult)
                            else:
                                stt(o, s_, w, o, ALU.mult, ALU.add, "conv_out" if j == TAPS - 1 else None)
                wait("sm_ps", 1, l)
                cp(sm[:, :, :].rearrange("p c f -> p (c f)"), ps[:, 3, 0:32 * NT])
                x3 = spw[:, 0, :].rearrange("p (c d h) -> p c d h", c=NT, d=2)
                for c in range(NT):
                    tt(x3[:, c, :, 0:HS], sm[:, c, 0:16].rearrange("p (d h) -> p d h", d=2), dtb[:, :, 0:HS], ALU.add)
                    tt(x3[:, c, :, HS:NDEC], sm[:, c, 16:24].rearrange("p (d h) -> p d h", d=2), dtb[:, :, HS:NDEC], ALU.add)
                    cp(beta[:, c, :, :].rearrange("p d h -> p (d h)"), sm[:, c, 24:32])
                dve.drain().then_inc(S["sp_x"], 1)
                wait("sp_exp", 1, l)
                ts(beta[:, :, :, :], beta[:, :, :, :], 1.0, None, ALU.add)
                do(V.reciprocal(beta[:, :, :, :], beta[:, :, :, :]))
                ts(spw[:, 3, :], spw[:, 1, :], 1.0, None, ALU.add)
                ts(spw[:, 3, :], spw[:, 3, :], -1.0, None, ALU.add)
                dtf = dt_[:, :, :, :].rearrange("p c d h -> p (c d h)")
                daf = da[:, :, :, :].rearrange("p c d h -> p (c d h)")
                ts(dtf, spw[:, 3, :], 0.0, None, ALU.is_equal)
                tt(spw[:, 2, :], spw[:, 2, :], dtf, ALU.add)
                tt(spw[:, 3, :], spw[:, 3, :], dtf, ALU.add)
                do(V.reciprocal(spw[:, 3, :], spw[:, 3, :]))
                tt(spw[:, 1, :], spw[:, 1, :], spw[:, 3, :], ALU.mult)
                tt(spw[:, 1, :], spw[:, 1, :], spw[:, 2, :], ALU.mult)
                stt(dtf, spw[:, 0, :], 0.0, spw[:, 1, :], ALU.max, ALU.add)
                stt(da[:, :, :, :].rearrange("p c d h -> p c (d h)"), dt_[:, :, :, :].rearrange("p c d h -> p c (d h)"), -1.0,
                    nega[:, :, :].rearrange("p d h -> p (d h)").unsqueeze(1).to_broadcast([P, NT, 2 * NDEC]),
                    ALU.mult, ALU.mult, "sp_done")
                wait("u_act", 2, l)
                wait("lowl", 1, l)
                raw = logf[:, :, :, :].rearrange("p a b t -> p (a b) t")
                ls = hk[:, :, :, :].rearrange("p a b t -> p (a b) t")
                for q in range(4):
                    V.tensor_scalar(hwx[:, q, :], raw[:, q, :], -1.0, lowv[:, 1, q % 2:q % 2 + 1], ALU.mult, ALU.add)
                dve.drain()
                wait("hg_b", 1, l)
                stt(ls, raw, 0.0, hwt[:, :, :], ALU.min, ALU.subtract)
                dve.drain().then_inc(S["hg_c"], 1)
                wait("cum_ps", 1, l)
                for d in range(2):
                    cp(acs[:, :, d, :], ps[:, 2, 48 * d:48 * d + 48].rearrange("p (c h) -> p c h", c=NT))
                cp(etot[:, :, :, :].rearrange("p c d h -> p (c d h)"), ps[:, 2, 96:192])
                tt(wend[:, :, :, :], etot[:, :, :, :], acs[:, :, :, :], ALU.subtract, "cum_dve")
                wait("hg_d", 1, l)
                stt(hwx[:, :, :], hwx[:, :, :], 0.0, hwt[:, :, :], ALU.max, ALU.add)
                tt(hwt[:, :, :], ls, raw, ALU.subtract)
                tt(raw, ls, hwx[:, :, :], ALU.add, "hg_e")
                for t in range(4):
                    if t >= 2:
                        wait("l2_ps", t - 1, l)
                    tt(sqw[:, t % 2, :], cv[:, 8 + t, :], cv[:, 8 + t, :], ALU.mult, "l2_sq")
                    if t >= 1:
                        wait("l2_act", t, l)
                        tt(cv[:, 7 + t, :], cv[:, 7 + t, :], lnx[:, :], ALU.mult, "l2_done")
                wait("l2_act", 4, l)
                tt(cv[:, 11, :], cv[:, 11, :], lnx[:, :], ALU.mult, "l2_done")
                wait("hg_f", 1, l)
                for t in range(2):
                    ts(hk[:, :, t, :], hk[:, :, t, :], lowv[:, 2, t:t + 1], None, ALU.mult)
                dve.drain()
                wait("cum_act", 1, l)
                tt(wdt[:, :, :, :], dt_[:, :, :, :], wend[:, :, :, :], ALU.mult)
                for t in range(2):
                    for par in range(2):
                        rows = slice(par * HD, (par + 1) * HD)
                        cp(dcol[rows, :, t], etot[rows, :, :, HS + 2 * t + par].rearrange("p c d -> p (c d)"))
                dve.drain().then_inc(S["small_done"], 1)
                for c in range(NT):
                    wait("tok_ps", c + 1, l)
                    b0 = 4 * (c % 2)
                    cp(cv[:, 0:4, tk(c)], ps[:, b0, :].rearrange("p (t f) -> p t f", t=4))
                    cp(cv[:, 12:14, tk(c)], ps[:, b0 + 2, 0:HW].rearrange("p (t f) -> p t f", t=2), "tok_d")
                wait("s_init", 1, l)
                def hgrn_decays(u):
                    _, d, c = UNITS[u]
                    end = P - 1 if d == 0 else 0
                    way = slice(None) if d == 0 else slice(None, None, -1)
                    b3 = bh[:, :].rearrange("p (t s) -> p t s", t=2)
                    for t in range(2):
                        V.tensor_tensor_scan(b3[:, t, way], ones[:, :], logf[:, d, t, tk(c)][:, way], 0.0, ALU.mult, ALU.add)
                    dve.drain()
                    for j in range(LEVELS):
                        w = 2 << j
                        mid = w // 2 - 1 if d == 0 else w // 2
                        v = bh[:, :].rearrange("p (n w) -> p n w", w=w)
                        V.tensor_tensor(e7[:, j, :].rearrange("p (n w) -> p n w", w=w), v,
                                        v[:, :, mid:mid + 1].to_broadcast([P, 2 * P // w, w]), ALU.subtract)
                    V.tensor_tensor(e1[:, :].rearrange("p (t s) -> p t s", t=2), b3, b3[:, :, end:end + 1].to_broadcast([P, 2, P]), ALU.subtract)
                    dve.drain().then_inc(S["b_ready"], 1)

                def decays(u, heads_, b, name):
                    _, d, c = UNITS[u]
                    for j in heads_:
                        V.scalar_tensor_tensor(E[:, j, :], ps[:, b + (j % HS) // 4, tk(j % 4)], acs[:, c, d, j:j + 1], negm[:, d, :],
                                               ALU.subtract, ALU.add)
                    dve.drain().then_inc(S[name], 1)

                def gdn_end(u):
                    i, d, c = UNITS[u]
                    gdn = lambda v: v.unsqueeze(2).to_broadcast([P, HH, HD])
                    wait("go_ps", u + 1, l)
                    t3 = tmp[:, 0:HW].rearrange("p (h v) -> p h v", h=HH)
                    tt(t3, ps[:, 2, 0:HW].rearrange("p (h v) -> p h v", h=HH), gdn(eacs[:, c, d, HS:NDEC]), ALU.mult)
                    o = yraw[:, c, SW + HW:DM]
                    if SEEN[c] == u:
                        tt(o, tmp[:, 0:HW], ps[:, 2, HW:2 * HW], ALU.add)
                    else:
                        tt(tmp[:, 0:HW], tmp[:, 0:HW], ps[:, 2, HW:2 * HW], ALU.add)
                        tt(o, o, tmp[:, 0:HW], ALU.add)
                    if i < NT - 1:
                        tt(tmp[:, 0:2 * P].rearrange("p (t v) -> p t v", t=2), ps[:, 3, 0:2 * P].rearrange("p (t v) -> p t v", t=2),
                           bd[:, :].unsqueeze(1).to_broadcast([P, 2, P]), ALU.mult)
                        for t in range(2):
                            V.scalar_tensor_tensor(Sg[:, d, t, :], Sg[:, d, t, :], dcol[:, 2 * c + d, t:t + 1],
                                                   tmp[:, t * P:(t + 1) * P], ALU.mult, ALU.add)
                    dve.drain().then_inc(S["gdn_done"], 1)

                hgrn_decays(0)
                for u, (i, d, c) in enumerate(UNITS):
                    first, last_step = SEEN[c] == u, i == NT - 1
                    end = P - 1 if d == 0 else 0
                    wait("pre_ps", u + 1, l)
                    decays(u, range(HS, NDEC), 4, "dm_gdn")
                    wait("e_gdn", u + 1, l)
                    a2 = lambda ap: ap.rearrange("p (a t) -> p a t", a=2)
                    for par in range(2):
                        V.tensor_tensor(AT[:, par:HH:2, :], a2(ps[:, 5 * par, 0:HW]), E[:, HS + par:NDEC:2, :], ALU.mult)
                    dve.drain()
                    tt(AT[:, :, :].rearrange("p h t -> p (h t)"), AT[:, :, :].rearrange("p h t -> p (h t)"), ps[:, 1, :], ALU.mult)
                    for par in range(2):
                        V.tensor_tensor(E[:, HS + par:NDEC:2, :], a2(ps[:, 5 * par, HW:2 * HW]), E[:, HS + par:NDEC:2, :], ALU.mult)
                    dve.drain().then_inc(S["at_ready"], 1)
                    if u:
                        gdn_end(u - 1)
                    wait("hexp", u + 1, l)
                    q3 = hq[:, :, tk(c)]
                    for j in range(LEVELS):
                        w = 2 << j
                        ej = e7[:, j, :].rearrange("p (t s) -> p t s", t=2)
                        V.tensor_tensor(late(ej, w, d), late(ej, w, d), late(q3, w, d), ALU.mult)
                    dve.drain().then_inc(S["ql_ready"], 1)
                    wait("ssd_pre", u + 1, l)
                    decays(u, range(HS), 6, "dm_ssd")
                    wait("eb_ready", u + 1, l)
                    cp(hdec[:, :], eb[:, :].rearrange("p (t s) -> p t s", t=2)[:, :, end])
                    tt(eb[:, :].rearrange("p (t s) -> p t s", t=2), eb[:, :].rearrange("p (t s) -> p t s", t=2), q3, ALU.mult)
                    tt(kend[:, :].rearrange("p (t s) -> p t s", t=2), e1[:, :].rearrange("p (t s) -> p t s", t=2), hk[:, d, :, tk(c)], ALU.mult)
                    xs = cv[:, 0:4, tk(c)].rearrange("p a (b x) -> p a b x", b=2)
                    by_head = lambda ap: ap.rearrange("p (a b x) -> p a b x", a=4, b=2)
                    heads = lambda v: v.rearrange("p (a b) -> p a b", b=2).unsqueeze(3).to_broadcast([P, 4, 2, HD])
                    id2 = ident[:, :].unsqueeze(1).to_broadcast([P, 2, P])
                    for j in range(LEVELS):
                        for hf in range(2):
                            if j == 0:
                                wait("p_ps", 2 * u * LEVELS + hf + 1, l)
                                tt(W[:, hf, 0:2, :], id2, ps[:, 1 + hf, 0:2 * P].rearrange("p (h t) -> p h t", h=2), ALU.subtract)
                                tt(W[:, hf, 2:4, :], id2, NTm[:, 0, 2 * hf:2 * hf + 2, :], ALU.subtract, "t_ready")
                            else:
                                wait("q_ps", 2 * (u * (LEVELS - 1) + j - 1) + hf + 1, l)
                                w0 = 0 if j < LEVELS - 1 else 2
                                tt(W[:, hf, w0:4, :], W[:, hf, w0:4, :],
                                   ps[:, (3, 0)[hf], w0 * P:4 * P].rearrange("p (h t) -> p h t", t=P), ALU.subtract, "t_ready")
                        if j < 4:
                            if j == 0:
                                wait("a_init", u + 1, l)
                            wait("h_ps", u * 4 + j + 1, l)
                            dve.sem_inc(S["past"], 1)
                            for r in range(2):
                                lv = 2 * j + r
                                for par in range(2):
                                    to = attH[:, par:HH:2, :]
                                    got = ps[:, 4 + par, r * 2 * P:(r + 1) * 2 * P].rearrange("p (a t) -> p a t", a=2)
                                    if lv < LEVELS:
                                        w = 2 << lv
                                        V.copy_predicated(late(to, w, d), late(lev[:, d, lv:lv + 1, :], w, d).bitcast(I32).to_broadcast([P, 2, P // w, w // 2]),
                                                          got[:, :, 0:HD].rearrange("p a (n w) -> p a n w", w=w // 2))
                                    else:
                                        V.copy_predicated(to, ident[:, :].bitcast(I32).unsqueeze(1).to_broadcast([P, 2, P]), got)
                                dve.drain()
                            dve.drain().then_inc(S["h_cp"], 1)
                        if j == 1:
                            wait("e_ssd", u + 1, l)
                            tt(E[:, 0:HS, :], E[:, 0:HS, :], dt_[:, c, d, 0:HS].unsqueeze(2).to_broadcast([P, HS, P]), ALU.mult)
                        if j == 2:
                            wait("cb_ps", u + 1, l)
                            tt(E[:, 0:HS, :].rearrange("p (g r) t -> p g r t", g=NG), E[:, 0:HS, :].rearrange("p (g r) t -> p g r t", g=NG),
                               ps[:, 6, 0:NG * P].rearrange("p (g t) -> p g t", g=NG).unsqueeze(2).to_broadcast([P, NG, HS // NG, P]), ALU.mult)
                            tt(by_head(xw[:, :]), xs, heads(wdt[:, c, d, 0:HS]), ALU.mult, "att_ready")
                        if j == 4:
                            wait("ssd_ps", u + 1, l)
                            tt(by_head(tmp[:, :]), by_head(ps[:, 6, :]), heads(eacs[:, c, d, 0:HS]), ALU.mult)
                            if first:
                                tt(yraw[:, c, 0:SW], tmp[:, :], ps[:, 7, :], ALU.add)
                                tt(by_head(tmp[:, :]), xs, heads(dsk[:, :]), ALU.mult)
                            else:
                                tt(tmp[:, :], tmp[:, :], ps[:, 7, :], ALU.add)
                            tt(yraw[:, c, 0:SW], yraw[:, c, 0:SW], tmp[:, :], ALU.add, "ssd_sb" if last_step else None)
                        if j == 5 and not last_step:
                            wait("ke_ps", u + 1, l)
                            sv = Ss[:, d, :, :].rearrange("p g f -> p (g f)")
                            tt(by_head(sv), by_head(sv), heads(etot[:, c, d, 0:HS]), ALU.mult)
                            tt(sv, sv, ps[:, 4, :], ALU.add, "ssd_sb")
                        if j == 5 and u + 1 < U:
                            hgrn_decays(u + 1)
                    wait("gks_ps", u + 1, l)
                    r3 = rr[:, :].rearrange("p (h v) -> p h v", h=HH)
                    gdn = lambda v: v.unsqueeze(2).to_broadcast([P, HH, HD])
                    tt(r3, ps[:, 1, 0:HW].rearrange("p (h v) -> p h v", h=HH), gdn(eacs[:, c, d, HS:NDEC]), ALU.mult)
                    r22 = rr[:, :].rearrange("p (a f) -> p a f", a=2)
                    tt(r22, cv[:, 12:14, tk(c)], r22, ALU.subtract)
                    tt(r3, r3, gdn(beta[:, c, d, :]), ALU.mult, "r_ready")
                    wait("ho_ps", u + 1, l)
                    o = yraw[:, c, SW:SW + HW]
                    if first:
                        cp(o, ps[:, 4, 0:HW])
                    else:
                        tt(o, o, ps[:, 4, 0:HW], ALU.add)
                    if last_step:
                        dve.drain().then_inc(S["hgrn_done"], 1)
                    else:
                        tt(tmp[:, 0:2 * P].rearrange("p (t v) -> p t v", t=2), ps[:, 5, 2 * P:4 * P].rearrange("p (t v) -> p t v", t=2),
                           bd[:, :].unsqueeze(1).to_broadcast([P, 2, P]), ALU.mult)
                        for t in range(2):
                            stt(Sh[:, d, t, :], Sh[:, d, t, :], hdec[:, t:t + 1], tmp[:, t * P:(t + 1) * P], ALU.mult, ALU.add)
                        dve.drain().then_inc(S["hgrn_done"], 1)
                gdn_end(U - 1)
                for c in range(NT):
                    tt(yraw[:, c, 0:SW], yraw[:, c, 0:SW], gates[:, c, 0:SW], ALU.mult)
                    tt(sqo[:, 0, :], yraw[:, c, :], yraw[:, c, :], ALU.mult)
                    do(V.tensor_reduce(ssq[:, c, 0:2], sqo[:, 0, 0:SW].rearrange("p (g f) -> p g f", g=2), AX.X, ALU.add))
                    do(V.tensor_reduce(ssq[:, c, 2:10], sqo[:, 0, SW:DM].rearrange("p (g f) -> p g f", g=8), AX.X, ALU.add))
                dve.drain().then_inc(S["y_sq"], 1)
                wait("nrow_loaded", 16 * NROW_DMAS, l)
                for base in (SW, SW + HW):
                    cp(nrow[:, base + HD:base + 2 * HD], nrow[:, base:base + HD])
                    cp(nrow[:, base + 2 * HD:base + 4 * HD], nrow[:, base:base + 2 * HD])
                wait("y_rstd", 1, l)
                for c in range(NT):
                    y = yraw[:, c, :]
                    v2 = y[:, 0:SW].rearrange("p (g f) -> p g f", g=2)
                    tt(v2, v2, ssq[:, c, 0:2].unsqueeze(2).to_broadcast([P, 2, HW]), ALU.mult)
                    v8_ = y[:, SW:DM].rearrange("p (g f) -> p g f", g=8)
                    tt(v8_, v8_, ssq[:, c, 2:10].unsqueeze(2).to_broadcast([P, 8, HD]), ALU.mult)
                    tt(y, y, nrow, ALU.mult)
                    tt(y[:, SW:DM], y[:, SW:DM], gates[:, c, SW:DM], ALU.mult, "y_ready")
                wait("grow_sb", 2, l)
                for n in range(N_OUT):
                    wait("wo_ps", n + 1, l)
                    b0 = 4 + 2 * (n % 2)
                    cols = slice(n * BW, (n + 1) * BW)
                    for j in range(2):
                        o = X[:, 0, 0:2 * BW].rearrange("p (c f) -> p c f", c=2)
                        tt(o, ps[:, b0 + j, :].rearrange("p (c f) -> p c f", c=2), grow[:, j, cols].unsqueeze(1).to_broadcast([P, 2, BW]), ALU.mult)
                        tt(h[:, 2 * j:2 * j + 2, cols], h[:, 2 * j:2 * j + 2, cols], o, ALU.add, "wo_sb" if j else None)
                norm_turn(1, l)
                wait("lg_exp", 1, l)
                do(V.memset(blank[:, :, 1:2], 0.0))
                do(V.memset(blank[:, :, 0:1].bitcast(I32), SKIP), "blank_ready")
                ts(scor[:, :, :], scor[:, :, :], 1.0, None, ALU.add)
                do(V.reciprocal(scor[:, :, :], scor[:, :, :]))
                tt(sel[:, :, :], scor[:, :, :], rbias[:, :].unsqueeze(1).to_broadcast([P, NT, NE]), ALU.add)
                for c in range(NT):
                    do(V.max(v8[:, c, :], sel[:, c, :]))
                    do(V.max_index(i8[:, c, :], v8[:, c, :], sel[:, c, :]))
                cp(if8[:, :, :], i8[:, :, :])
                eight = lambda ap: ap.unsqueeze(1).to_broadcast([P, TOPK, NE])
                for c in range(NT):
                    hv = hots[:, c, :].rearrange("p (k e) -> p k e", k=TOPK)
                    tt(hv, eight(iota_e[:, :]), if8[:, c, :].unsqueeze(2).to_broadcast([P, TOPK, NE]), ALU.is_equal)
                    do(V.tensor_reduce(mask[:, c, :], hots[:, c, :].rearrange("p (k e) -> p e k", k=TOPK), AX.X, ALU.add))
                cp(lcur[:, :], live[:, L1, :].rearrange("p o c -> p (o c)"))
                tt(mask[:, :, :], mask[:, :, :], lcur[:, :].unsqueeze(2).to_broadcast([P, NT, NE]), ALU.mult)
                ts(lcur[:, :], lcur[:, :], -float(SKIP), float(SKIP), ALU.mult, ALU.add)
                dve.drain().then_inc(S["mask_ready"], 1)
                for c in range(NT):
                    hv = hots[:, c, :].rearrange("p (k e) -> p k e", k=TOPK)
                    tt(hot2[:, :, :], hv, eight(scor[:, c, :]), ALU.mult)
                    do(V.tensor_reduce(s8[:, c, :], hot2[:, :, :], AX.X, ALU.add))
                do(V.tensor_reduce(gsum[:, :], s8[:, :, :], AX.X, ALU.add))
                do(V.reciprocal(gsum[:, :], gsum[:, :]))
                tt(s8[:, :, :], s8[:, :, :], gsum[:, :].unsqueeze(2).to_broadcast([P, NT, TOPK]), ALU.mult)
                ts(pay[:, :, 1], s8[:, :, :].rearrange("p c k -> p (c k)"), ROUTED_SCALE, None, ALU.mult)
                cp(pay[:, :, 0].bitcast(I32).rearrange("p (c k) -> p c k", c=NT), tokid[:, :].unsqueeze(2).to_broadcast([P, NT, TOPK]))
                wait("pos_ps", 1, l)
                cp(pos[:, :, :].rearrange("p c e -> p (c e)"), ps[:, 7, 0:NT * NE])
                for c in range(NT):
                    hv = hots[:, c, :].rearrange("p (k e) -> p k e", k=TOPK)
                    tt(hot2[:, :, :], hv, eight(pos[:, c, :]), ALU.mult)
                    do(V.tensor_reduce(p8[:, c, :], hot2[:, :, :], AX.X, ALU.add))
                stt(dst8[:, :, :], p8[:, :, :], float(NE), if8[:, :, :], ALU.mult, ALU.add)
                tt(dst8[:, :, :], dst8[:, :, :], lcur[:, :].unsqueeze(2).to_broadcast([P, NT, TOPK]), ALU.add)
                cp(dsti[:, :, 0], dst8[:, :, :].rearrange("p c k -> p (c k)"), "pay_ready")
                for b in range(NBLK):
                    ts(moref[:, b, :], ps[0:1, 7, NT * NE:(NT + 1) * NE], float(P * b if b else HD), None, ALU.is_gt)
                do(V.tensor_copy(more[:, :], moref[:, :, :].rearrange("p b e -> p (b e)")))
                do(V.tensor_reduce(flag[0:1, 0:1], ps[0:1, 7, NT * NE:(NT + 1) * NE], AX.X, ALU.max))
                ts(flag[0:1, 1:2], flag[0:1, 0:1], float(P), None, ALU.is_gt)
                ts(flag[0:1, 2:3], flag[0:1, 0:1], float(P), None, ALU.is_le)
                do(V.tensor_copy(flagi[:, :], flag[0:1, 1:3]), "flag_ready")
                for c in range(NT):
                    wait("ftok_ps", c + 1, l)
                    if c >= 2:
                        wait(f"x_stored{c % 2}", 16 * (c // 2), l)
                    cp(X[:, c % 2, :], bank(4 + 2 * (c % 2), 2), "ftok_sb")
                wait("sh_silu", 1, l)
                wait("sh_ps", 2, l)
                tt(hsh[:, :, :], sgT[:, :, :], ps[:, 2:4, :], ALU.mult, "sh_mul")
                for c in range(NT):
                    wait("shd_ps", c + 1, l)
                    wait(f"x_stored{c % 2}", 32 if c < 2 else 48, l)
                    cp(X[:, c % 2, :], bank(4 + 2 * (c % 2), 2), "shd_sb")

                def x_half(e, b):
                    dve.wait_ge(S["xt_ps"], e + 1)
                    cp(xgT[b][:, 4:8, :].rearrange("p k t -> p (k t)"), ps[:, 1, :], "xt_sb")

                def gate_up(e, b):
                    dve.wait_ge(S["gu_silu"], e + 1)
                    tt(hTe[b].rearrange("p k t -> p (k t)"), sg[b].rearrange("p k t -> p (k t)"), ps[:, 2 + b, ED:2 * ED], ALU.mult, "gu_mul")

                def slots_of(idx, e, name):
                    at_ = slice(e, e + 1) if isinstance(e, int) else bass.ds(e, 1)
                    cp(idx[:, :].bitcast(I32), tabA[:, at_, :].rearrange("p a t -> p (a t)").bitcast(I32), name)

                def dve_step(i, s, ahead):
                    e = l * NE + i * NSLOT + s
                    if ahead > NSLOT:
                        slots_of(idxG[s], i * NSLOT + (s + NSLOT), "idx_in")
                    if ahead > 1:
                        gate_up(e + 1, (s + 1) % 2)
                    if ahead > 2:
                        x_half(e + 2, s % 2)
                    if not (isinstance(i, int) and i == 0 and s < 2):
                        dve.wait_ge(S[f"scattered{s % 2}"], l * (8 * NE) + i * 32 + (s // 2) * 16)
                    if ahead > 2:
                        dve.sem_inc(S["past"], 1)
                        slots_of(idxS[(s + 2) % NSLOT], i * NSLOT + (s + 2), "idx_out")
                    dve.wait_ge(S["dn_ps"], e + 1)
                    ts(oe[s % 2][:, 512:DM], ps[:, 5 + 2 * (s % 2), :], idxS[s][:, 1:2], None, ALU.mult, name="oe_dve")

                wait("tab_loaded", 16, l)
                for s in range(NSLOT):
                    slots_of(idxG[s], s, "idx_in")
                for s in range(2):
                    slots_of(idxS[s], s, "idx_out")
                x_half(l * NE, 0)
                gate_up(l * NE, 0)
                x_half(l * NE + 1, 1)
                for s in range(NSLOT):
                    dve_step(0, s, NSLOT + 1)
                with dve.Fori(1, NE // NSLOT - 1) as i:
                    for s in range(NSLOT):
                        dve_step(i, s, NSLOT + 1)
                for s in range(NSLOT):
                    dve_step(NE // NSLOT - 1, s, NSLOT - s)
                over = dve.value_load(flagi[0:1, 0:1], min_val=0, max_val=1)
                with dve.If(over > 0):
                    with dve.Fori(0, OVER) as n_:
                        n = l * OVER + n_
                        need = dve.value_load(more[0:1, bass.ds(n_ + NE, 1)], min_val=0, max_val=1)
                        with dve.If(need > 0):
                            dve.wait_ge(S["ov_xt"], n + 1)
                            cp(xgT[0].rearrange("p k t -> p (k t)"), bank(0, 2), "ov_xs")
                            dve.wait_ge(S["ov_sl"], n + 1)
                            tt(hTe[0].rearrange("p k t -> p (k t)"), sg[0].rearrange("p k t -> p (k t)"), ps[:, 2, ED:2 * ED], ALU.mult, "ov_mu")
                            dve.wait_ge(S["ov_dn"], n + 1)
                            ts(oe[0], bank(4, 2), idxS[0][:, 1:2], None, ALU.mult, name="ov_oe")
                        with dve.Else():
                            for name in ("ov_xs", "ov_mu", "ov_oe"):
                                dve.sem_inc(S[name], 1)
                none = dve.value_load(flagi[0:1, 1:2], min_val=0, max_val=1)
                with dve.If(none > 0):
                    for name in ("ov_xs", "ov_mu", "ov_oe"):
                        dve.sem_inc(S[name], OVER)
                wait("gf_ps", 1, l)
                wait("odd_loaded", 16, l)
                wait("even_loaded", 16, l)
                for c in range(NT):
                    tt(sums[:, c, :], sums[:, c, :], yraw[:, c, :], ALU.add)
                    tt(sums[:, c, :], sums[:, c, :], bank(2 * (c // 2), 2), ALU.mult)
                    tt(h[:, c, :], h[:, c, :], sums[:, c, :], ALU.add)
                dve.drain().then_inc(S["h_ready"], 1)
            for c in range(2):
                V.tensor_tensor_reduce(out=X[:, c, :], in0=h[:, 2 + c, :], in1=h[:, 2 + c, :], scale=1.0, scalar=0.0,
                                       op0=ALU.mult, op1=ALU.add, accum_out=st[:, c:c + 1])
                dve.drain()
            dve.drain().then_inc(S["sumsq"], 1)
            wait("rstd", 1, DEPTH)
            dve.wait_ge(S["head_loaded"], 16 * 6)
            for c in range(2):
                ts(X[:, c, :], h[:, 2 + c, :], st[:, 8 + c:9 + c], None, ALU.mult)
                tt(X[:, c, :], X[:, c, :], grow[:, 0, :], ALU.mult, "out_ready")


        @block.tensor
        def _(pe):
            MM = nc.tensor.matmul

            def wait(name, n, l):
                pe.wait_ge(S[name], l * PER[name] + n)

            def mm(out_, lhsT, rhs, start=True, stop=True):
                return MM(out_, lhsT, rhs, start=start, stop=stop)

            def turn(out_, in_):
                k = in_.shape[0]
                return nc.tensor.transpose(out_, in_, ident[0:k, 0:k])

            def column(ap):
                return ap.to_broadcast([P, P])

            def ring_wait(m, l):
                pe.wait_ge(S[f"ring_full{m % 2}"], l * (16 * RING // 2) + 16 * (m // 2 + 1))

            W_MOD = 16 * N_MOD // NSLOT

            pe.wait_ge(S["const_ready"], 1)
            pe.wait_ge(S["head_loaded"], 16 * 5)
            turn(ps[:, 0, 0:2 * KT], stage[0:2 * KT, 0, :])
            turn(ps[:, 3, 0:4], stage[0:4, 1, :]).then_inc(S["cond_ps"], 1)

            def norm_turn(q, l):
                for c in range(NT):
                    wait("xn", q * NT + c + 1, l)
                    if c >= 2:
                        wait("feat_d", q * NT + c - 1, l)
                        wait("feat_a", q * NT + c - 1, l)
                    for k in range(KT):
                        ins = turn(bank(4 + 2 * (c % 2), 2)[:, tk(k)], X[:, c % 2, tk(k)])
                    ins.then_inc(S["xT_ps"], 1)

            pe.wait_ge(S["cond_sb"], 1)
            with pe.Fori(0, DEPTH) as l:
                with pe.Fori(0, N_MOD // NSLOT) as i:
                    def mod_turn(s):
                        pe.wait_ge(S["mod_row"], l * N_MOD + i * NSLOT + (s + 1))
                        pe.sem_inc(S["past"], 1)
                        for q in range(MW // P):
                            mm(ps[:, 6, bass.ds(i * (NSLOT * 8) + (s * 8 + q * 2), 2)], X[0:2, s % 2, tk(q)], ident[0:2, 0:2])

                    for s in range(NSLOT):
                        pe.wait_ge(S[f"w{s}"], l * PER["w0"] + i * 16 + 16)
                        for k in range(KT):
                            ins = mm(ps[0:2, 4 + s % 2, :], condT[:, :, k], wgu[s][:, k, :], k == 0, k == KT - 1)
                        ins.then_inc(S["mod_used"], 1)
                        if s:
                            mod_turn(s - 1)
                    mod_turn(NSLOT - 1)
                wait("prm_loaded", 16 * PRM_DMAS, l)
                pe.sem_inc(S["past"], 1)
                turn(ps[:, 7, 0:64], stage[0:64, 0, :])
                turn(ps[:, 7, 64:N_PRM], stage[0:N_PRM - 64, 1, :]).then_inc(S["prm_ps"], 1)
                pe.drain().then_inc(S["mod_ps"], 1)
                wait("h_ready", 1, l)
                wait("mod_sb", 1, l)
                norm_turn(0, l)
                wait("feat_d", NT, l)
                wait("feat_a", NT, l)
                wait("small_loaded", 32, l)
                for c in range(NT):
                    for k in range(KT):
                        ins = mm(ps[:, 3, 32 * c:32 * c + 32], featT[:, k, tk(c)], wsm[:, k, :], k == 0, k == KT - 1)
                ins.then_inc(S["sm_ps"], 1)
                for n, (kind, _, _) in enumerate(IN_BLOCKS):
                    m = n
                    b0 = UB[n % 3]
                    ring_wait(m, l)
                    if n >= 3:
                        wait("u_dve", n - 2, l) if n - 3 < N_CONV else wait("u_act", n - 2 - N_CONV, l)
                    if kind in ("conv", "hq", "hf"):
                        for half in range(2):
                            for k in range(KT):
                                ins = mm(ps[:, b0 + half, :], ring[:, m % 2, k, tk(half)], featT[:, k, :], k == 0, k == KT - 1)
                    else:
                        for c in range(NT):
                            for k in range(KT):
                                ins = mm(bank(b0, 2)[:, c * BW:(c + 1) * BW], featT[:, k, tk(c)], ring[:, m % 2, k, :], k == 0, k == KT - 1)
                    ins.then_inc(S["u_ps"], 1)
                    pe.drain().then_inc(S["ring_used"], 1)
                    if n == N_CONV + 2:
                        wait("sp_done", 1, l)
                        for d in range(2):
                            mm(ps[:, 2, 48 * d:48 * d + 48], tri[:, d, :], da[:, :, d, :])
                        mm(ps[:, 2, 96:192], ones[:, :], da[:, :, :, :].rearrange("p c d h -> p (c d h)")).then_inc(S["cum_ps"], 1)
                    if n in (N_CONV + 4, N_CONV + 5):
                        wait("cum_dve", 1, l)
                        for t in range(2):
                            t += 2 * (n - N_CONV - 4)
                            wait("l2_sq", t + 1, l)
                            if t >= 2:
                                wait("l2_act", t - 1, l)
                            mm(ps[:, 2 + t % 2, :], bd[:, :], sqw[:, t % 2, :]).then_inc(S["l2_ps"], 1)
                wait("u_act", N_IN - N_CONV, l)
                wait("l2_done", 4, l)
                wait("silu_out", CT, l)
                for c in range(NT):
                    b0 = 4 * (c % 2)
                    if c >= 2:
                        wait("tok_d", c - 1, l)
                        wait("tok_a", c - 1, l)
                    for t in range(4):
                        turn(ps[:, b0, tk(t)], cv[:, t, tk(c)])
                    for t in range(2):
                        turn(ps[:, b0 + 1, tk(t)], cv[:, 4 + t, tk(c)])
                        turn(ps[:, b0 + 1, HW + t * P:HW + (t + 1) * P], cv[:, 10 + t, tk(c)])
                        ins = turn(ps[:, b0 + 2, tk(t)], cv[:, 12 + t, tk(c)])
                    ins.then_inc(S["tok_ps"], 1)
                wait("small_done", 1, l)
                wait("tok_d", NT, l)
                wait("tok_a", NT, l)
                wait("s_init", 1, l)
                def key_products(u, par):
                    _, _, c = UNITS[u]
                    rows = slice(par * HD, (par + 1) * HD)
                    for a in range(2):
                        mm(ps[:, 5 * par, tk(a)], cv[rows, 10 + a, tk(c)], cv[rows, 10 + a, tk(c)])
                        mm(ps[:, 5 * par, tk(2 + a)], cv[rows, 10 + a, tk(c)], cv[rows, 8 + a, tk(c)])

                def decay_rows(u, heads_, b):
                    _, d, c = UNITS[u]
                    for j in heads_:
                        ins = mm(ps[:, b + (j % HS) // 4, tk(j % 4)], column(da[:, c, d, j:j + 1]), tri[:, d, :])
                    return ins

                def pre_a(u):
                    key_products(u, 0)

                def pre_b(u):
                    _, d, c = UNITS[u]
                    key_products(u, 1)
                    decay_rows(u, range(HS, NDEC), 4)
                    for j in range(HH):
                        ins = mm(ps[:, 1, tk(j)], column(beta[:, c, d, j:j + 1]), ident[:, :])
                    ins.then_inc(S["pre_ps"], 1)
                    decay_rows(u, range(HS), 6).then_inc(S["ssd_pre"], 1)

                pre_a(0)
                pre_b(0)
                for u, (i, d, c) in enumerate(UNITS):
                    last_step = i == NT - 1
                    if u:
                        wait("gdn_done", u, l)
                    for j in range(LEVELS):
                        wait("nt_ready", u * LEVELS + j + 1, l)
                        for hf in range(2):
                            if j:
                                wait("t_ready", 2 * (u * LEVELS + j - 1) + hf + 1, l)
                            for q in range(2):
                                ins = mm(ps[:, 1 + hf, tk(q)], NTm[:, j % 2, 2 * hf + q, :], W[:, hf, q, :] if j else ident[:, :])
                            ins.then_inc(S["p_ps"], 1)
                        if j == 0:
                            wait("ql_ready", u + 1, l)
                            wait("kl_ready", u + 1, l)
                        if j < 4:
                            if j:
                                wait("h_cp", u * 4 + j, l)
                            for r in range(2):
                                lv = 2 * j + r
                                for par in range(2):
                                    rows = slice(par * HD, (par + 1) * HD)
                                    for a in range(2):
                                        at_ = (2 * r + a) * P
                                        if lv < LEVELS:
                                            w = 2 << lv
                                            ej = e7[rows, lv, :].rearrange("p (t s) -> p t s", t=2)
                                            ins = mm(ps[:, 4 + par, at_:at_ + HD].rearrange("p (n w) -> p n w", w=w // 2),
                                                     e7[rows, lv, tk(a)], late(ej, w, d)[:, a, :, :])
                                        else:
                                            ins = mm(ps[:, 4 + par, at_:at_ + P], hk[rows, d, a, tk(c)], hq[rows, a, tk(c)])
                            ins.then_inc(S["h_ps"], 1)
                        if j == 4:
                            wait("h_cp", u * 4 + 4, l)
                            if not last_step:
                                for g in range(NG):
                                    mm(ps[:, 4, g * HW:(g + 1) * HW], Btok[:, c, tk(g)], xw[:, g * HW:(g + 1) * HW])
                            for a in range(2):
                                ins = turn(ps[:, 5, tk(a)], kend[:, tk(a)])
                            ins.then_inc(S["ke_ps"], 1)
                        for hf in range(2):
                            if j:
                                wait("p_sb", 2 * (u * (LEVELS - 1) + j - 1) + hf + 1, l)
                                for q in range(2):
                                    got, b = Pm[:, 2 * hf + q, :], (3, 0)[hf]
                                    if j < LEVELS - 1:
                                        mm(ps[:, b, tk(q)], W[:, hf, 2 + q, :], got)
                                    ins = mm(ps[:, b, tk(2 + q)], got, W[:, hf, 2 + q, :])
                                ins.then_inc(S["q_ps"], 1)
                        if j == 1:
                            wait("dm_ssd", u + 1, l)
                            for g in range(NG):
                                ins = mm(ps[:, 6, tk(g)], cv[:, 4 + g, tk(c)], cv[:, 6 + g, tk(c)])
                            ins.then_inc(S["cb_ps"], 1)
                        if j == 3:
                            wait("att_ready", u + 1, l)
                            for q in range(HS):
                                mm(ps[:, 7, q * HD:(q + 1) * HD], E[:, q, :], cv[:, q // 2, c * P + (q % 2) * HD:c * P + (q % 2 + 1) * HD])
                            for g in range(NG):
                                ins = mm(ps[:, 6, g * HW:(g + 1) * HW], cv[:, 6 + g, tk(c)], Ss[:, d, g, :])
                            ins.then_inc(S["ssd_ps"], 1)
                    wait("ssd_sb", u + 1, l)
                    for a in range(2):
                        mm(ps[:, 4, tk(a)], eb[:, tk(a)], Sh[:, d, a, :], True, False)
                        for par in range(2):
                            q = 2 * a + par
                            mm(ps[:, 4, q * HD:(q + 1) * HD], attH[:, q, :], val[:, c, q * HD:(q + 1) * HD], False, par == 1)
                    wait("ke_sb", u + 1, l)
                    for a in range(2):
                        ins = mm(ps[:, 5, tk(2 + a)], kendT[:, tk(a)], val[:, c, tk(a)])
                    ins.then_inc(S["ho_ps"], 1)
                    wait("t_ready", 2 * (u + 1) * LEVELS, l)
                    for a in range(2):
                        ins = mm(ps[:, 1, tk(a)], cv[:, 10 + a, tk(c)], Sg[:, d, a, :])
                    ins.then_inc(S["gks_ps"], 1)
                    for a in range(2):
                        mm(ps[:, 2, tk(a)], cv[:, 8 + a, tk(c)], Sg[:, d, a, :])
                    if u + 1 < U:
                        pre_a(u + 1)
                    wait("r_ready", u + 1, l)
                    for q in range(HH):
                        ins = mm(ps[:, 1, HW + q * HD:HW + (q + 1) * HD], W[:, q // 2, 2 + q % 2, :], rr[:, q * HD:(q + 1) * HD])
                    ins.then_inc(S["vn_ps"], 1)
                    wait("vn_sb", u + 1, l)
                    wait("kw_ready", u + 1, l)
                    for q in range(HH):
                        mm(ps[:, 2, HW + q * HD:HW + (q + 1) * HD], E[:, HS + q, :], vn[:, q * HD:(q + 1) * HD])
                    for a in range(2):
                        ins = mm(ps[:, 3, tk(a)], kw[:, tk(a)], vn[:, tk(a)])
                    ins.then_inc(S["go_ps"], 1)
                    if u + 1 < U:
                        wait("hgrn_done", u + 1, l)
                        pre_b(u + 1)
                wait("gdn_done", U, l)
                wait("ssd_sb", U, l)
                def gate_rows(first, name, b0):
                    for j in range(2):
                        for k in range(KT):
                            ins = mm(bank(b0 + 2 * j, 2)[:, tk(k)], column(mod[:, first + k, j:j + 1]), ident[:, :])
                        if name:
                            ins.then_inc(S[name], 1)
                    return ins

                gate_rows(16, "grow_ps", 0)
                for c in range(NT):
                    wait("y_ready", c + 1, l)
                    if c >= 2:
                        wait("yT_sb", c - 1, l)
                    for k in range(KT):
                        ins = turn(bank(4 + 2 * (c % 2), 2)[:, tk(k)], yraw[:, c, tk(k)])
                    ins.then_inc(S["yT_ps"], 1)
                wait("yT_sb", NT, l)
                for n in range(N_OUT):
                    m = N_IN + n
                    ring_wait(m, l)
                    if n >= 2:
                        wait("wo_sb", n - 1, l)
                    for c in range(NT):
                        for k in range(KT):
                            ins = mm(bank(4 + 2 * (n % 2), 2)[:, c * BW:(c + 1) * BW], yT[:, k, tk(c)], ring[:, m % 2, k, :], k == 0, k == KT - 1)
                    ins.then_inc(S["wo_ps"], 1)
                    pe.drain().then_inc(S["ring_used"], 1)
                norm_turn(1, l)
                wait("feat_d", 2 * NT, l)
                wait("feat_a", 2 * NT, l)
                wait("rw_loaded", 16, l)
                wait("grow_sb", 2, l)
                for c in range(NT):
                    for k in range(KT):
                        ins = mm(ps[:, 0, c * NE:(c + 1) * NE], featT[:, k, tk(c)], rw[:, k, :], k == 0, k == KT - 1)
                ins.then_inc(S["lg_ps"], 1)
                wait("lg_exp", 1, l)
                for n in range(2):
                    m = N_IN + N_OUT + n
                    ring_wait(m, l)
                    for half in range(2):
                        for k in range(KT):
                            ins = mm(ps[:, 2 * n + half, :], ring[:, m % 2, k, tk(half)], featT[:, k, :], k == 0, k == KT - 1)
                    ins.then_inc(S["sh_ps"], 1)
                    pe.drain().then_inc(S["ring_used"], 1)
                    if n == 0:
                        wait("mask_ready", 1, l)
                        for c in range(NT + 1):
                            for c2 in range(min(c + 1, NT)):
                                w = triS if c2 == c else ones
                                ins = mm(ps[:, 7, c * NE:(c + 1) * NE], w[:, :], mask[:, c2, :], c2 == 0, c2 == min(c, NT - 1))
                        ins.then_inc(S["pos_ps"], 1)
                wait("flag_ready", 1, l)
                for c in range(NT):
                    if c >= 2:
                        wait("ftok_sb", c - 1, l)
                    for k in range(KT):
                        ins = turn(bank(4 + 2 * (c % 2), 2)[:, tk(k)], featT[:, k, tk(c)])
                    ins.then_inc(S["ftok_ps"], 1)
                m = N_IN + N_OUT + 2
                wait("ftok_sb", NT, l)
                wait("sh_mul", 1, l)
                ring_wait(m, l)
                down = ring[:, m % 2, :, :].rearrange("p (a b) n -> p a (b n)", a=2)
                for c in range(NT):
                    if c:
                        wait("shd_sb", c - 1, l) if c > 1 else None
                    for half in range(2):
                        for k in range(2):
                            ins = mm(ps[:, 4 + 2 * (c % 2) + half, :], hsh[:, k, tk(c)], down[:, k, half * 512:(half + 1) * 512], k == 0, k == 1)
                    ins.then_inc(S["shd_ps"], 1)
                pe.drain().then_inc(S["ring_used"], 1)
                wait("shd_sb", NT, l)

                def rows_T(s, n):
                    pe.wait_ge(S[f"gathered{s}"], n)
                    for k in range(KT):
                        ins = turn(bank(0, 2)[:, tk(k)], xg[s][:, tk(k)])
                    ins.then_inc(S["xt_ps"], 1)

                def gate_up_T(b, s, n):
                    for q in range(4):
                        for k in range(KT):
                            ins = mm(ps[:, 2 + b, q * P:q * P + n], wgu[s][:, k, tk(q)], xgT[b][:, k, 0:n], k == 0, k == KT - 1)
                    return ins

                def gate_up(e, at_, s, ws):
                    b = s % 2
                    pe.wait_ge(S["xt_sb"], e * 2 + 2)
                    pe.wait_ge(S[f"w{s}"], ws)
                    pe.sem_inc(S["past"], 1)
                    wide = pe.value_load(more[0:1, at_], min_val=0, max_val=1)
                    with pe.If(wide > 0):
                        gate_up_T(b, s, P).then_inc(S["gu_ps"], 1)
                    with pe.Else():
                        gate_up_T(b, s, HD).then_inc(S["gu_ps"], 1)

                def pe_step(i, s, ahead):
                    e = l * NE + i * NSLOT + s
                    weights = l * PER["w0"] + i * 48 + (W_MOD + 48)
                    if ahead > 1:
                        j = i * NSLOT + s + 1
                        gate_up(e + 1, slice(j, j + 1) if isinstance(i, int) else bass.ds(j, 1), (s + 1) % NSLOT,
                                weights if s < NSLOT - 1 else weights + 48)
                    if ahead > 2:
                        rows_T((s + 2) % NSLOT, l * (4 * NE) + i * 16 + (16 if s < 2 else 32))
                    pe.wait_ge(S["gu_mul"], e + 1)
                    if not (isinstance(i, int) and i == 0 and s < 2):
                        pe.wait_ge(S["oe_act"], e - 1)
                        pe.wait_ge(S["oe_dve"], e - 1)
                    for half in range(2):
                        for k in range(2):
                            ins = mm(ps[:, 4 + 2 * (s % 2) + half, :], hTe[s % 2][:, k, :], wdn[s][:, k, half * 512:(half + 1) * 512], k == 0, k == 1)
                    ins.then_inc(S["dn_ps"], 1)

                rows_T(0, l * (4 * NE) + 16)
                gate_up(l * NE, slice(0, 1), 0, l * PER["w0"] + W_MOD + 48)
                rows_T(1, l * (4 * NE) + 16)
                for s in range(NSLOT):
                    pe_step(0, s, NSLOT + 1)
                with pe.Fori(1, NE // NSLOT - 1) as i:
                    for s in range(NSLOT):
                        pe_step(i, s, NSLOT + 1)
                for s in range(NSLOT):
                    pe_step(NE // NSLOT - 1, s, NSLOT - s)
                wait("oe_act", NE, l)
                wait("oe_dve", NE, l)
                pe.sem_inc(S["past"], 1)
                over = pe.value_load(flagi[0:1, 0:1], min_val=0, max_val=1)
                with pe.If(over > 0):
                    with pe.Fori(0, OVER) as n_:
                        n = l * OVER + n_
                        need = pe.value_load(more[0:1, bass.ds(n_ + NE, 1)], min_val=0, max_val=1)
                        with pe.If(need > 0):
                            pe.wait_ge(S["ov_g"], n + 1)
                            for k in range(KT):
                                ins = turn(bank(0, 2)[:, tk(k)], xg[0][:, tk(k)])
                            ins.then_inc(S["ov_xt"], 1)
                            pe.wait_ge(S["ov_xs"], n + 1)
                            pe.wait_ge(S["ov_w"], n * 48 + 48)
                            gate_up_T(0, 0, P).then_inc(S["ov_gu"], 1)
                            pe.wait_ge(S["ov_mu"], n + 1)
                            for half in range(2):
                                for k in range(2):
                                    ins = mm(ps[:, 4 + half, :], hTe[0][:, k, :], wdn[0][:, k, half * 512:(half + 1) * 512], k == 0, k == 1)
                            ins.then_inc(S["ov_dn"], 1)
                        with pe.Else():
                            pe.drain()
                            for name in ("ov_xt", "ov_gu", "ov_dn"):
                                pe.sem_inc(S[name], 1)
                none = pe.value_load(flagi[0:1, 1:2], min_val=0, max_val=1)
                with pe.If(none > 0):
                    for name in ("ov_xt", "ov_gu", "ov_dn"):
                        pe.sem_inc(S[name], OVER)
                pe.wait_ge(S["ov_oe"], l * OVER + OVER)
                gate_rows(40, None, 0).then_inc(S["gf_ps"], 1)


_INS = ["x", "c", "ctx", "c_ctx", "w_mod", "b_mod", "norm_mix", "w_in", "ssd_conv_w", "ssd_conv_b", "ssd_dt_bias",
        "ssd_a_log", "ssd_d", "ssd_norm", "hgrn_lb", "hgrn_norm", "gdn_conv_w", "gdn_dt_bias", "gdn_a_log", "gdn_norm",
        "w_out", "norm_ffn", "router_w", "router_bias", "exp_gate", "exp_up", "exp_down", "sh_gate", "sh_up", "sh_down",
        "norm_final"]


def kernel(**inputs):
    import concourse.bacc as bacc
    from concourse.bass_utils import run_bass_kernel_spmd

    nc = bacc.Bacc("TRN2", target_bir_lowering=False, num_devices=1)
    arrays, A = {}, {}
    for name in _INS:
        a = np.ascontiguousarray(inputs[name])
        arrays[f"in_{name}"] = a
        A[name] = nc.dram_tensor(f"in_{name}", a.shape, mybir.dt.from_np(a.dtype), kind="ExternalInput").ap()
    out = nc.dram_tensor("out", (1, SEQ, DM), F32, kind="ExternalOutput").ap()
    scratch = (nc.dram_tensor("ffn_rows", (TOK, DM), F32, kind="Internal").ap(),
               nc.dram_tensor("ffn_sum_even", (TOK, DM), F32, kind="Internal").ap(),
               nc.dram_tensor("ffn_sum_odd", (TOK, DM), F32, kind="Internal").ap(),
               nc.dram_tensor("slots", (CAP, NE, 2), F32, kind="Internal").ap())
    build(nc, A, out, scratch)
    r = run_bass_kernel_spmd(nc, [arrays], core_ids=[0])
    return r.results[0]["out"]
```
